# Optimizing a Trainium2 kernel written in Bass

```python
import math
import jax
import jax.numpy as jnp
from jax import lax
import numpy as np

D_MODEL = 1024
BATCH = 1
SEQ = 512
DEPTH = 1

CTX_LEN = 256
GRID_W = 64
EPS = 1e-6
HEAD_DIM = 64
ROPE_THETA = 10000.0
ATT_HEADS = 8
ATT_KV_HEADS = 2
ATT_GROUP = ATT_HEADS // ATT_KV_HEADS
WINDOW = 128
ATT_BLOCK = 128
ATT_Q_W = ATT_HEADS * HEAD_DIM
ATT_KV_W = ATT_KV_HEADS * HEAD_DIM
SSM_HEADS = 8
SSM_HEAD_DIM = 64
SSM_INNER = SSM_HEADS * SSM_HEAD_DIM
SSM_GROUPS = 2
SSM_STATE = 64
SSM_CONV = 3
SSM_CHUNK = 128
SSM_BC_W = SSM_GROUPS * SSM_STATE
SSM_XBC_W = SSM_INNER + 2 * SSM_BC_W
DT_MIN = 0.001
DT_MAX = 0.1
FNET_GROUPS = 8
FNET_GROUP_DIM = 64
FNET_WIDTH = FNET_GROUPS * FNET_GROUP_DIM
SCONV_WIDTH = 512
SCONV_K = 3
N_BRANCHES = 4
BRANCH_W = 512
IN_SIZES = (ATT_Q_W, ATT_KV_W, ATT_KV_W, SSM_INNER, SSM_XBC_W, 2 * SSM_HEADS, FNET_WIDTH, 3 * SCONV_WIDTH)
IN_PROJ_W = sum(IN_SIZES)
N_EXPERTS = 32
N_EXPERT_GROUPS = 8
EXPERTS_PER_GROUP = N_EXPERTS // N_EXPERT_GROUPS
TOP_K = 2
D_EXPERT = 512
EXPERT_BLOCK = 128

kernel_name = "hybrid_gated_mixers_moe_dit"

def _rmsnorm(x, g):
    xf = x.astype(jnp.float32)
    y = xf * lax.rsqrt(jnp.mean(xf * xf, axis=-1, keepdims=True) + EPS)
    return y.astype(x.dtype) * g

def _modulate(h, shift, scale):
    return h * (1 + scale) + shift

def _dwconv(x, w, b=None):
    k, ch = w.shape
    y = lax.conv_general_dilated(x, w[:, None, :], window_strides=(1,), padding=[((k - 1) // 2, k // 2)],
                                 dimension_numbers=("NWC", "WIO", "NWC"), feature_group_count=ch)
    return y if b is None else y + b

def _split_in(p):
    cuts = np.cumsum(IN_SIZES)[:-1].tolist()
    return jnp.split(p, cuts, axis=-1)

def _axial_rope(n):
    rows = n // GRID_W
    row = jnp.repeat(jnp.arange(rows, dtype=jnp.float32), GRID_W)
    col = jnp.tile(jnp.arange(GRID_W, dtype=jnp.float32), rows)
    pairs = HEAD_DIM // 4
    inv_freq = ROPE_THETA ** (-jnp.arange(pairs, dtype=jnp.float32) / pairs)
    ang = jnp.concatenate([row[:, None] * inv_freq, col[:, None] * inv_freq], axis=-1)
    return jnp.cos(ang), jnp.sin(ang)

def _rope(x, cos, sin):
    x1, x2 = jnp.split(x, 2, axis=-1)
    c = cos[:, None, :].astype(x.dtype)
    s = sin[:, None, :].astype(x.dtype)
    return jnp.concatenate([x1 * c - x2 * s, x2 * c + x1 * s], axis=-1)

def _window_attention(q, k, v, k_ctx, v_ctx, sink):
    b, s, kvh, g, dh = q.shape
    nb = s // ATT_BLOCK
    scale = dh ** -0.5
    qb = q.reshape(b, nb, ATT_BLOCK, kvh, g, dh)

    def band(t):
        tb = t.reshape(b, nb, ATT_BLOCK, kvh, dh)
        z = jnp.zeros_like(tb[:, :1])
        tp = jnp.concatenate([z, tb, z], axis=1)
        return jnp.concatenate([tp[:, :-2], tp[:, 1:-1], tp[:, 2:]], axis=2)

    kw, vw = band(k), band(v)
    sink_f = sink.astype(jnp.float32).reshape(kvh, g, 1, 1)
    qi = jnp.arange(ATT_BLOCK)
    kj = jnp.arange(3 * ATT_BLOCK)

    def block(args):
        qn, kn, vn, n = args
        s_loc = jnp.einsum("bqkgd,bjkd->bkgqj", qn, kn).astype(jnp.float32) * scale
        kabs = (n - 1) * ATT_BLOCK + kj
        qabs = n * ATT_BLOCK + qi
        valid = (jnp.abs(kabs[None, :] - qabs[:, None]) <= WINDOW) & (kabs >= 0)[None, :] & (kabs < s)[None, :]
        s_loc = jnp.where(valid, s_loc, -jnp.inf)
        s_ctx = jnp.einsum("bqkgd,bckd->bkgqc", qn, k_ctx).astype(jnp.float32) * scale
        sink_col = jnp.broadcast_to(sink_f, s_loc.shape[:-1] + (1,))
        probs = jax.nn.softmax(jnp.concatenate([s_loc, s_ctx, sink_col], axis=-1), axis=-1).astype(vn.dtype)
        p_loc = probs[..., :3 * ATT_BLOCK]
        p_ctx = probs[..., 3 * ATT_BLOCK:-1]
        return (jnp.einsum("bkgqj,bjkd->bqkgd", p_loc, vn)
                + jnp.einsum("bkgqc,bckd->bqkgd", p_ctx, v_ctx))

    outs = lax.map(block, (jnp.moveaxis(qb, 1, 0), jnp.moveaxis(kw, 1, 0), jnp.moveaxis(vw, 1, 0),
                           jnp.arange(nb)))
    return jnp.moveaxis(outs, 0, 1).reshape(b, s, kvh * g * dh)

def _context_attention(q, k, v, sink):
    b, lc, kvh, g, dh = q.shape
    sc = jnp.einsum("bqkgd,bckd->bkgqc", q, k).astype(jnp.float32) * dh ** -0.5
    sink_col = jnp.broadcast_to(sink.astype(jnp.float32).reshape(kvh, g, 1, 1), sc.shape[:-1] + (1,))
    probs = jax.nn.softmax(jnp.concatenate([sc, sink_col], axis=-1), axis=-1)[..., :-1].astype(v.dtype)
    return jnp.einsum("bkgqc,bckd->bqkgd", probs, v).reshape(b, lc, kvh * g * dh)

def _ssd(x, dt, a, bm, cm, init, with_output):
    b, l, h, p = x.shape
    n = bm.shape[-1]
    nc = l // SSM_CHUNK
    a_cs = jnp.cumsum((dt * a).reshape(b, nc, SSM_CHUNK, h), axis=2)
    xd = (x * dt[..., None]).reshape(b, nc, SSM_CHUNK, h, p)
    bc = bm.reshape(b, nc, SSM_CHUNK, h, n)
    decay_to_end = jnp.exp(a_cs[:, :, -1:] - a_cs)
    chunk_states = jnp.einsum("bcqhn,bcqhp->bchpn", bc * decay_to_end[..., None], xd)
    chunk_decay = jnp.exp(a_cs[:, :, -1])

    def step(state, inp):
        st, dec = inp
        return state * dec[:, :, None, None] + st, state

    final, prev = lax.scan(step, init, (jnp.moveaxis(chunk_states, 1, 0), jnp.moveaxis(chunk_decay, 1, 0)))
    if not with_output:
        return None, final
    prev = jnp.moveaxis(prev, 0, 1)
    cc = cm.reshape(b, nc, SSM_CHUNK, h, n)
    seg = a_cs[:, :, :, None, :] - a_cs[:, :, None, :, :]
    tri = jnp.tril(jnp.ones((SSM_CHUNK, SSM_CHUNK), dtype=bool))[None, None, :, :, None]
    lmat = jnp.exp(jnp.where(tri, seg, -jnp.inf))
    scores = jnp.einsum("bcihn,bcjhn->bcijh", cc, bc) * lmat
    y_diag = jnp.einsum("bcijh,bcjhp->bcihp", scores, xd)
    y_off = jnp.einsum("bcihn,bchpn->bcihp", cc, prev) * jnp.exp(a_cs)[..., None]
    return (y_diag + y_off).reshape(b, l, h, p), final

def _ssm_prep(xbc, dt_raw, conv_w, conv_b, dt_bias):
    b, l, _ = xbc.shape
    xbc = jax.nn.silu(_dwconv(xbc, conv_w, conv_b)).astype(jnp.float32)
    xs, bg, cg = jnp.split(xbc, [SSM_INNER, SSM_INNER + SSM_BC_W], axis=-1)
    rep = SSM_HEADS // SSM_GROUPS
    xs = xs.reshape(b, l, SSM_HEADS, SSM_HEAD_DIM)
    bm = jnp.repeat(bg.reshape(b, l, SSM_GROUPS, SSM_STATE), rep, axis=2)
    cm = jnp.repeat(cg.reshape(b, l, SSM_GROUPS, SSM_STATE), rep, axis=2)
    dt = jax.nn.softplus(dt_raw.astype(jnp.float32).reshape(b, l, 2, SSM_HEADS) + dt_bias.astype(jnp.float32))
    return xs, bm, cm, dt

def _ssm_bidir(xs, bm, cm, dt, a_log, init_f, init_b, with_output):
    a = -jnp.exp(a_log.astype(jnp.float32))
    flip = lambda t: jnp.flip(t, axis=1)
    y_f, fin_f = _ssd(xs, dt[:, :, 0], a[0], bm, cm, init_f, with_output)
    y_b, fin_b = _ssd(flip(xs), flip(dt[:, :, 1]), a[1], flip(bm), flip(cm), init_b, with_output)
    if not with_output:
        return None, fin_f, fin_b
    return y_f + flip(y_b), fin_f, fin_b

def _ssm_out(y, xs, z, d_skip, norm_w):
    b, l = z.shape[:2]
    y = (y + d_skip.astype(jnp.float32)[:, None] * xs).reshape(b, l, SSM_INNER)
    y = y * jax.nn.silu(z.astype(jnp.float32))
    return _rmsnorm(y, norm_w).astype(z.dtype)

def _fourier(u):
    b, l, _ = u.shape
    uf = u.astype(jnp.float32).reshape(b, l, FNET_GROUPS, FNET_GROUP_DIM)
    y = jnp.fft.fft2(uf, axes=(1, 3), norm="ortho").real
    return y.reshape(b, l, FNET_WIDTH).astype(u.dtype)

def _short_conv(p, w):
    bg, cg, xs = jnp.split(p, 3, axis=-1)
    return bg * _dwconv(cg * xs, w)

def _merge(h, branches, w_gate, b_gate, w_branch, w_o):
    b, l, d = h.shape
    gates = jax.nn.sigmoid(h @ w_gate + b_gate).reshape(b, l, N_BRANCHES, d)
    proj = jnp.einsum("blnw,nwd->blnd", branches, w_branch)
    return jnp.sum(gates * proj, axis=2) @ w_o

def _token_mixer(h, hc, w_in, sink, conv_w, conv_b, dt_bias, a_log, d_skip, ssm_norm_w, sconv_w,
                 w_gate, b_gate, w_branch, w_o, cos, sin, need_ctx):
    b, s, _ = h.shape
    lc = hc.shape[1]
    q, k, v, z, xbc, dtr, fu, su = _split_in(h @ w_in)
    qc, kc, vc, zc, xbcc, dtrc, fuc, suc = _split_in(hc @ w_in)
    q = _rope(q.reshape(b, s, ATT_HEADS, HEAD_DIM), cos, sin).reshape(b, s, ATT_KV_HEADS, ATT_GROUP, HEAD_DIM)
    k = _rope(k.reshape(b, s, ATT_KV_HEADS, HEAD_DIM), cos, sin)
    v = v.reshape(b, s, ATT_KV_HEADS, HEAD_DIM)
    kc = kc.reshape(b, lc, ATT_KV_HEADS, HEAD_DIM)
    vc = vc.reshape(b, lc, ATT_KV_HEADS, HEAD_DIM)
    att = _window_attention(q, k, v, kc, vc, sink)
    xs_c, bm_c, cm_c, dt_c = _ssm_prep(xbcc, dtrc, conv_w, conv_b, dt_bias)
    zero = jnp.zeros((b, SSM_HEADS, SSM_HEAD_DIM, SSM_STATE), jnp.float32)
    y_c, fin_f, fin_b = _ssm_bidir(xs_c, bm_c, cm_c, dt_c, a_log, zero, zero, need_ctx)
    xs, bm, cm, dt = _ssm_prep(xbc, dtr, conv_w, conv_b, dt_bias)
    y, _, _ = _ssm_bidir(xs, bm, cm, dt, a_log, fin_f, fin_b, True)
    ssm = _ssm_out(y, xs, z, d_skip, ssm_norm_w)
    branches = jnp.stack([att, ssm, _fourier(fu), _short_conv(su, sconv_w)], axis=2)
    out = _merge(h, branches, w_gate, b_gate, w_branch, w_o)
    if not need_ctx:
        return out, None
    att_c = _context_attention(qc.reshape(b, lc, ATT_KV_HEADS, ATT_GROUP, HEAD_DIM), kc, vc, sink)
    ssm_c = _ssm_out(y_c, xs_c, zc, d_skip, ssm_norm_w)
    branches_c = jnp.stack([att_c, ssm_c, _fourier(fuc), _short_conv(suc, sconv_w)], axis=2)
    return out, _merge(hc, branches_c, w_gate, b_gate, w_branch, w_o)

def _route(t, w_router, router_bias):
    n = t.shape[0]
    scores = jax.nn.sigmoid((t @ w_router).astype(jnp.float32))
    sel = (scores + router_bias.astype(jnp.float32)).reshape(n, N_EXPERT_GROUPS, EXPERTS_PER_GROUP)
    group_score = jnp.sum(lax.top_k(sel, 2)[0], axis=-1)
    best = jnp.argmax(group_score, axis=-1)
    in_group = jnp.take_along_axis(sel, best[:, None, None], axis=1)[:, 0]
    _, local = lax.top_k(in_group, TOP_K)
    idx = best[:, None] * EXPERTS_PER_GROUP + local
    w = jnp.take_along_axis(scores, idx, axis=1)
    return idx, w / jnp.sum(w, axis=-1, keepdims=True)

def _expert_ffn(t, idx, wts, w1, w3, w2):
    n, d = t.shape
    flat_e = idx.reshape(-1)
    a = flat_e.shape[0]
    order = jnp.argsort(flat_e)
    e_sorted = flat_e[order]
    tok = order // TOP_K
    counts = jnp.bincount(flat_e, length=N_EXPERTS)
    padded = (counts + EXPERT_BLOCK - 1) // EXPERT_BLOCK * EXPERT_BLOCK
    pad_end = jnp.cumsum(padded)
    grp_start = jnp.cumsum(counts) - counts
    dest = (pad_end - padded)[e_sorted] + jnp.arange(a) - grp_start[e_sorted]
    n_blocks = -(-a // EXPERT_BLOCK) + N_EXPERTS
    buf = jnp.zeros((n_blocks * EXPERT_BLOCK, d), t.dtype).at[dest].set(t[tok])
    block_expert = jnp.minimum(jnp.searchsorted(pad_end, jnp.arange(n_blocks) * EXPERT_BLOCK, side="right"),
                               N_EXPERTS - 1)

    def expert_block(args):
        xb, e = args
        return (jax.nn.silu(xb @ w1[e]) * (xb @ w3[e])) @ w2[e]

    yb = lax.map(expert_block, (buf.reshape(n_blocks, EXPERT_BLOCK, d), block_expert))
    y_rows = yb.reshape(-1, d)[dest] * wts.reshape(-1)[order][:, None].astype(t.dtype)
    return jnp.zeros_like(t).at[tok].add(y_rows)

def _moe(t, w_router, router_bias, w1, w3, w2):
    idx, wts = _route(t, w_router, router_bias)
    return _expert_ffn(t, idx, wts, w1, w3, w2)

def setup_inputs(seed: int = 0) -> dict:
    key = jax.random.key(seed)
    ks = jax.random.split(key, 28)
    f32 = jnp.float32
    nrm = lambda k, shape, scale: jax.random.normal(k, shape, f32) * scale
    L, D = DEPTH, D_MODEL
    dt0 = jnp.exp(jax.random.uniform(ks[12], (L, 2, SSM_HEADS), f32, math.log(DT_MIN), math.log(DT_MAX)))
    return {
        "x": nrm(ks[0], (BATCH, SEQ, D), 1.0),
        "c": nrm(ks[1], (BATCH, D), 1.0),
        "ctx": nrm(ks[2], (BATCH, CTX_LEN, D), 1.0),
        "c_ctx": nrm(ks[3], (D,), 1.0),
        "norm1_w": 1.0 + nrm(ks[4], (L, D), 0.02),
        "norm2_w": 1.0 + nrm(ks[5], (L, D), 0.02),
        "w_ada": nrm(ks[6], (L, D, 6 * D), 0.5 * D ** -0.5),
        "b_ada": nrm(ks[7], (L, 6 * D), 0.02),
        "w_in": nrm(ks[8], (L, D, IN_PROJ_W), D ** -0.5),
        "attn_sink": nrm(ks[9], (L, ATT_HEADS), 0.5),
        "ssm_conv_w": nrm(ks[10], (L, SSM_CONV, SSM_XBC_W), SSM_CONV ** -0.5),
        "ssm_conv_b": nrm(ks[11], (L, SSM_XBC_W), 0.02),
        "ssm_dt_bias": dt0 + jnp.log(-jnp.expm1(-dt0)),
        "ssm_a_log": jnp.log(jax.random.uniform(ks[13], (L, 2, SSM_HEADS), f32, 1.0, 16.0)),
        "ssm_d": 1.0 + nrm(ks[14], (L, SSM_HEADS), 0.1),
        "ssm_norm_w": 1.0 + nrm(ks[15], (L, SSM_INNER), 0.02),
        "sconv_w": nrm(ks[16], (L, SCONV_K, SCONV_WIDTH), SCONV_K ** -0.5),
        "w_gate": nrm(ks[17], (L, D, N_BRANCHES * D), D ** -0.5),
        "b_gate": nrm(ks[18], (L, N_BRANCHES * D), 0.02),
        "w_branch": nrm(ks[19], (L, N_BRANCHES, BRANCH_W, D), BRANCH_W ** -0.5),
        "w_o": nrm(ks[20], (L, D, D), D ** -0.5),
        "w_router": nrm(ks[21], (D, N_EXPERTS), D ** -0.5),
        "router_bias": nrm(ks[22], (N_EXPERTS,), 0.01),
        "moe_w1": nrm(ks[23], (L, N_EXPERTS, D, D_EXPERT), D ** -0.5),
        "moe_w3": nrm(ks[24], (L, N_EXPERTS, D, D_EXPERT), D ** -0.5),
        "moe_w2": nrm(ks[25], (L, N_EXPERTS, D_EXPERT, D), D_EXPERT ** -0.5),
        "final_norm_w": 1.0 + nrm(ks[26], (D,), 0.02),
    }

def reference(x, c, ctx, c_ctx, norm1_w, norm2_w, w_ada, b_ada, w_in, attn_sink, ssm_conv_w, ssm_conv_b,
              ssm_dt_bias, ssm_a_log, ssm_d, ssm_norm_w, sconv_w, w_gate, b_gate, w_branch, w_o,
              w_router, router_bias, moe_w1, moe_w3, moe_w2, final_norm_w):
    b, s, d = x.shape
    lc = ctx.shape[1]
    cos, sin = _axial_rope(s)
    sc = jax.nn.silu(c)
    scc = jax.nn.silu(c_ctx)
    xc = ctx
    for layer in range(DEPTH):
        need_ctx = layer + 1 < DEPTH
        mod = jnp.split(sc @ w_ada[layer] + b_ada[layer], 6, axis=-1)
        mod_c = jnp.split(scc @ w_ada[layer] + b_ada[layer], 6, axis=-1)
        h = _modulate(_rmsnorm(x, norm1_w[layer]), mod[0][:, None], mod[1][:, None])
        hc = _modulate(_rmsnorm(xc, norm1_w[layer]), mod_c[0], mod_c[1])
        y, yc = _token_mixer(h, hc, w_in[layer], attn_sink[layer], ssm_conv_w[layer], ssm_conv_b[layer],
                             ssm_dt_bias[layer], ssm_a_log[layer], ssm_d[layer], ssm_norm_w[layer],
                             sconv_w[layer], w_gate[layer], b_gate[layer], w_branch[layer], w_o[layer],
                             cos, sin, need_ctx)
        x = x + mod[2][:, None] * y
        h2 = _modulate(_rmsnorm(x, norm2_w[layer]), mod[3][:, None], mod[4][:, None])
        if need_ctx:
            xc = xc + mod_c[2] * yc
            h2c = _modulate(_rmsnorm(xc, norm2_w[layer]), mod_c[3], mod_c[4])
            tokens = jnp.concatenate([h2.reshape(-1, d), h2c.reshape(-1, d)], axis=0)
            f = _moe(tokens, w_router, router_bias, moe_w1[layer], moe_w3[layer], moe_w2[layer])
            x = x + mod[5][:, None] * f[:b * s].reshape(b, s, d)
            xc = xc + mod_c[5] * f[b * s:].reshape(b, lc, d)
        else:
            f = _moe(h2.reshape(-1, d), w_router, router_bias, moe_w1[layer], moe_w3[layer], moe_w2[layer])
            x = x + mod[5][:, None] * f.reshape(b, s, d)
    return _rmsnorm(x, final_norm_w)


_drawn_inputs = setup_inputs


def setup_inputs(seed=0):
    import zlib

    import numpy as np

    out = dict(_drawn_inputs(seed))
    spreads = {}
    factors = {'ctx': 2.737,
     'norm1_w': 3.072,
     'attn_sink': 64.0,
     'ssm_conv_b': 39.36,
     'ssm_norm_w': 36.112,
     'b_gate': 6.059,
     'final_norm_w': 8.199,
     'norm2_w': 8.0,
     'ssm_d': 8.0,
     'router_bias': 8.0}
    for name, (base, spread) in spreads.items():
        noise = np.random.default_rng([zlib.crc32(name.encode()), seed]).standard_normal(out[name].shape)
        drawn = base * np.exp(spread * noise) if base else spread * noise
        out[name] = jnp.asarray(drawn.astype(out[name].dtype))
    for name, factor in factors.items():
        out[name] = (out[name] * factor).astype(out[name].dtype)
    return out
```

```python
from contextlib import ExitStack

import numpy as np
import concourse.bass as bass
from concourse import mybir

F32 = mybir.dt.float32
I32 = mybir.dt.int32
U32 = mybir.dt.uint32
ALU = mybir.AluOpType
ACT = mybir.ActivationFunctionType
AX = mybir.AxisListType

P = 128
D, KD = 1024, 8
S, NCH = 512, 4
SC, NCC = 256, 2
EPS = 1e-6
NEG = -1.0e30
HD = 64
NE, NG, EPG = 32, 8, 4
BLK = 64
MAXB = 2 * S // BLK + NE - 1
UNIT = 4096
RING = 3
PAIRS = (MAXB + 1) // 2

C_ID, C_LE, C_GE, C_LT, C_GT, C_ONE, C_PERM, C_BD, C_MASK = 0, 128, 256, 384, 512, 640, 768, 896, 1152
C_N = C_MASK + 7 * 128
Q_G1, Q_G2, Q_GF, Q_BADA, Q_BG, Q_CW, Q_CB, Q_SW, Q_SN, Q_C, Q_EPS, Q_EPS4, Q_ZERO, Q_IOTA = (
    0, 8, 16, 24, 72, 104, 122, 128, 140, 144, 160, 161, 162, 163)
Q_N = 164
R_DTB, R_ALOG, R_D, R_SINK, R_RB, R_IE, R_IG, R_IB = 0, 16, 32, 40, 48, 80, 112, 120
R_N = 184

MIX_ORDER = (3, 2, 0, 1)
N_ADA1, N_IN = 4, 8


def timeline():
    t = [("ssq",), ("ssqc",), ("mod", 0)]
    for m in range(4):
        t += [("xbc", m), ("xbcc", m)]
    for m in (4, 5):
        t += [("xbc", m), ("xbcc", m)]
    t += [("k",), ("kc",), ("dt",), ("v",), ("rot", 0), ("vc",)]
    t += [("fu", m) for m in range(4)]
    t += [("dec",)]
    for m in range(4):
        t += [("q", m)]
        if m:
            t += [("rot", m)]
    for m in range(4):
        t += [("cg", m)] + ([("rot", 4)] if m == 0 else []) + [("sx", m), ("bg", m)]
    t += [("z", c) for c in range(NCH)]
    t += [("xtr", c) for c in (4, 5, 0, 1, 2, 3)] + [("btr", 0), ("btr", 1)]
    t += [("V", 0), ("V", 1), ("F", 0), ("V", 2), ("F", 1), ("V", 3), ("F", 2), ("F", 3)]

    ssm = [("st", d, k) for k in range(5) for d in range(2)]
    for c in range(NCH):
        for g in range(2):
            ssm += [("G", c, g), ("seg", c, g, 0), ("seg", c, g, 1), ("yoff", c, g), ("y", c, g)]
    ssm += [("ynorm",)] + [("ytr", c) for c in range(NCH)]
    n_att = 32 + 3
    point = 0

    def side():
        nonlocal point
        out = []
        if point % 2 == 0 and point // 2 < n_att:
            h = point // 2
            if h < 32:
                out.append(("S", h))
            if 0 <= h - 2 < 32:
                out.append(("T", h - 2))
            if 0 <= h - 3 < 32:
                out.append(("O", h - 3))
        elif ssm:
            out.append(ssm.pop(0))
        point += 1
        return out

    for i, n in enumerate(MIX_ORDER):
        if i == 2:
            for u in range(8):
                t += [("mod", 1 + u)] + side() + side()
        if i == 3:
            t += ssm
            ssm = []
        for d in range(8):
            t += [("gate", n, d)] + side() + side() + [("proj", n, d)] + side() + side()
    t += [("wo", d) for d in range(8)]
    t += [("ssq2",)] + [("h2tr", c) for c in range(NCH)] + [("rt",), ("cnt",), ("bexp",)]
    return t


ROT3 = {"xbc", "xbcc", "k", "kc", "dt", "v", "vc", "fu", "q", "rot", "cg", "sx", "bg", "z", "wo"}


def bank_plan(steps):
    used, plan, rot, alt = {}, {}, 0, 0
    for s in steps:
        k = s[0]
        if k in ROT3:
            b = rot % 3
            rot += 1
        elif k == "gate":
            b = s[2] % 2
        elif k == "proj":
            b = 2
        elif k in ("S", "h2tr"):
            b = 3
        elif k in ("V", "T"):
            b = 5
        elif k in ("xtr", "btr", "F"):
            b = 3
        elif k in ("ssq", "mod", "ssq2"):
            b = 0
        elif k == "ssqc":
            b = 1
        elif k == "ynorm":
            continue
        elif k == "rt":
            b = 1
        elif k == "cnt":
            b = 2
        else:
            b = 7
        used[b] = used.get(b, 0) + 1
        plan[s] = (b, used[b])
    return plan


def head(h):
    blk, g, j = h // 8, (h // 4) % 2, h % 4
    if blk == 0:
        return blk, g, j, [0, 1, 4, 5], 3 * P
    keys = [4, 5] + [c for c in (blk - 1, blk, blk + 1) if c < NCH]
    return blk, g, j, keys, 0


def hd_index(h):
    return h // 4 % 2 * 4 + h % 4


def chunk_cols(c):
    return c * P if c < NCH else S + 2 + (c - NCH) * P


class Tally:

    def __init__(self, eng):
        self.eng, self.count, self.last = eng, {}, None

    def __call__(self, sem, value=None):
        n = self.count.get(sem.name, 0) + 1 if value is None else value
        self.count[sem.name] = n
        self.last = (sem, n)
        return sem, 1

    def settle(self):
        if self.last:
            self.eng.wait_ge(*self.last)
            self.last = None


def build(nc, xT, ctxT, stream, consts, cossin, dft, cols, rows, wdt, wrt, w1, w3, w2, ybuf, outT):
    ctx = ExitStack()
    BASE = 16512

    def at(name, off, shape, dt=F32):
        return nc.alloc_sbuf_tensor_at(name, shape, dt, offset=BASE + off)

    ring = at("ring", 0, [P, RING, UNIT])
    dftm = at("dftm", 49152, [P, 2, NCH, S])
    merged = at("merged", 49152, [P, KD, S])
    sq = at("sq", 49152, [P, 12, S])
    ropet = at("ropet", 65536, [P, 4, S])
    V = at("V", 65536, [P, 2, NCH * 256])
    E = at("E", 65536, [P, 2, S])
    Am = at("Am", 65536 + 4096, [P, 2, S])
    pads = at("pads", 73728, [P, 2, 772])
    acc = at("acc", 73728 + 6176, [P, 2, 772])
    th = at("th", 73728 + 12352, [P, 2, 772])
    sc = at("sc", 73728, [P, 3, 640])
    PT = at("PT", 73728 + 7680, [P, 640])
    gth = at("gth", 73728 + 10240, [P, S])
    xdd = at("xdd", 73728 + 12288, [P, S])
    ytmp = at("ytmp", 73728 + 14336, [P, 3, 256])
    amx = at("amx", 73728 + 17408, [P, 32, 8])
    xbcT = at("xbcT", 92288, [P, 6, 770])
    prevS = at("prevS", 92288, [P, 2, NCH, 256])
    tmpS = at("tmpS", 92288 + 8192, [P, 2, 256])
    Gm = at("Gm", 92288 + 10240, [P, 2, P])
    uT = at("uT", 110784, [P, NCH, S])
    hc = at("hc", 118976, [P, KD, SC])
    attT = at("attT", 118976, [P, 4, S])
    qT = at("qT", 127168, [P, 4, S])
    dts = at("dts", 127168, [P, 8, 96])
    ssmT = at("ssmT", 127168, [P, 4, S])
    kT = at("kT", 135360, [P, S])
    kcT = at("kcT", 137408, [P, SC])
    vt = at("vt", 138432, [P, 6, P])
    scT = at("scT", 141504, [P, 4, S])
    zs = at("zs", 149696, [P, NCH, S])
    xs = at("xs", 157888, [P, 6, S])
    btm = at("btm", 157888 + 12288, [P, 6, P])
    cs = at("cs", 173248, [P, 2, S])
    xd = at("xd", 173248, [P, 2, S])
    H = at("H", 177344, [P, KD, S])
    CT = at("CT", 193728, [P, C_N])
    o = 193728 + C_N * 4

    def up(n):
        return (n + 31) // 32 * 32

    QC = at("QC", o, [P, Q_N]); o += up(Q_N * 4)
    RW = at("RW", o, [P, R_N]); o += up(R_N * 4)
    WDT = at("WDT", o, [P, KD, 16]); o += up(512)
    rsx = at("rsx", o, [P, S]); mtmp = at("mtmp", o, [P, S]); o += up(2048)
    rsc = at("rsc", o, [P, SC]); o += up(1024)
    mods = at("mods", o, [P, 48, 2]); o += up(384)
    A1 = at("A1", o, [P, KD, 2]); o += up(64)
    half = at("half", o, [P, 56]); o += up(224)
    sil = at("sil", o, [P, 16]); o += up(64)
    dtv = at("dtv", o, [P, 6, 16]); o += up(384)
    dta = at("dta", o, [P, 6, 16]); o += up(384)
    ea = at("ea", o, [P, 16]); o += up(64)
    dec = at("dec", o, [P, 6, 48]); o += up(1152)
    wdd = at("wdd", o, [P, 6, 16]); o += up(384)
    cds = at("cds", o, [P, 6, 2, 4]); o += up(192)
    yst = at("yst", o, [P, 12]); o += up(64)
    assert o <= 229368 - BASE, o

    ering = at("ering", 0, [P, 2, 3, UNIT])
    h2 = at("h2", 98304, [P, KD, S])
    h2t = at("h2t", 114688, [P, NCH, D])
    m0 = 131072
    WR = at("WR", m0, [P, KD, NE]); m0 += 1024
    lg = at("lg", m0, [P, NCH, NE]); m0 += 512
    sel = at("sel", m0, [P, NCH, NE]); m0 += 512
    selm = at("selm", m0, [P, NCH, NE]); m0 += 512
    oh = at("oh", m0, [P, 2, NCH, NE]); m0 += 1024
    asg = at("asg", m0, [P, NCH, NE]); m0 += 512
    w32 = at("w32", m0, [P, NCH, NE]); m0 += 512
    w32b = at("w32b", m0, [P, NCH, NE]); m0 += 512
    g16 = at("g16", m0, [P, 4, NCH, 16]); m0 += 1024
    g8 = at("g8", m0, [P, 6, NCH, 8]); m0 += 768
    sml = at("sml", m0, [P, 16, NCH]); m0 += 256
    cnt = at("cnt", m0, [P, 4, NE]); m0 += 512
    slotf = at("slotf", m0, [P, 2, NCH]); m0 += 32
    sloti = at("sloti", m0, [P, 2, NCH], U32); m0 += 32
    wts = at("wts", m0, [P, 2, NCH]); m0 += 32
    bex = at("bex", m0, [P, NE]); m0 += 128
    bec = at("bec", m0, [P, 2]); m0 += 32
    brow = at("brow", m0, [1, P], I32); m0 += 512
    nbk = at("nbk", m0, [1, 1], I32); m0 += 32
    pos = at("pos", m0, [P, 2, NCH]); m0 += 32
    oneh = at("oneh", m0, [P, 2, 2, NCH, BLK]); m0 += 4096
    xb = at("xb", m0, [P, 2, KD * BLK]); m0 += 4096
    sg = at("sg", m0, [P, 4 * BLK]); m0 += 1024
    a1 = at("a1", m0, [P, 4 * BLK]); m0 += 1024
    act_ = at("act_", m0, [P, 2, 4 * BLK]); m0 += 2048
    ysb = at("ysb", m0, [BLK, 2, D]); m0 += 8192
    assert m0 <= 173248, m0
    rs2 = at("rs2", 173248, [P, S])
    sq2 = at("sq2", 49152, [P, KD, S])
    gat = at("gat", 0, [P, 2, NCH, D])
    fin = at("fin", 32768, [P, NCH, D])
    sq3 = at("sq3", 49152, [P, KD, S])
    x2 = at("x2", 98304, [P, KD, S])

    psum = ctx.enter_context(nc.psum_tensor("psum", [P, 8, 512], F32))

    def bk(b, n=1):
        return psum[:, b:b + n, :].rearrange("p b n -> p (b n)")

    steps = timeline()
    plan = bank_plan(steps)
    full = [ctx.enter_context(nc.semaphore(f"bank_full{i}")) for i in range(8)]
    empty = [ctx.enter_context(nc.semaphore(f"bank_read{i}")) for i in range(8)]

    def sem(name):
        return ctx.enter_context(nc.semaphore(name))

    x_in, c_in, const_in, cs_in, dft_in, small_in = map(sem, "x_in c_in const_in cs_in dft_in small_in".split())
    unit_in = [sem(f"unit_in{i}") for i in range(RING)]
    ada_free = sem("ada_free")
    y_zero = sem("y_zero")
    x_again, wr_in = sem("x_again"), sem("wr_in")
    dve_c, act_c, pool_c = sem("dve_chain"), sem("act_chain"), sem("pool_chain")
    sq_ready, std_ready, silu_e, sil_ready, prep_ready = map(sem, "sq_ready std_ready silu_e sil_ready prep_ready".split())
    hm_ready, h_ready, padz = map(sem, "hm_ready h_ready padz".split())
    conv_done, tanh_done, xbc_ready, rope_ready = map(sem, "conv_done tanh_done xbc_ready rope_ready".split())
    dt_abs, dt_exp, dta_ready, ea_ready, wdd_ready, cds_ready = map(sem, "dt_abs dt_exp dta_ready ea_ready wdd_ready cds_ready".split())
    z_tanh, sc_ready = sem("z_tanh"), sem("sc_ready")
    smax_ready, exp_done, prob_ready = sem("smax_ready"), sem("exp_done"), sem("prob_ready")
    xdd_ready, xdd_used, state_ready, am_ready, am_used, xd_ready = map(sem, "xdd_ready xdd_used state_ready am_ready am_used xd_ready".split())
    decay_done, m_ready, gm_ready, y_done, ysq_done, ystd, ynorm_done = map(sem, "decay_done m_ready gm_ready y_done ysq_done ystd ynorm_done".split())
    gate_done, merge_done = sem("gate_done"), sem("merge_done")
    xb_full, xb_ready, oneh_ready, gate_mm, up_mm, down_mm = map(sem, "xb_full xb_ready oneh_ready gate_mm up_mm down_mm".split())
    act_ready, ya_done, yd_done, sig_ready, a1_done, pos_done, eq_done = map(sem, "act_ready ya_done yd_done sig_ready a1_done pos_done eq_done".split())
    w_in = [[sem(f"w_in{j}_{k}") for k in range(3)] for j in range(2)]
    y_out, gat_in = [sem(f"y_out{j}") for j in range(2)], [[sem(f"gat_in{k}_{c}") for c in range(NCH)] for k in range(2)]
    fin_ready, fT_full, x2_ready, sq3_ready, ssq3_full, std3, out_ready, out_done, lg_ready, slot_ready = map(
        sem, "fin_ready fT_full x2_ready sq3_ready ssq3_full std3 out_ready out_done lg_ready slot_ready".split())
    x1_done, sq2_ready, h2_pre, h2_ready, half_ready = map(sem, "x1_done sq2_ready h2_pre h2_ready half_ready".split())
    rexp, rt_ready, asg_ready, bex_ready, route_done, brow_done, h2t_done = map(sem, "rexp rt_ready asg_ready bex_ready route_done brow_done h2t_done".split())

    def slot(u):
        return ring[:, u % RING, :]

    def arrived(eng, u):
        eng.wait_ge(unit_in[u % RING], 16 * (u // RING + 1))

    def job_full(eng, s):
        b, n = plan[s]
        eng.wait_ge(full[b], n)

    def job_read(eng, s):
        b, n = plan[s]
        eng.wait_ge(empty[b], n)

    def claim(eng, s):
        b, n = plan[s]
        if n > 1:
            eng.wait_ge(empty[b], n - 1)
        return b

    U_IN = N_ADA1
    first_mix = U_IN + N_IN
    mix_unit = {}
    u = first_mix
    for i, n in enumerate(MIX_ORDER):
        if i == 2:
            ADA2 = u
            u += 8
        mix_unit[n] = u
        u += 3
    U_WO = u
    N_UNITS = u + 2
    in_unit = {"xbc": lambda m: (0, m) if m < 4 else (1, m - 4), "k": lambda m: (1, 2), "v": lambda m: (1, 3),
               "fu": lambda m: (2, m), "q": lambda m: (3, m), "cg": lambda m: (4 + 3 * m // 4, 3 * m % 4),
               "sx": lambda m: (4 + (3 * m + 1) // 4, (3 * m + 1) % 4),
               "bg": lambda m: (4 + (3 * m + 2) // 4, (3 * m + 2) % 4)}
    unit_last = {N_ADA1 - 1: ("mod", 0)}
    for i, x in enumerate([("xbcc", 3), ("vc",), ("fu", 3), ("q", 3), ("cg", 1), ("sx", 2), ("bg", 3), ("z", 3)]):
        unit_last[U_IN + i] = x
    for i in range(8):
        unit_last[ADA2 + i] = ("mod", 1 + i)
    for n, x in mix_unit.items():
        unit_last.update({x: ("gate", n, 3), x + 1: ("proj", n, 7), x + 2: ("gate", n, 7)})

    st_chunk = ([4, 5, 0, 1, 2, 3], [5, 4, 3, 2, 1, 0])
    st_steps = [s for s in steps if s[0] == "st"]
    st_index = {s: i for i, s in enumerate(st_steps)}
    st_prev = {s: st_steps[i - 1] for i, s in enumerate(st_steps) if i}

    block = ctx.enter_context(nc.Block())

    @block.sync
    def _(sp):
        sp.dma_start(H[:, :, :], xT).then_inc(x_in, 16)
        sp.dma_start(QC[:, :], cols).then_inc(small_in, 16)
        sp.dma_start(RW[:, :], rows).then_inc(small_in, 16)
        sp.dma_start(CT[:, :], consts).then_inc(const_in, 16)
        sp.dma_start(hc[:, :, :], ctxT).then_inc(c_in, 16)
        sp.dma_start(WDT[:, :, :], wdt).then_inc(small_in, 16)
        for u in range(N_UNITS):
            if u >= RING:
                if u - RING < N_ADA1 - 1:
                    sp.wait_ge(ada_free, u - RING + 1)
                else:
                    job_full(sp, unit_last[u - RING])
            sp.dma_start(slot(u), stream[u]).then_inc(unit_in[u % RING], 16)
            if u == RING - 1:
                sp.dma_start(cs[:, :, :], cossin).then_inc(cs_in, 16)
            if u == N_ADA1 + 2:
                job_full(sp, ("ssq",))
                job_full(sp, ("ssqc",))
                sp.dma_start(dftm[:, :, :, :], dft).then_inc(dft_in, 16)
            if u == U_IN + N_IN:
                zero = CT[:, C_MASK:C_MASK + 256].unsqueeze(1).to_broadcast([P, 2 * PAIRS * BLK * D // (P * 256), 256])
                sp.dma_start(ybuf.rearrange("b (q r) n -> (b q) (r n)", q=1).rearrange("b (q n) -> (b q) n", n=256)
                             .rearrange("(p r) n -> p r n", p=P), zero).then_inc(y_zero, 16)
        job_full(sp, ("gate", MIX_ORDER[-1], 7))
        sp.dma_start(H[:, :, :], xT).then_inc(x_again, 16)
        job_full(sp, ("proj", MIX_ORDER[-1], 7))
        sp.dma_start(WR[:, :, :], wrt).then_inc(wr_in, 16)

        job_full(sp, ("bexp",))
        sp.wait_ge(route_done, 2)
        n = sp.value_load(nbk[0:1, 0:1], min_val=1, max_val=MAXB)
        with sp.Fori(0, PAIRS) as i:
            for j in range(2):
                b = i * 2 + j
                with sp.If(b < n):
                    e = sp.value_load(brow[0:1, bass.ds(b, 1)], min_val=0, max_val=NE - 1)
                    for k, (w, used) in enumerate(((w1, gate_mm), (w3, up_mm), (w2, down_mm))):
                        sp.wait_ge(used, b + 1)
                        sp.dma_start(ering[:, j, k, :], w[bass.ds(e, 1), :, :].rearrange("a p n -> (a p) n")
                                     ).then_inc(w_in[j][k], 16)
        for k in range(KD):
            sp.wait_ge(out_ready, k + 1)
            sp.dma_start(outT[:, k, :], x2[:, k, :]).then_inc(out_done, 16)
        sp.wait_ge(out_done, 16 * KD)

    @block.tensor
    def _(pe):
        def mm(out, lhsT, rhs, start, stop):
            return nc.tensor.matmul(out, lhsT, rhs, start=start, stop=stop)

        ID = CT[:, C_ID:C_ID + P]

        def project(s, cols, unit, tile, ctx_side):
            b = claim(pe, s)
            w = slot(unit)
            for k in range(KD):
                rhs = hc[:, k, :] if ctx_side else H[:, k, :]
                ins = mm(bk(b)[:, 0:cols], w[:, k * S + tile * P:k * S + tile * P + P], rhs, k == 0, k == KD - 1)
            return ins.then_inc(full[b], 1)

        for s in steps:
            k0 = s[0]
            if k0 in ("ssq", "ssqc"):
                if k0 == "ssq":
                    pe.wait_ge(const_in, 16)
                b = claim(pe, s)
                n = S if k0 == "ssq" else SC
                for k in range(KD):
                    if k0 == "ssq":
                        pe.wait_ge(sq_ready, k + 1)
                        rhs = sq[:, k, :]
                    else:
                        pe.wait_ge(sq_ready, KD + k // 2 + 1)
                        rhs = sq[:, KD + k // 2, (k % 2) * SC:(k % 2) * SC + SC]
                    ins = mm(bk(b)[:, 0:n], CT[:, C_ONE:C_ONE + P], rhs, k == 0, k == KD - 1)
                ins.then_inc(full[b], 1)
            elif k0 == "mod":
                b = claim(pe, s)
                units = range(4) if s[1] == 0 else [ADA2 + s[1] - 1]
                if s[1] == 0:
                    pe.wait_ge(sil_ready, 1)
                for ui, u in enumerate(units):
                    arrived(pe, u)
                    for j in range(4):
                        o = (ui * 4 + j) * 2
                        for k in range(KD):
                            ins = mm(bk(b)[:, o:o + 2], slot(u)[:, k * S + j * P:k * S + j * P + P],
                                     sil[:, 2 * k:2 * k + 2], k == 0, k == KD - 1)
                    if u != units[-1]:
                        ins.then_inc(ada_free, 1)
                ins.then_inc(full[b], 1)
            elif k0 in ("xbc", "xbcc", "k", "kc", "fu", "q", "cg", "sx", "bg"):
                ctx_side = k0 in ("xbcc", "kc")
                base, m = {"xbcc": "xbc", "kc": "k"}.get(k0, k0), s[1] if len(s) > 1 else 0
                iu, tile = in_unit[base](m)
                arrived(pe, U_IN + iu)
                if s == ("xbc", 0):
                    pe.wait_ge(h_ready, KD)
                if s == ("xbcc", 0):
                    pe.wait_ge(h_ready, 2 * KD)
                project(s, SC if ctx_side else S, U_IN + iu, tile, ctx_side)
            elif k0 in ("v", "vc"):
                b = claim(pe, s)
                for c in range(NCH if k0 == "v" else NCC):
                    for k in range(KD):
                        src = H if k0 == "v" else hc
                        ins = mm(bk(b)[:, c * P:c * P + P], src[:, k, c * P:c * P + P],
                                 slot(U_IN + 1)[:, k * S + 3 * P:k * S + 4 * P], k == 0, k == KD - 1)
                ins.then_inc(full[b], 1)
            elif k0 == "dt":
                b = claim(pe, s)
                pe.wait_ge(small_in, 48)
                for c in range(6):
                    src, cc = (H, c) if c < NCH else (hc, c - NCH)
                    for k in range(KD):
                        ins = mm(bk(b)[:, c * 16:c * 16 + 16], src[:, k, cc * P:cc * P + P], WDT[:, k, :],
                                 k == 0, k == KD - 1)
                ins.then_inc(full[b], 1)
            elif k0 == "z":
                b = claim(pe, s)
                c = s[1]
                arrived(pe, U_IN + 7)
                for k in range(KD):
                    ins = mm(bk(b), H[:, k, c * P:c * P + P], slot(U_IN + 7)[:, k * S:k * S + S], k == 0, k == KD - 1)
                ins.then_inc(full[b], 1)
            elif k0 == "rot":
                b = claim(pe, s)
                job_read(pe, ("k",) if s[1] == 0 else ("q", s[1] - 1))
                mm(bk(b), CT[:, C_PERM:C_PERM + P], ropet[:, s[1] % 2, :], True, True).then_inc(full[b], 1)
            elif k0 == "dec":
                b = claim(pe, s)
                pe.wait_ge(dta_ready, 1)
                for c in range(6):
                    o = c * 48
                    for col, (m, r0, r1) in zip((0, 8, 16, 24, 32), ((C_LE, 0, 8), (C_GE, 8, 16), (C_GT, 0, 8),
                                                                     (C_LT, 8, 16), (C_ONE, 0, 16))):
                        ins = mm(bk(b)[:, o + col:o + col + r1 - r0], CT[:, m:m + P], dta[:, c, r0:r1], True, True)
                ins.then_inc(full[b], 1)
            elif k0 == "xtr":
                b = claim(pe, s)
                pe.wait_ge(xbc_ready, 6)
                o = chunk_cols(s[1])
                for m in range(4):
                    ins = nc.tensor.transpose(bk(b)[:, m * P:m * P + P], xbcT[:, m, o:o + P], ID)
                ins.then_inc(full[b], 1)
            elif k0 == "btr":
                b = claim(pe, s)
                for i in range(3):
                    o = chunk_cols(3 * s[1] + i)
                    ins = nc.tensor.transpose(bk(b)[:, i * P:i * P + P], xbcT[:, 4, o:o + P], ID)
                ins.then_inc(full[b], 1)
            elif k0 == "V":
                b = claim(pe, s)
                ft = s[1]
                job_read(pe, ("fu", ft))
                for c in range(NCH):
                    ins = mm(bk(b, 2)[:, c * 256:c * 256 + 256], uT[:, ft, c * P:c * P + P],
                             CT[:, C_BD:C_BD + 256], True, True)
                ins.then_inc(full[b], 1)
            elif k0 == "F":
                b = claim(pe, s)
                ft = s[1]
                job_read(pe, ("V", ft))
                pe.wait_ge(dft_in, 16)
                for i in range(8):
                    c, part = i // 2, i % 2
                    ins = mm(bk(b), V[:, ft % 2, c * 256 + part * P:c * 256 + part * P + P],
                             dftm[:, part, c, :], i == 0, i == 7)
                ins.then_inc(full[b], 1)
            elif k0 == "st":
                d, k = s[1:]
                b = claim(pe, s)
                pe.wait_ge(xdd_ready, st_index[s] + 1)
                if s == ("st", 0, 0):
                    job_read(pe, ("btr", 1))
                c = st_chunk[d][k]
                for g in range(2):
                    ins = mm(bk(b)[g * 64:g * 64 + 64, 0:256], btm[:, c, g * 64:g * 64 + 64],
                             xdd[:, g * 256:g * 256 + 256], True, True)
                ins.then_inc(full[b], 1)
            elif k0 == "G":
                c, g = s[1:]
                b = claim(pe, s)
                o = c * P
                mm(bk(b)[:, 0:P], xbcT[g * 64:g * 64 + 64, 4, o:o + P], xbcT[g * 64:g * 64 + 64, 5, o:o + P],
                   True, True).then_inc(full[b], 1)
            elif k0 == "seg":
                c, g, d = s[1:]
                b = claim(pe, s)
                pe.wait_ge(am_ready, 2 * (2 * c + g) + d + 1)
                m = C_GT if d == 0 else C_LT
                mm(bk(b), CT[:, m:m + P], Am[:, d, :], True, True).then_inc(full[b], 1)
            elif k0 == "yoff":
                c, g = s[1:]
                b = claim(pe, s)
                for d in range(2):
                    if (c, g) == (0, 0):
                        job_read(pe, ("st", d, 4))
                    ins = mm(bk(b)[:, d * 256:d * 256 + 256], xbcT[g * 64:g * 64 + 64, 5, c * P:c * P + P],
                             prevS[g * 64:g * 64 + 64, d, c, :], True, True)
                ins.then_inc(full[b], 1)
            elif k0 == "y":
                c, g = s[1:]
                b = claim(pe, s)
                pe.wait_ge(m_ready, 2 * (2 * c + g + 1))
                pe.wait_ge(xd_ready, 2 * (c + 1))
                for h in range(4):
                    for d in range(2):
                        ins = mm(bk(b)[:, h * HD:h * HD + HD], E[:, d, h * P:h * P + P],
                                 xd[:, d, (g * 4 + h) * HD:(g * 4 + h) * HD + HD], d == 0, d == 1)
                ins.then_inc(full[b], 1)
            elif k0 == "ytr":
                b = claim(pe, s)
                c = s[1]
                pe.wait_ge(ynorm_done, c + 1)
                for m in range(4):
                    ins = nc.tensor.transpose(bk(b)[:, m * P:m * P + P], zs[:, c, m * P:m * P + P], ID)
                ins.then_inc(full[b], 1)
            elif k0 == "S":
                blk, g, j, keys, _ = head(s[1])
                b = claim(pe, s)
                if s[1] == 0:
                    pe.wait_ge(rope_ready, 5)
                    job_read(pe, ("kc",))
                rows_ = slice(g * 64, g * 64 + 64)
                for i, c in enumerate(keys):
                    rhs = kT[rows_, c * P:c * P + P] if c < NCH else kcT[rows_, (c - NCH) * P:(c - NCH) * P + P]
                    ins = mm(bk(b, 2)[:, i * P:i * P + P], qT[rows_, j, blk * P:blk * P + P], rhs, True, True)
                ins.then_inc(full[b], 1)
            elif k0 == "T":
                h = s[1]
                b = claim(pe, s)
                pe.wait_ge(prob_ready, h + 1)
                for i in range(len(head(h)[3])):
                    ins = nc.tensor.transpose(bk(b, 2)[:, i * P:i * P + P], sc[:, h % 3, i * P:i * P + P], ID)
                ins.then_inc(full[b], 1)
            elif k0 == "O":
                h = s[1]
                blk, g, j, keys, _ = head(h)
                b = claim(pe, s)
                job_read(pe, ("T", h))
                if h == 0:
                    job_read(pe, ("vc",))
                for i, c in enumerate(keys):
                    ins = mm(bk(b)[g * 64:g * 64 + 64, 0:P], vt[:, c, g * 64:g * 64 + 64], PT[:, i * P:i * P + P],
                             i == 0, i == len(keys) - 1)
                ins.then_inc(full[b], 1)
            elif k0 == "gate":
                n, d = s[1:]
                u = mix_unit[n] + (0 if d < 4 else 2)
                arrived(pe, u)
                project(s, S, u, d % 4, False)
            elif k0 == "proj":
                n, d = s[1:]
                b = claim(pe, s)
                if d == 0:
                    arrived(pe, mix_unit[n] + 1)
                    job_read(pe, {3: ("bg", 3), 2: ("F", 3), 0: ("O", 31), 1: ("ytr", 3)}[n])
                src = {3: scT, 2: uT, 0: attT, 1: ssmT}[n]
                for k in range(4):
                    ins = mm(bk(b), slot(mix_unit[n] + 1)[:, k * D + d * P:k * D + d * P + P], src[:, k, :],
                             k == 0, k == 3)
                ins.then_inc(full[b], 1)
            elif k0 == "wo":
                d = s[1]
                b = claim(pe, s)
                arrived(pe, U_WO + d // 4)
                pe.wait_ge(merge_done, 32)
                for k in range(KD):
                    ins = mm(bk(b), slot(U_WO + d // 4)[:, k * S + (d % 4) * P:k * S + (d % 4) * P + P],
                             merged[:, k, :], k == 0, k == KD - 1)
                ins.then_inc(full[b], 1)
            elif k0 == "ssq2":
                b = claim(pe, s)
                for k in range(KD):
                    pe.wait_ge(sq2_ready, k + 1)
                    ins = mm(bk(b), CT[:, C_ONE:C_ONE + P], sq2[:, k, :], k == 0, k == KD - 1)
                ins.then_inc(full[b], 1)
            elif k0 == "h2tr":
                b = claim(pe, s)
                c = s[1]
                pe.wait_ge(h2_ready, KD)
                for k in range(KD):
                    ins = nc.tensor.transpose(bk(b, 2)[:, k * P:k * P + P], h2[:, k, c * P:c * P + P], ID)
                ins.then_inc(full[b], 1)
            elif k0 == "rt":
                b = claim(pe, s)
                pe.wait_ge(wr_in, 16)
                for c in range(NCH):
                    for k in range(KD):
                        ins = mm(bk(b)[:, c * NE:c * NE + NE], h2[:, k, c * P:c * P + P], WR[:, k, :],
                                 k == 0, k == KD - 1)
                ins.then_inc(full[b], 1)
            elif k0 == "cnt":
                b = claim(pe, s)
                pe.wait_ge(asg_ready, 1)
                ones = CT[:, C_ONE:C_ONE + P]
                for c in range(NCH):
                    mm(bk(b)[:, 0:NE], ones, asg[:, c, :], c == 0, c == NCH - 1)
                for c in range(NCH):
                    for c2 in range(c + 1):
                        ins = mm(bk(b)[:, NE + c * NE:NE + c * NE + NE],
                                 CT[:, C_LT:C_LT + P] if c2 == c else ones, asg[:, c2, :], c2 == 0, c2 == c)
                ins.then_inc(full[b], 1)
            elif k0 == "bexp":
                b = claim(pe, s)
                pe.wait_ge(bex_ready, 1)
                mm(bk(b)[0:1, 0:P], bec[:, 0:1], ID, True, True).then_inc(full[b], 1)

        for credit, v in ((gate_mm, 2), (up_mm, 2), (down_mm, 2)):
            pe.sem_inc(credit, v)
        XB, HB, YB = bk(3), bk(4), bk(5, 2)

        def gather(par):
            for d in range(KD):
                for c in range(NCH):
                    ins = mm(XB[:, d * BLK:d * BLK + BLK], h2t[:, c, d * P:d * P + P], oneh[:, par, 0, c, :],
                             c == 0, c == NCH - 1)
            return ins

        for s in (("h2tr", c) for c in range(NCH)):
            job_read(pe, s)
        pe.wait_ge(route_done, 2)
        pe.wait_ge(oneh_ready, 1)
        gather(0).then_inc(xb_full, 1)
        n = pe.value_load(nbk[0:1, 0:1], min_val=1, max_val=MAXB)
        with pe.Fori(0, PAIRS) as i:
            for j in range(2):
                b = i * 2 + j
                with pe.If(b < n):
                    pe.wait_ge(xb_ready, b + 1)
                    pe.wait_ge(act_ready, b + 1)
                    for k, done in ((0, gate_mm), (1, up_mm)):
                        pe.wait_ge(w_in[j][k], i * 16 + 16)
                        for f in range(4):
                            for d in range(KD):
                                o = (4 * k + f) * BLK
                                ins = mm(HB[:, o:o + BLK], ering[:, j, k, d * S + f * P:d * S + f * P + P],
                                         xb[:, j, d * BLK:d * BLK + BLK], d == 0, d == KD - 1)
                        ins.then_inc(done, 1)
                    pe.wait_ge(oneh_ready, b + 2)
                    gather(1 - j).then_inc(xb_full, 1)
                    pe.wait_ge(act_ready, b + 2)
                    pe.wait_ge(ya_done, b + 1)
                    pe.wait_ge(yd_done, b + 1)
                    pe.wait_ge(w_in[j][2], i * 16 + 16)
                    for hf in range(2):
                        for f in range(4):
                            ins = mm(YB[0:BLK, hf * S:hf * S + S], act_[:, j, f * BLK:f * BLK + BLK],
                                     ering[:, j, 2, f * D + hf * S:f * D + hf * S + S], f == 0, f == 3)
                    ins.then_inc(down_mm, 1)
        for k in range(KD):
            b = k % 2
            if k == 0:
                pe.wait_ge(fin_ready, NCH)
            if k >= 2:
                pe.wait_ge(x2_ready, k - 1)
            for c in range(NCH):
                ins = nc.tensor.transpose(bk(b)[:, c * P:c * P + P], fin[:, c, k * P:k * P + P], ID)
            ins.then_inc(fT_full, 1)
        for k in range(KD):
            pe.wait_ge(sq3_ready, k + 1)
            ins = mm(bk(2), CT[:, C_ONE:C_ONE + P], sq3[:, k, :], k == 0, k == KD - 1)
        ins.then_inc(ssq3_full, 1)

    @block.scalar
    def _(act):
        t = Tally(act)
        def A(out, in_, f, **kw):
            return nc.scalar.activation(out, in_, f, **kw)

        act.wait_ge(small_in, 48)
        A(sil[:, :], QC[:, Q_C:Q_C + 16], ACT.Exp, scale=-1.0).then_inc(*t(silu_e))
        A(ea[:, :], RW[:, R_ALOG:R_ALOG + 16], ACT.Exp).then_inc(*t(ea_ready))
        act.wait_ge(x_in, 16)
        for k in range(KD):
            A(sq[:, k, :], H[:, k, :], ACT.Square).then_inc(*t(sq_ready))
        act.wait_ge(c_in, 16)
        for k in range(NCC * 2):
            A(sq[:, KD + k, :], hc[:, 2 * k:2 * k + 2, :].rearrange("p a n -> p (a n)"), ACT.Square).then_inc(*t(sq_ready))
        convs, ropes, z_i = 0, 0, 0
        for s in steps:
            k0 = s[0]
            t.settle()
            if k0 in ("ssq", "ssqc"):
                b, _n = plan[s]
                job_full(act, s)
                n, out = (S, rsx) if k0 == "ssq" else (SC, rsc)
                A(out[:, :], bk(b)[:, 0:n], ACT.Sqrt, scale=1.0 / D, bias=QC[:, Q_EPS:Q_EPS + 1]).then_inc(*t(empty[b], plan[s][1]))
            elif s == ("mod", 0):
                for w, dst in enumerate((H, hc)):
                    for k in range(KD):
                        act.wait_ge(hm_ready, w * KD + k + 1)
                        A(dst[:, k, :], dst[:, k, :], ACT.Identity, bias=mods[:, k, w:w + 1]).then_inc(*t(h_ready))
            elif k0 in ("xbc", "xbcc"):
                m = s[1]
                b, _n = plan[s]
                if k0 == "xbc" and m >= 2:
                    act.wait_ge(conv_done, m - 1)
                if s == ("xbc", 0):
                    act.wait_ge(padz, 1)
                job_full(act, s)
                if k0 == "xbc":
                    A(pads[:, m % 2, 1:1 + S], bk(b), ACT.Copy).then_inc(*t(empty[b], plan[s][1]))
                else:
                    A(pads[:, m % 2, S + 3:S + 3 + SC], bk(b)[:, 0:SC], ACT.Copy).then_inc(*t(empty[b], plan[s][1]))
                    for mm_ in ([m - 1] if m else []) + ([m] if m == 5 else []):
                        act.wait_ge(conv_done, mm_ + 1)
                        if mm_ >= 2:
                            act.wait_ge(xbc_ready, mm_ - 1)
                        A(th[:, mm_ % 2, 0:770], acc[:, mm_ % 2, 0:770], ACT.Tanh).then_inc(*t(tanh_done))
            elif k0 in ("k", "q"):
                i = 0 if k0 == "k" else s[1] + 1
                b, _n = plan[s]
                job_full(act, s)
                if i >= 2:
                    act.wait_ge(rope_ready, i - 1)
                A(ropet[:, i % 2, :], bk(b), ACT.Copy).then_inc(*t(empty[b], plan[s][1]))
            elif k0 in ("kc", "v", "vc", "fu"):
                b, _n = plan[s]
                job_full(act, s)
                out = {"kc": lambda: kcT[:, :], "v": lambda: vt[:, 0:4, :].rearrange("p a n -> p (a n)"),
                       "vc": lambda: vt[:, 4:6, :].rearrange("p a n -> p (a n)"), "fu": lambda: uT[:, s[1], :]}[k0]()
                n = SC if k0 in ("kc", "vc") else S
                A(out, bk(b)[:, 0:n], ACT.Copy).then_inc(*t(empty[b], plan[s][1]))
            elif k0 == "dt":
                act.wait_ge(dt_abs, 1)
                A(dts[:, 2, :], dts[:, 1, :], ACT.Exp, scale=-1.0).then_inc(*t(dt_exp))
            elif k0 == "dec":
                b, _n = plan[s]
                job_full(act, s)
                A(dec[:, :, :].rearrange("p a n -> p (a n)"), bk(b)[:, 0:288], ACT.Exp).then_inc(*t(empty[b], plan[s][1]))
            elif k0 == "cg":
                m = s[1]
                b, _n = plan[s]
                job_full(act, s)
                if m == 0:
                    act.wait_ge(xbc_ready, 6)
                else:
                    job_read(act, ("sx", m - 1))
                A(th[:, 0, 0:S], bk(b), ACT.Copy).then_inc(*t(empty[b], plan[s][1]))
            elif k0 == "z":
                c = s[1]
                b, _n = plan[s]
                job_full(act, s)
                if c == 0:
                    job_read(act, ("sx", 3))
                else:
                    job_read(act, ("z", c - 1))
                A(th[:, 0, 0:S], bk(b), ACT.Tanh, scale=0.5).then_inc(*t(z_tanh))
            elif k0 in ("xtr", "btr"):
                b, _n = plan[s]
                job_full(act, s)
                if k0 == "xtr":
                    A(xs[:, s[1], :], bk(b), ACT.Copy).then_inc(*t(empty[b], plan[s][1]))
                else:
                    A(btm[:, 3 * s[1]:3 * s[1] + 3, :].rearrange("p a n -> p (a n)"), bk(b)[:, 0:384],
                      ACT.Copy).then_inc(*t(empty[b], plan[s][1]))
            elif k0 == "V":
                ft = s[1]
                b, _n = plan[s]
                job_full(act, s)
                if ft == 0:
                    act.wait_ge(rope_ready, 5)
                if ft >= 2:
                    job_full(act, ("F", ft - 2))
                A(V[:, ft % 2, :], bk(b, 2), ACT.Copy).then_inc(*t(empty[b], plan[s][1]))
            elif k0 == "S":
                h = s[1]
                W = len(head(h)[3]) * P
                act.wait_ge(smax_ready, h + 1)
                A(sc[:, h % 3, 0:W], sc[:, h % 3, 0:W], ACT.Exp, bias=amx[:, h, 1:2],
                  accum_out=amx[:, h, 2:3]).then_inc(*t(exp_done))
                A(amx[:, h, 3:4], RW[:, R_SINK + hd_index(h):R_SINK + hd_index(h) + 1], ACT.Exp,
                  bias=amx[:, h, 1:2]).then_inc(*t(exp_done))
            elif k0 == "T":
                h = s[1]
                b, _n = plan[s]
                W = len(head(h)[3]) * P
                job_full(act, s)
                if h == 0:
                    job_read(act, ("z", 3))
                else:
                    job_full(act, ("O", h - 1))
                A(PT[:, 0:W], bk(b, 2)[:, 0:W], ACT.Copy).then_inc(*t(empty[b], plan[s][1]))
            elif k0 == "seg":
                c, g, d = s[1:]
                b, _n = plan[s]
                job_full(act, s)
                if 2 * c + g == 0:
                    job_full(act, ("F", 3))
                else:
                    job_full(act, ("y", (2 * c + g - 1) // 2, (2 * c + g - 1) % 2))
                A(E[:, d, :], bk(b), ACT.Exp).then_inc(*t(empty[b], plan[s][1]))
            elif k0 == "ynorm":
                act.wait_ge(y_done, 8)
                for c in range(NCH):
                    t.settle()
                    A(E[:, 0, :], zs[:, c, :], ACT.Square, accum_out=yst[:, c:c + 1]).then_inc(*t(ysq_done))
                act.wait_ge(ysq_done, NCH)
                A(yst[:, 4:8], yst[:, 0:4], ACT.Sqrt, scale=1.0 / S, bias=QC[:, Q_EPS4:Q_EPS4 + 1]).then_inc(*t(ystd))
            elif k0 == "gate":
                n, d = s[1:]
                b, _n = plan[s]
                job_full(act, s)
                i = MIX_ORDER.index(n) * 8 + d
                if i:
                    job_read(act, ("proj", MIX_ORDER[(i - 1) // 8], (i - 1) % 8))
                else:
                    job_read(act, ("z", 3))
                    act.wait_ge(half_ready, 1)
                A(gth[:, :], bk(b), ACT.Tanh, scale=0.5, bias=half[:, n * 8 + d:n * 8 + d + 1]).then_inc(*t(empty[b], plan[s][1]))
            elif k0 == "ssq2":
                for k in range(KD):
                    if k == 0:
                        job_full(act, ("wo", 7))
                    job_read(act, ("wo", k))
                    A(sq2[:, k, :], H[:, k, :], ACT.Square).then_inc(*t(sq2_ready))
                b, _n = plan[s]
                job_full(act, s)
                A(rs2[:, :], bk(b), ACT.Sqrt, scale=1.0 / D, bias=QC[:, Q_EPS:Q_EPS + 1]).then_inc(*t(empty[b], plan[s][1]))
                for k in range(KD):
                    act.wait_ge(h2_pre, k + 1)
                    A(h2[:, k, :], h2[:, k, :], ACT.Identity, bias=mods[:, 24 + k, 0:1]).then_inc(*t(h2_ready))
            elif k0 == "h2tr":
                b, _n = plan[s]
                job_full(act, s)
                A(h2t[:, s[1], :], bk(b, 2), ACT.Copy).then_inc(*t(empty[b], plan[s][1]))
            elif k0 == "rt":
                act.wait_ge(lg_ready, 1)
                A(w32[:, :, :], lg[:, :, :], ACT.Exp, scale=-1.0).then_inc(*t(rexp))

        act.sem_inc(ya_done, 1)
        for j in range(2):
            act.sem_inc(y_out[j], 16)
        HB, YB = bk(4), bk(5)
        act.wait_ge(route_done, 2)
        act.wait_ge(y_zero, 16)
        n = act.value_load(nbk[0:1, 0:1], min_val=1, max_val=MAXB)
        with act.Fori(0, PAIRS) as i:
            for j in range(2):
                b = i * 2 + j
                with act.If(b < n):
                    act.wait_ge(up_mm, b + 3)
                    A(sg[:, :], HB[:, 0:4 * BLK], ACT.Sigmoid).then_inc(sig_ready, 1)
                    act.wait_ge(down_mm, b + 3)
                    act.wait_ge(y_out[j], i * 16 + 16)
                    A(ysb[:, j, 0:S], YB[0:BLK, :], ACT.Copy).then_inc(ya_done, 1)
                    act.wait_ge(yd_done, b + 2)
                    act.wait_ge(ya_done, b + 2)
                    act.dma_start(ybuf[bass.ds(b, 1), :, :].rearrange("a p n -> (a p) n"), ysb[:, j, :]
                                  ).then_inc(y_out[j], 16)
                with act.Else():
                    act.sem_inc(y_out[j], 16)
        for k in range(KD):
            act.wait_ge(x2_ready, k + 1)
            A(sq3[:, k, :], x2[:, k, :], ACT.Square).then_inc(sq3_ready, 1)
        act.wait_ge(ssq3_full, 1)
        A(rs2[:, :], bk(2), ACT.Sqrt, scale=1.0 / D, bias=QC[:, Q_EPS:Q_EPS + 1]).then_inc(std3, 1)

    @block.vector
    def _(v):
        t = Tally(v)
        V_ = nc.vector

        def link(ins):
            ins.then_inc(*t(dve_c))
            t.settle()

        def TT(out, a, b, op):
            return V_.tensor_tensor(out, a, b, op)

        link(V_.memset(pads[:, :, :], 0.0))
        V_.memset(yst[:, :], 0.0).then_inc(*t(padz))
        v.wait_ge(small_in, 48)
        V_.tensor_scalar(half[:, :], QC[:, Q_BG:Q_BG + 56], 0.5, None, ALU.mult).then_inc(*t(half_ready))
        v.wait_ge(silu_e, 1)
        link(V_.tensor_scalar(sil[:, :], sil[:, :], 1.0, None, ALU.add))
        link(V_.reciprocal(sil[:, :], sil[:, :]))
        TT(sil[:, :], sil[:, :], QC[:, Q_C:Q_C + 16], ALU.mult).then_inc(*t(sil_ready))

        def conv(x, w, a, n):
            link(V_.scalar_tensor_tensor(a, x[:, 1:1 + n], w[1], a, ALU.mult, ALU.add))
            return V_.scalar_tensor_tensor(a, x[:, 2:2 + n], w[2], a, ALU.mult, ALU.add)

        def xbc_finish(m):
            v.wait_ge(tanh_done, m + 1)
            V_.scalar_tensor_tensor(xbcT[:, m, :], th[:, m % 2, 0:770], 1.0, acc[:, m % 2, 0:770], ALU.add,
                                    ALU.mult).then_inc(*t(xbc_ready))

        def norm_probs(h):
            W = len(head(h)[3]) * P
            v.wait_ge(exp_done, 2 * h + 2)
            link(TT(amx[:, h, 4:5], amx[:, h, 2:3], amx[:, h, 3:4], ALU.add))
            link(V_.reciprocal(amx[:, h, 5:6], amx[:, h, 4:5]))
            V_.tensor_scalar(sc[:, h % 3, 0:W], sc[:, h % 3, 0:W], amx[:, h, 5:6], None, ALU.mult).then_inc(*t(prob_ready))

        def hb(ap, n):
            return ap.unsqueeze(2).to_broadcast([P, ap.shape[1], n])

        for s in steps:
            k0 = s[0]
            t.settle()
            b = plan[s][0] if s in plan else None
            if s == ("mod", 0):
                job_read(v, ("ssq",))
                link(V_.reciprocal(rsx[:, :], rsx[:, :]))
                job_read(v, ("ssqc",))
                link(V_.reciprocal(rsc[:, :], rsc[:, :]))
                job_full(v, s)
                TT(mods[:, 0:16, :], bk(b)[:, 0:32].rearrange("p (j w) -> p j w", w=2),
                   hb(QC[:, Q_BADA:Q_BADA + 16], 2), ALU.add).then_inc(*t(empty[b], plan[s][1]))
                job_read(v, s)
                link(V_.scalar_tensor_tensor(A1[:, :, :], mods[:, 8:16, :], 1.0, hb(QC[:, Q_G1:Q_G1 + 8], 2),
                                             ALU.add, ALU.mult))
                for k in range(KD):
                    V_.scalar_tensor_tensor(H[:, k, :], H[:, k, :], A1[:, k, 0:1], rsx[:, :], ALU.mult,
                                            ALU.mult).then_inc(*t(hm_ready))
                for k in range(KD):
                    V_.scalar_tensor_tensor(hc[:, k, :], hc[:, k, :], A1[:, k, 1:2], rsc[:, :], ALU.mult,
                                            ALU.mult).then_inc(*t(hm_ready))
            elif k0 == "mod":
                job_full(v, s)
                o = 16 + 4 * (s[1] - 1)
                TT(mods[:, o:o + 4, :], bk(b)[:, 0:8].rearrange("p (j w) -> p j w", w=2),
                   hb(QC[:, Q_BADA + o:Q_BADA + o + 4], 2), ALU.add).then_inc(*t(empty[b], plan[s][1]))
            elif k0 == "xbcc":
                m = s[1]
                job_read(v, ("xbc", m))
                job_read(v, s)
                w = [half[:, 32 + q * 6 + m:33 + q * 6 + m] for q in range(3)]
                x, a = pads[:, m % 2, :], acc[:, m % 2, 0:770]
                link(V_.tensor_scalar(a, x[:, 0:770], w[0], half[:, 50 + m:51 + m], ALU.mult, ALU.add))
                conv(x, w, a, 770).then_inc(*t(conv_done))
                if m:
                    xbc_finish(m - 1)
                if m == 5:
                    xbc_finish(5)
            elif k0 == "dt":
                job_full(v, s)
                T_ = [dts[:, i, :] for i in range(8)]
                x3 = dts[:, 0, :].rearrange("p (c n) -> p c n", n=16)
                TT(x3, bk(b)[:, 0:96].rearrange("p (c n) -> p c n", n=16),
                   RW[:, R_DTB:R_DTB + 16].unsqueeze(1).to_broadcast([P, 6, 16]), ALU.add).then_inc(*t(empty[b], plan[s][1]))
                job_read(v, s)
                V_.scalar_tensor_tensor(T_[1], T_[0], -1.0, T_[0], ALU.mult, ALU.max).then_inc(*t(dt_abs))
                v.wait_ge(dt_exp, 1)
                link(V_.tensor_scalar(T_[3], T_[2], 2.0, None, ALU.add))
                link(V_.reciprocal(T_[3], T_[3]))
                link(TT(T_[3], T_[2], T_[3], ALU.mult))
                link(TT(T_[4], T_[3], T_[3], ALU.mult))
                link(V_.tensor_scalar(T_[5], T_[4], 1.0 / 15, None, ALU.mult))
                for q in (13, 11, 9, 7, 5, 3):
                    link(V_.scalar_tensor_tensor(T_[5], T_[5], 1.0 / q, T_[4], ALU.add, ALU.mult))
                link(V_.scalar_tensor_tensor(T_[5], T_[5], 1.0, T_[3], ALU.add, ALU.mult))
                link(V_.tensor_scalar(T_[6], T_[0], 0.0, None, ALU.max))
                link(V_.scalar_tensor_tensor(dtv[:, :, :].rearrange("p c n -> p (c n)"), T_[5], 2.0, T_[6],
                                             ALU.mult, ALU.add))
                v.wait_ge(ea_ready, 1)
                V_.scalar_tensor_tensor(dta[:, :, :], dtv[:, :, :], -1.0,
                                        ea[:, :].unsqueeze(1).to_broadcast([P, 6, 16]), ALU.mult,
                                        ALU.mult).then_inc(*t(dta_ready))
            elif k0 == "dec":
                job_read(v, s)
                TT(wdd[:, :, :], dtv[:, :, :], dec[:, :, 16:32], ALU.mult).then_inc(*t(wdd_ready))
                for g in range(2):
                    r = slice(g * 64, g * 64 + 64)
                    for d in range(2):
                        V_.tensor_copy(cds[r, :, d, :], dec[r, :, 32 + d * 8 + g * 4:36 + d * 8 + g * 4]).then_inc(*t(cds_ready))
            elif k0 == "rot":
                i = s[1]
                job_full(v, s)
                v.wait_ge(cs_in, 16)
                link(TT(ropet[:, 2, :], ropet[:, i % 2, :], cs[:, 0, :], ALU.mult))
                TT(ropet[:, 3, :], bk(b), cs[:, 1, :], ALU.mult).then_inc(*t(empty[b], plan[s][1]))
                job_read(v, s)
                TT(kT[:, :] if i == 0 else qT[:, i - 1, :], ropet[:, 2, :], ropet[:, 3, :], ALU.add).then_inc(*t(rope_ready))
            elif k0 == "sx":
                m = s[1]
                job_read(v, ("cg", m))
                job_full(v, s)
                TT(pads[:, m % 2, 1:1 + S], bk(b), th[:, 0, 0:S], ALU.mult).then_inc(*t(empty[b], plan[s][1]))
                job_read(v, s)
                if m < 2:
                    link(V_.memset(pads[:, m % 2, 1 + S:2 + S], 0.0))
                w = [QC[:, Q_SW + q * 4 + m:Q_SW + q * 4 + m + 1] for q in range(3)]
                x, a = pads[:, m % 2, :], acc[:, m % 2, 0:S]
                link(V_.tensor_scalar(a, x[:, 0:S], w[0], None, ALU.mult))
                link(conv(x, w, a, S))
            elif k0 == "bg":
                m = s[1]
                job_full(v, s)
                TT(scT[:, m, :], bk(b), acc[:, m % 2, 0:S], ALU.mult).then_inc(*t(empty[b], plan[s][1]))
            elif k0 == "z":
                c = s[1]
                v.wait_ge(z_tanh, c + 1)
                V_.scalar_tensor_tensor(zs[:, c, :], th[:, 0, 0:S], 1.0, bk(b), ALU.add, ALU.mult).then_inc(*t(empty[b], plan[s][1]))
            elif k0 == "F":
                job_full(v, s)
                V_.tensor_copy(uT[:, s[1], :], bk(b)).then_inc(*t(empty[b], plan[s][1]))
            elif k0 == "S":
                h = s[1]
                keys, mo = head(h)[3:]
                W = len(keys) * P
                job_full(v, s)
                if h >= 3:
                    job_full(v, ("T", h - 3))
                V_.scalar_tensor_tensor(sc[:, h % 3, 0:W], bk(b, 2)[:, 0:W], HD ** -0.5,
                                        CT[:, C_MASK + mo:C_MASK + mo + W], ALU.mult, ALU.add).then_inc(*t(empty[b], plan[s][1]))
                job_read(v, s)
                link(V_.tensor_reduce(amx[:, h, 0:1], sc[:, h % 3, 0:W], AX.X, ALU.max))
                V_.tensor_scalar(amx[:, h, 1:2], amx[:, h, 0:1], RW[:, R_SINK + hd_index(h):R_SINK + hd_index(h) + 1],
                                 -1.0, ALU.max, ALU.mult).then_inc(*t(smax_ready))
                if h >= 1:
                    norm_probs(h - 1)
            elif k0 == "T":
                if s[1] == 30:
                    norm_probs(31)
            elif k0 == "O":
                h = s[1]
                blk, g, j = head(h)[:3]
                r = slice(g * 64, g * 64 + 64)
                job_full(v, s)
                V_.tensor_copy(attT[r, j, blk * P:blk * P + P], bk(b)[r, 0:P]).then_inc(*t(empty[b], plan[s][1]))
            elif k0 == "st":
                d, k = s[1:]
                c = st_chunk[d][k]
                if s == ("st", 0, 0):
                    job_full(v, ("xtr", 3))
                    v.wait_ge(cds_ready, 4)
                dst = tmpS[:, d, :] if k == 0 else prevS[:, d, st_chunk[d][k + 1], :]
                job_full(v, s)
                if k == 0:
                    V_.tensor_copy(dst, bk(b)[:, 0:256]).then_inc(*t(empty[b], plan[s][1]))
                else:
                    old = tmpS[:, d, :] if k == 1 else prevS[:, d, c, :]
                    job_read(v, ("st", d, k - 1))
                    link(TT(ytmp[:, 0, :].rearrange("p (h n) -> p h n", h=4), old.rearrange("p (h n) -> p h n", h=4),
                            hb(cds[:, c, d, :], HD), ALU.mult))
                    TT(dst, ytmp[:, 0, :], bk(b)[:, 0:256], ALU.add).then_inc(*t(empty[b], plan[s][1]))
            elif k0 == "G":
                job_full(v, s)
                if s[1:] == (0, 0):
                    link(TT(Gm[:, 0, :], bk(b)[:, 0:P], CT[:, C_LE:C_LE + P], ALU.mult))
                else:
                    TT(Gm[:, 0, :], bk(b)[:, 0:P], CT[:, C_LE:C_LE + P], ALU.mult).then_inc(*t(gm_ready))
                TT(Gm[:, 1, :], bk(b)[:, 0:P], CT[:, C_GE:C_GE + P], ALU.mult).then_inc(*t(empty[b], plan[s][1]))
            elif k0 == "seg":
                c, g, d = s[1:]
                job_read(v, ("G", c, g))
                job_read(v, s)
                e3 = E[:, d, :].rearrange("p (h n) -> p h n", h=4)
                TT(e3, e3, Gm[:, d, :].unsqueeze(1).to_broadcast([P, 4, P]), ALU.mult).then_inc(*t(m_ready))
            elif k0 == "yoff":
                c, g = s[1:]
                job_full(v, s)
                y4 = ytmp[:, 0:2, :].rearrange("p d (h n) -> p d h n", h=4)
                e4 = dec[:, c, 0:16].rearrange("p (d h) -> p d h", d=2)[:, :, g * 4:g * 4 + 4]
                TT(y4, bk(b).rearrange("p (d h n) -> p d h n", d=2, h=4),
                   e4.unsqueeze(3).to_broadcast([P, 2, 4, HD]), ALU.mult).then_inc(*t(empty[b], plan[s][1]))
            elif k0 == "y":
                c, g = s[1:]
                job_read(v, ("yoff", c, g))
                x3 = xs[:, c, g * 256:g * 256 + 256].rearrange("p (h n) -> p h n", h=4)
                link(TT(ytmp[:, 2, :].rearrange("p (h n) -> p h n", h=4), x3,
                        hb(RW[:, R_D + g * 4:R_D + g * 4 + 4], HD), ALU.mult))
                link(TT(ytmp[:, 0, :], ytmp[:, 0, :], ytmp[:, 1, :], ALU.add))
                link(TT(ytmp[:, 0, :], ytmp[:, 0, :], ytmp[:, 2, :], ALU.add))
                job_full(v, s)
                TT(ytmp[:, 0, :], ytmp[:, 0, :], bk(b)[:, 0:256], ALU.add).then_inc(*t(empty[b], plan[s][1]))
                job_read(v, s)
                zz = zs[:, c, g * 256:g * 256 + 256]
                TT(zz, zz, ytmp[:, 0, :], ALU.mult).then_inc(*t(y_done))
            elif k0 == "ynorm":
                v.wait_ge(ystd, 1)
                link(V_.reciprocal(yst[:, 8:12], yst[:, 4:8]))
                for c in range(NCH):
                    V_.tensor_scalar(zs[:, c, :], zs[:, c, :], yst[:, 8 + c:9 + c], None, ALU.mult).then_inc(*t(ynorm_done))
            elif k0 == "ytr":
                c = s[1]
                job_full(v, s)
                TT(ssmT[:, :, c * P:c * P + P], bk(b).rearrange("p (m n) -> p m n", m=4),
                   hb(QC[:, Q_SN:Q_SN + 4], P), ALU.mult).then_inc(*t(empty[b], plan[s][1]))
            elif k0 == "proj":
                n, d = s[1:]
                job_full(v, s)
                job_read(v, ("gate", n, d))
                first = n == MIX_ORDER[0]
                V_.scalar_tensor_tensor(merged[:, d, :] if first else mtmp[:, :], gth[:, :], 1.0, bk(b), ALU.add,
                                        ALU.mult).then_inc(*t(empty[b], plan[s][1]))
                if first:
                    V_.memset(yst[:, 0:1], 0.0).then_inc(*t(merge_done))
                else:
                    job_read(v, s)
                    TT(merged[:, d, :], merged[:, d, :], mtmp[:, :], ALU.add).then_inc(*t(merge_done))
            elif k0 == "wo":
                d = s[1]
                if d == 0:
                    link(V_.tensor_scalar(A1[:, :, 0], mods[:, 16:24, 0], 0.5, None, ALU.mult))
                    v.wait_ge(x_again, 16)
                job_full(v, s)
                V_.scalar_tensor_tensor(H[:, d, :], bk(b), A1[:, d, 0:1], H[:, d, :], ALU.mult,
                                        ALU.add).then_inc(*t(empty[b], plan[s][1]))
            elif k0 == "ssq2":
                link(V_.scalar_tensor_tensor(A1[:, :, 1], mods[:, 32:40, 0], 1.0, QC[:, Q_G2:Q_G2 + 8], ALU.add, ALU.mult))
                job_read(v, s)
                link(V_.reciprocal(rs2[:, :], rs2[:, :]))
                for k in range(KD):
                    V_.scalar_tensor_tensor(h2[:, k, :], H[:, k, :], A1[:, k, 1:2], rs2[:, :], ALU.mult,
                                            ALU.mult).then_inc(*t(h2_pre))
            elif k0 == "rt":
                job_full(v, s)
                V_.tensor_scalar(lg[:, :, :].rearrange("p c n -> p (c n)"), bk(b)[:, 0:NCH * NE], -87.0, None,
                                 ALU.max).then_inc(*t(lg_ready))
                v.wait_ge(rexp, 1)
                link(V_.tensor_scalar(w32[:, :, :], w32[:, :, :], 1.0, None, ALU.add))
                link(V_.reciprocal(lg[:, :, :], w32[:, :, :]))
                link(TT(sel[:, :, :], lg[:, :, :], RW[:, R_RB:R_RB + NE].unsqueeze(1).to_broadcast([P, NCH, NE]), ALU.add))
                p2 = sel[:, :, :].rearrange("p c (h t) -> p c h t", t=2)
                link(TT(g16[:, 0], p2[:, :, :, 0], p2[:, :, :, 1], ALU.max))
                link(TT(g16[:, 1], p2[:, :, :, 0], p2[:, :, :, 1], ALU.min))
                hi = g16[:, 0].rearrange("p c (g t) -> p c g t", t=2)
                lo = g16[:, 1].rearrange("p c (g t) -> p c g t", t=2)
                link(TT(g8[:, 0], hi[:, :, :, 0], hi[:, :, :, 1], ALU.max))
                link(TT(g8[:, 1], hi[:, :, :, 0], hi[:, :, :, 1], ALU.min))
                link(TT(g8[:, 2], lo[:, :, :, 0], lo[:, :, :, 1], ALU.max))
                link(TT(g8[:, 1], g8[:, 1], g8[:, 2], ALU.max))
                link(TT(g8[:, 0], g8[:, 0], g8[:, 1], ALU.add))

                def first_max(out, x, iota, tmp, sm):
                    n = x.shape[2]
                    link(V_.tensor_reduce(sm, x, AX.X, ALU.max))
                    link(TT(tmp, x, sm.unsqueeze(2).to_broadcast([P, NCH, n]), ALU.is_equal))
                    link(V_.scalar_tensor_tensor(tmp, tmp, -1000.0, iota.unsqueeze(1).to_broadcast([P, NCH, n]),
                                                 ALU.mult, ALU.add))
                    link(V_.tensor_reduce(sm, tmp, AX.X, ALU.min))
                    link(TT(out, tmp, sm.unsqueeze(2).to_broadcast([P, NCH, n]), ALU.is_equal))

                first_max(g8[:, 3], g8[:, 0], RW[:, R_IG:R_IG + 8], g8[:, 1], sml[:, 0])
                link(V_.tensor_scalar(g8[:, 4], g8[:, 3], 1.0e30, -1.0e30, ALU.mult, ALU.add))
                s4 = sel[:, :, :].rearrange("p c (g t) -> p (c g) t", t=4)
                m4 = selm[:, :, :].rearrange("p c (g t) -> p (c g) t", t=4)

                def flat(x):
                    return x.rearrange("p c g -> p (c g)").unsqueeze(2).to_broadcast([P, NCH * 8, 4])

                link(TT(m4, s4, flat(g8[:, 3]), ALU.mult))
                link(TT(m4, m4, flat(g8[:, 4]), ALU.add))
                first_max(oh[:, 0], selm[:, :, :], RW[:, R_IE:R_IE + NE], w32[:, :, :], sml[:, 1])
                link(V_.scalar_tensor_tensor(selm[:, :, :], oh[:, 0], -1.0e31, selm[:, :, :], ALU.mult, ALU.add))
                first_max(oh[:, 1], selm[:, :, :], RW[:, R_IE:R_IE + NE], w32[:, :, :], sml[:, 1])
                TT(asg[:, :, :], oh[:, 0], oh[:, 1], ALU.add).then_inc(*t(asg_ready))
                for k in range(2):
                    link(TT(w32[:, :, :], oh[:, k], lg[:, :, :], ALU.mult))
                    link(V_.tensor_reduce(wts[:, k, :], w32[:, :, :], AX.X, ALU.add))
                link(TT(sml[:, 2], wts[:, 0, :], wts[:, 1, :], ALU.add))
                link(V_.reciprocal(sml[:, 2], sml[:, 2]))
                for k in range(2):
                    link(TT(wts[:, k, :], wts[:, k, :], sml[:, 2], ALU.mult))
            elif k0 == "cnt":
                job_full(v, s)
                C = cnt
                link(V_.tensor_copy(C[:, 0, :], bk(b)[:, 0:NE]))
                link(V_.tensor_scalar(C[:, 1, :], C[:, 0, :], 0.0, None, ALU.is_gt))
                for q in range(1, S // BLK):
                    link(V_.scalar_tensor_tensor(C[:, 1, :], C[:, 0, :], float(q * BLK), C[:, 1, :], ALU.is_gt, ALU.add))
                link(V_.memset(C[:, 3, :], 0.0))
                link(V_.tensor_tensor_scan(C[:, 2, :], C[:, 1, :], C[:, 3, :], 0.0, ALU.add, ALU.add))
                link(TT(C[:, 3, :], C[:, 2, :], C[:, 1, :], ALU.subtract))
                link(V_.tensor_scalar(bex[:, :], C[:, 2, :], QC[:, Q_IOTA:Q_IOTA + 1], None, ALU.is_le))
                link(V_.tensor_reduce(bec[:, 1:2], bex[:, :], AX.X, ALU.add))
                V_.tensor_scalar(bec[:, 0:1], bec[:, 1:2], float(NE - 1), None, ALU.min).then_inc(*t(bex_ready))
                rk = bk(b)[:, NE:NE + NCH * NE].rearrange("p (c n) -> p c n", n=NE)
                st64 = C[:, 3, :].unsqueeze(1).to_broadcast([P, NCH, NE])
                V_.scalar_tensor_tensor(w32b[:, :, :], st64, float(BLK), rk, ALU.mult, ALU.add).then_inc(*t(empty[b], plan[s][1]))
                job_read(v, s)
                for k in range(2):
                    link(TT(w32[:, :, :], oh[:, k], w32b[:, :, :], ALU.mult))
                    link(V_.tensor_reduce(slotf[:, k, :], w32[:, :, :], AX.X, ALU.add))
                V_.tensor_copy(sloti[:, :, :], slotf[:, :, :]).then_inc(*t(slot_ready))
                link(V_.tensor_copy(pos[:, :, :], slotf[:, :, :]))
            elif k0 == "bexp":
                job_full(v, s)
                V_.tensor_copy(brow[0:1, :], bk(b)[0:1, 0:P]).then_inc(*t(route_done))
                V_.tensor_copy(nbk[0:1, 0:1], cnt[0:1, 2, NE - 1:NE]).then_inc(*t(route_done))

        v.sem_inc(act_ready, 1)
        v.sem_inc(yd_done, 1)
        XB, HB, YB = bk(3), bk(4), bk(6)
        iota64 = RW[:, R_IB:R_IB + BLK].unsqueeze(1).to_broadcast([P, 2 * NCH, BLK])

        def pos8():
            return pos[:, :, :].rearrange("p k c -> p (k c)").unsqueeze(2).to_broadcast([P, 2 * NCH, BLK])

        def eight(par):
            return oneh[:, par].rearrange("p k c n -> p (k c) n")

        link(TT(eight(0), iota64, pos8(), ALU.is_equal))
        TT(oneh[:, 0, 0], oneh[:, 0, 0], oneh[:, 0, 1], ALU.add).then_inc(oneh_ready, 1)
        v.wait_ge(xb_full, 1)
        V_.tensor_copy(xb[:, 0, :], XB).then_inc(xb_ready, 1)
        v.wait_ge(route_done, 2)
        n = v.value_load(nbk[0:1, 0:1], min_val=1, max_val=MAXB)
        with v.Fori(0, PAIRS) as i:
            for j in range(2):
                b = i * 2 + j
                with v.If(b < n):
                    V_.tensor_scalar(pos[:, :, :], pos[:, :, :], -float(BLK), None, ALU.add).then_inc(pos_done, 1)
                    v.wait_ge(pos_done, b + 1)
                    TT(eight(1 - j), iota64, pos8(), ALU.is_equal).then_inc(eq_done, 1)
                    v.wait_ge(eq_done, b + 1)
                    TT(oneh[:, 1 - j, 0], oneh[:, 1 - j, 0], oneh[:, 1 - j, 1], ALU.add).then_inc(oneh_ready, 1)
                    v.wait_ge(sig_ready, b + 1)
                    TT(a1[:, :], sg[:, :], HB[:, 0:4 * BLK], ALU.mult).then_inc(a1_done, 1)
                    v.wait_ge(a1_done, b + 1)
                    TT(act_[:, j, :], a1[:, :], HB[:, 4 * BLK:8 * BLK], ALU.mult).then_inc(act_ready, 1)
                    v.wait_ge(xb_full, b + 2)
                    V_.tensor_copy(xb[:, 1 - j, :], XB).then_inc(xb_ready, 1)
                    v.wait_ge(down_mm, b + 3)
                    v.wait_ge(y_out[j], i * 16 + 16)
                    V_.tensor_copy(ysb[:, j, S:2 * S], YB[0:BLK, :]).then_inc(yd_done, 1)
        for c in range(NCH):
            v.wait_ge(gat_in[0][c], 16)
            v.wait_ge(gat_in[1][c], 16)
            link(V_.tensor_scalar(fin[:, c, :], gat[:, 0, c, :], wts[:, 0, c:c + 1], None, ALU.mult))
            V_.scalar_tensor_tensor(fin[:, c, :], gat[:, 1, c, :], wts[:, 1, c:c + 1], fin[:, c, :], ALU.mult,
                                    ALU.add).then_inc(fin_ready, 1)
        for k in range(KD):
            v.wait_ge(fT_full, k + 1)
            V_.scalar_tensor_tensor(x2[:, k, :], bk(k % 2), mods[:, 40 + k, 0:1], H[:, k, :], ALU.mult,
                                    ALU.add).then_inc(x2_ready, 1)
        v.wait_ge(std3, 1)
        link(V_.reciprocal(rs2[:, :], rs2[:, :]))
        for k in range(KD):
            if k == 0:
                v.wait_ge(sq3_ready, KD)
            V_.scalar_tensor_tensor(x2[:, k, :], x2[:, k, :], QC[:, Q_GF + k:Q_GF + k + 1], rs2[:, :], ALU.mult,
                                    ALU.mult).then_inc(out_ready, 1)

    @block.gpsimd
    def _(g_):
        t = Tally(g_)
        G_ = nc.gpsimd

        def hb(ap, n):
            return ap.unsqueeze(2).to_broadcast([P, ap.shape[1], n])

        seg_i = 0
        for s in steps:
            k0 = s[0]
            t.settle()
            if k0 == "st":
                d, k = s[1:]
                c = st_chunk[d][k]
                if s == ("st", 0, 0):
                    g_.wait_ge(wdd_ready, 1)
                    job_read(g_, ("z", 3))
                else:
                    job_full(g_, st_prev[s])
                job_read(g_, ("xtr", c))
                G_.tensor_tensor(xdd[:, :].rearrange("p (h n) -> p h n", h=8),
                                 xs[:, c, :].rearrange("p (h n) -> p h n", h=8),
                                 hb(wdd[:, c, d * 8:d * 8 + 8], HD), ALU.mult).then_inc(*t(xdd_ready))
            elif k0 == "seg":
                c, g, d = s[1:]
                if (c, g) == (0, 0):
                    job_full(g_, ("F", 3))
                    g_.wait_ge(rope_ready, 5)
                else:
                    job_full(g_, ("seg", (2 * c + g - 1) // 2, (2 * c + g - 1) % 2, d))
                m = C_LE if d == 0 else C_GE
                G_.tensor_tensor(Am[:, d, :].rearrange("p (h n) -> p h n", h=4),
                                 CT[:, m:m + P].unsqueeze(1).to_broadcast([P, 4, P]),
                                 hb(dta[:, c, d * 8 + g * 4:d * 8 + g * 4 + 4], P), ALU.mult).then_inc(*t(am_ready))
                if g == 0:
                    if c:
                        job_full(g_, ("y", c - 1, 1))
                    G_.tensor_tensor(xd[:, d, :].rearrange("p (h n) -> p h n", h=8),
                                     xs[:, c, :].rearrange("p (h n) -> p h n", h=8),
                                     hb(dtv[:, c, d * 8:d * 8 + 8], HD), ALU.mult).then_inc(*t(xd_ready))
        g_.wait_ge(slot_ready, 1)
        for j in range(2):
            g_.wait_ge(y_out[j], 16 * (PAIRS + 1))
        for c in range(NCH):
            for k in range(2):
                G_.indirect_dma_start(out=gat[:, k, c, :], out_offset=None,
                                      in_=ybuf.rearrange("b p n -> (b p) n"),
                                      in_offset=bass.IndirectOffsetOnAxis(ap=sloti[:, k, c:c + 1], axis=0)
                                      ).then_inc(gat_in[k][c], 16)

    ctx.close()


def constants():
    p, f = np.arange(P)[:, None], np.arange(P)[None, :]
    perm = np.zeros((P, P))
    for m in range(P):
        if m % HD < HD // 2:
            perm[m + HD // 2, m] = -1.0
        else:
            perm[m - HD // 2, m] = 1.0
    same = p // HD == f // HD
    w = 2 * np.pi * ((p % HD) * (f % HD) % HD) / HD
    prev = np.where(f >= p, 0.0, NEG)
    nxt = np.where(f <= p, 0.0, NEG)
    z = np.zeros((P, P))
    pack = [np.eye(P), p <= f, p >= f, p < f, p > f, np.ones((P, P)), perm, same * np.cos(w), same * np.sin(w),
            z, z, prev, z, nxt, z, z]
    consts = np.concatenate([np.asarray(x, np.float32) for x in pack], axis=1)
    t = np.arange(S)
    ang = 2 * np.pi * (t[:, None] * t[None, :] % S) / S
    nrm = 1.0 / np.sqrt(S * HD)
    dft = np.stack([np.cos(ang) * nrm, -np.sin(ang) * nrm]).astype(np.float32)
    dft = np.ascontiguousarray(dft.reshape(2, NCH, P, S).transpose(2, 0, 1, 3))
    pairs = HD // 4
    inv = np.float32(10000.0) ** (-np.arange(pairs, dtype=np.float32) / np.float32(pairs))
    row, col = (t // 64).astype(np.float32), (t % 64).astype(np.float32)
    a = np.concatenate([row[:, None] * inv, col[:, None] * inv], axis=1).astype(np.float32).T
    a = a[np.arange(P) % 32]
    cossin = np.ascontiguousarray(np.stack([np.cos(a), np.sin(a)], axis=1).astype(np.float32))
    return consts, cossin, dft


def kernel(**inputs):
    import numpy as _np
    import concourse.bacc as _bacc
    from concourse import mybir as _mybir
    from concourse.bass_utils import run_bass_kernel_spmd as _run

    a = {k: _np.asarray(v) for k, v in inputs.items()}

    def chan(x, n):
        return x.reshape(n, P, -1).transpose(1, 0, 2)

    xT = chan(a["x"][0].T, KD)
    ctxT = chan(a["ctx"][0].T, KD)
    w_in = a["w_in"][0]
    cut = _np.cumsum([0, 512, 128, 128, 512, 768, 16, 512, 1536])
    q, k, v, z, xbc, dt, fu, su = [w_in[:, cut[i]:cut[i + 1]] for i in range(8)]
    q = q.reshape(D, 2, 4, HD).transpose(0, 2, 1, 3).reshape(D, 512)
    su = su.reshape(D, 3, 4, P)[:, [1, 2, 0]].transpose(0, 2, 1, 3).reshape(D, 1536)
    w_in8 = _np.concatenate([xbc[:, :512], xbc[:, 512:], k, v, fu, q, su, z], axis=1)

    def units(w):
        n = w.shape[1] // S
        return w.reshape(KD, P, n, S).transpose(2, 1, 0, 3).reshape(n, P, UNIT)

    ada = units(a["w_ada"][0])
    wg, wb = units(a["w_gate"][0]), a["w_branch"][0]
    parts = [ada[:4], units(w_in8)]
    for i, n in enumerate(MIX_ORDER):
        if i == 2:
            parts.append(ada[4:])
        b = wb[n]
        if n == 0:
            b = b.reshape(2, 4, HD, D).transpose(1, 0, 2, 3).reshape(512, D)
        parts += [wg[2 * n:2 * n + 1], chan(b, 4).reshape(1, P, UNIT), wg[2 * n + 1:2 * n + 2]]
    parts.append(units(a["w_o"][0]))
    stream = _np.concatenate(parts)

    def col(x):
        return x.reshape(-1, P).T

    consts, cossin, dft = constants()
    cv = _np.stack([a["c"][0], a["c_ctx"]], axis=1)
    cols = _np.concatenate([
        col(a["norm1_w"][0]), col(a["norm2_w"][0]), col(a["final_norm_w"]), col(a["b_ada"][0]), col(a["b_gate"][0]),
        col(a["ssm_conv_w"][0]), col(a["ssm_conv_b"][0]), col(a["sconv_w"][0]), col(a["ssm_norm_w"][0]),
        chan(cv, KD).reshape(P, 16), _np.full((P, 1), EPS, _np.float32), _np.full((P, 1), 4 * EPS, _np.float32),
        _np.zeros((P, 1), _np.float32), _np.arange(P, dtype=_np.float32)[:, None]], axis=1)
    rows = _np.concatenate([
        a["ssm_dt_bias"][0].reshape(-1), a["ssm_a_log"][0].reshape(-1), a["ssm_d"][0], a["attn_sink"][0],
        a["router_bias"], _np.arange(32, dtype=_np.float32), _np.arange(8, dtype=_np.float32),
        _np.arange(64, dtype=_np.float32)])
    rows = _np.broadcast_to(rows[None, :], (P, R_N))
    w2 = a["moe_w2"][0].reshape(NE, 4, P, D).transpose(0, 2, 1, 3).reshape(NE, P, UNIT)
    w1, w3 = [a[x][0].reshape(NE, KD, P, S).transpose(0, 2, 1, 3).reshape(NE, P, UNIT) for x in ("moe_w1", "moe_w3")]
    ins = {"xT": xT, "ctxT": ctxT, "stream": stream, "consts": consts, "cossin": cossin, "dft": dft, "cols": cols,
           "rows": rows, "wdt": chan(dt, KD), "wrt": chan(a["w_router"], KD), "w1": w1, "w3": w3, "w2": w2}
    ins = {"in_" + k: _np.ascontiguousarray(v) for k, v in ins.items()}

    nc = _bacc.Bacc("TRN2", target_bir_lowering=False, num_devices=1)
    aps = {k[3:]: nc.dram_tensor(k, list(v.shape), _mybir.dt.from_np(v.dtype), kind="ExternalInput").ap()
           for k, v in ins.items()}
    aps["ybuf"] = nc.dram_tensor("expert_rows", [2 * PAIRS, BLK, D], _mybir.dt.float32, kind="Internal").ap()
    aps["outT"] = nc.dram_tensor("outT", [P, KD, S], _mybir.dt.float32, kind="ExternalOutput").ap()
    build(nc, **aps)
    r = _run(nc, [ins], core_ids=[0])
    o = _np.asarray(r.results[0]["outT"])
    return _np.ascontiguousarray(o.transpose(1, 0, 2).reshape(D, S).T)[None]
```

```python
from contextlib import ExitStack

import numpy as np
import concourse.bass as bass
from concourse import mybir

F32 = mybir.dt.float32
I32 = mybir.dt.int32
U32 = mybir.dt.uint32
ALU = mybir.AluOpType
ACT = mybir.ActivationFunctionType
AX = mybir.AxisListType

P = 128
D, KD = 1024, 8
S, NCH = 512, 4
SC, NCC = 256, 2
EPS = 1e-6
NEG = -1.0e30
HD = 64
NE, NG, EPG = 32, 8, 4
BLK = 128
MAXB = 2 * S // BLK + NE - 1
UNIT = 4096
RING = 3
PAIRS = (MAXB + 1) // 2
NTAB = 2 * PAIRS + 2

C_ID, C_LE, C_GE, C_LT, C_GT, C_ONE, C_PERM, C_BD, C_MASK = 0, 128, 256, 384, 512, 640, 768, 896, 1152
C_N = C_MASK + 7 * 128
Q_G1, Q_G2, Q_GF, Q_BADA, Q_BG, Q_CW, Q_CB, Q_SW, Q_SN, Q_C, Q_EPS, Q_EPS4, Q_ZERO, Q_IOTA, Q_DUMP, Q_DST = (
    0, 8, 16, 24, 72, 104, 122, 128, 140, 144, 160, 161, 162, 163, 164, 165)
Q_N = 173
R_DTB, R_ALOG, R_D, R_SINK, R_RB, R_IE, R_IG, R_IB = 0, 16, 32, 40, 48, 80, 112, 120
R_N = 248

MIX_ORDER = (3, 2, 0, 1)
N_ADA1, N_IN = 4, 8


def timeline():
    t = [("mod01",), ("ssq",), ("ssqc",), ("mod", 0)]
    for m in range(4):
        t += [("xbc", m), ("xbcc", m)]
        if m == 1:
            t += [("macc", 1)]
    t += [("mod", 1)]
    for m in (4, 5):
        t += [("xbc", m), ("xbcc", m)]
    t += [("macc", 2), ("k",), ("kc",), ("dt",), ("v",), ("rot", 0), ("vc",), ("mod", 2)]
    for m in range(4):
        t += [("fu", m)]
        if m == 1:
            t += [("macc", 3)]
    t += [("dec",), ("mod", 3)]
    for m in range(4):
        t += [("q", m)]
        if m:
            t += [("rot", m)]
        if m == 1:
            t += [("macc", 4)]
    t += [("mod", 4)]
    for m in range(4):
        t += [("cg", m)] + ([("rot", 4)] if m == 0 else []) 
        t += [("macc", 5 + m)] if m < 3 else []
        t += [("sx", m), ("bg", m)]
        t += [("mod", 5 + m)] if m < 3 else []
    for c in range(NCH):
        t += [("z", c)]
        if c == 1:
            t += [("macc", 8)]
    t += [("mod", 8)]
    t += [("xtr", c) for c in (4, 5, 0, 1, 2, 3)] + [("btr", 0), ("btr", 1)]
    t += [("V", 0), ("V", 1), ("F", 0), ("V", 2), ("F", 1), ("V", 3), ("F", 2), ("F", 3)]

    ssm = [("st", d, k) for k in range(5) for d in range(2)]
    for c in range(NCH):
        for g in range(2):
            ssm += [("G", c, g), ("seg", c, g, 0), ("seg", c, g, 1), ("yoff", c, g), ("y", c, g)]
    ssm += [("ynorm",)] + [("ytr", c) for c in range(NCH)]
    n_att = 32 + 3
    point = att_step = 0

    def side():
        nonlocal point, att_step
        out = []
        if (point % 2 == 0 or point % 8 == 7) and att_step < n_att:
            h = att_step
            att_step += 1
            if h < 32:
                out.append(("S", h))
            if 0 <= h - 2 < 32:
                out.append(("T", h - 2))
            if 0 <= h - 3 < 32:
                out.append(("O", h - 3))
        elif ssm:
            out.append(ssm.pop(0))
        point += 1
        return out

    for i, n in enumerate(MIX_ORDER):
        if i == 3:
            t += ssm
            ssm = []
        for d in range(8):
            t += [("gate", n, d)] + side() + side() + [("proj", n, d)] + side() + side()
    t += [("wo", d) for d in range(8)]
    t += [("ssq2",), ("rt",), ("rtt",)] + [("h2tr", c) for c in range(NCH)] + [("cnt",), ("tab",), ("bexp",)]
    return t


ROT3 = {"xbc", "xbcc", "k", "kc", "dt", "v", "vc", "fu", "q", "rot", "cg", "sx", "bg", "z", "wo"}


def bank_plan(steps):
    used, plan, rot, alt = {}, {}, 0, 0
    for s in steps:
        k = s[0]
        if k in ROT3:
            b = rot % 3
            rot += 1
        elif k == "gate":
            b = s[2] % 2
        elif k == "proj":
            b = 2
        elif k == "S":
            b = 3
        elif k == "h2tr":
            b = 3 + s[1] % 2 * 2
        elif k in ("V", "T"):
            b = 5
        elif k in ("xtr", "btr", "F"):
            b = 3
        elif k == "ssq2" or s == ("mod", 0):
            b = 0
        elif k in ("ssqc", "rtt"):
            b = 1
        elif k == "ssq":
            b = 3
        elif k in ("ynorm", "mod01", "macc"):
            continue
        elif k == "rt":
            b = 7
        elif k == "cnt":
            b = 2
        elif k == "tab":
            b = 2
        else:
            b = 7
        used[b] = used.get(b, 0) + 1
        plan[s] = (b, used[b])
    return plan


def head(h):
    blk, g, j = h // 8, (h // 4) % 2, h % 4
    if blk == 0:
        return blk, g, j, [0, 1, 4, 5], 3 * P
    keys = [4, 5] + [c for c in (blk - 1, blk, blk + 1) if c < NCH]
    return blk, g, j, keys, 0


def hd_index(h):
    return h // 4 % 2 * 4 + h % 4


def chunk_cols(c):
    return c * P if c < NCH else S + 2 + (c - NCH) * P


class Tally:

    def __init__(self, eng):
        self.eng, self.count, self.last = eng, {}, None

    def __call__(self, sem, value=None):
        n = self.count.get(sem.name, 0) + 1 if value is None else value
        self.count[sem.name] = n
        self.last = (sem, n)
        return sem, 1

    def settle(self):
        if self.last:
            self.eng.wait_ge(*self.last)
            self.last = None


def build(nc, xT, ctxT, stream, consts, cossin, dft, cols, rows, wdt, wrt, w1, w3, w2, h2d, ybuf, outT):
    ctx = ExitStack()
    BASE = 16512

    def at(name, off, shape, dt=F32):
        return nc.alloc_sbuf_tensor_at(name, shape, dt, offset=BASE + off)

    ring = at("ring", 0, [P, RING, UNIT])
    dftm = at("dftm", 49152, [P, 2, NCH, S])
    merged = at("merged", 49152, [P, KD, S])
    sq = at("sq", 49152, [P, 12, S])
    ropet = at("ropet", 65536, [P, 4, S])
    V = at("V", 65536, [P, 2, NCH * 256])
    E = at("E", 65536, [P, 2, S])
    Am = at("Am", 65536 + 4096, [P, 2, S])
    pads = at("pads", 73728, [P, 2, 772])
    acc = at("acc", 73728 + 6176, [P, 2, 772])
    th = at("th", 73728 + 12352, [P, 2, 772])
    sc = at("sc", 73728, [P, 3, 640])
    PT = at("PT", 73728 + 7680, [P, 640])
    gth = at("gth", 73728 + 10240, [P, S])
    xdd = at("xdd", 73728 + 12288, [P, S])
    ytmp = at("ytmp", 73728 + 14336, [P, 3, 256])
    amx = at("amx", 73728 + 17408, [P, 32, 8])
    xbcT = at("xbcT", 92288, [P, 6, 770])
    prevS = at("prevS", 92288, [P, 2, NCH, 256])
    tmpS = at("tmpS", 92288 + 8192, [P, 2, 256])
    Gm = at("Gm", 92288 + 10240, [P, 2, P])
    uT = at("uT", 110784, [P, NCH, S])
    hc = at("hc", 118976, [P, KD, SC])
    attT = at("attT", 118976, [P, 4, S])
    qT = at("qT", 127168, [P, 4, S])
    dts = at("dts", 127168, [P, 8, 96])
    ssmT = at("ssmT", 127168, [P, 4, S])
    kT = at("kT", 135360, [P, S])
    kcT = at("kcT", 137408, [P, SC])
    vt = at("vt", 138432, [P, 6, P])
    scT = at("scT", 141504, [P, 4, S])
    zs = at("zs", 149696, [P, NCH, S])
    ada3 = at("ada3", 141504, [P, UNIT])
    xs = at("xs", 157888, [P, 6, S])
    btm = at("btm", 157888 + 12288, [P, 6, P])
    cs = at("cs", 173248, [P, 2, S])
    xd = at("xd", 173248, [P, 2, S])
    H = at("H", 177344, [P, KD, S])
    CT = at("CT", 193728, [P, C_N])
    o = 193728 + C_N * 4

    def up(n):
        return (n + 31) // 32 * 32

    QC = at("QC", o, [P, Q_N]); o += up(Q_N * 4)
    RW = at("RW", o, [P, R_N]); o += up(R_N * 4)
    WDT = at("WDT", o, [P, KD, 16]); o += up(512)
    rsx = at("rsx", o, [P, S]); macc = at("macc", o, [P, S]); mtmp = at("mtmp", o, [P, S]); o += up(2048)
    rsc = at("rsc", o, [P, SC]); o += up(1024)
    mods = at("mods", o, [P, 48, 2]); o += up(384)
    A1 = at("A1", o, [P, KD, 2]); o += up(64)
    half = at("half", o, [P, 56]); o += up(224)
    sil = at("sil", o, [P, 16]); o += up(64)
    dtv = at("dtv", o, [P, 6, 16]); o += up(384)
    dta = at("dta", o, [P, 6, 16]); o += up(384)
    ea = at("ea", o, [P, 16]); o += up(64)
    dec = at("dec", o, [P, 6, 48]); o += up(1152)
    wdd = at("wdd", o, [P, 6, 16]); o += up(384)
    cds = at("cds", o, [P, 6, 2, 4]); o += up(192)
    sqw = at("sqw", o, [P, 1]); o += 32
    yst = at("yst", o, [P, 12]); o += up(64)
    assert o <= 229368 - BASE, o

    ering = at("ering", 0, [P, 2, 3, UNIT])
    h2 = at("h2", 98304, [P, KD, S])
    h2t = at("h2t", 114688, [P, NCH, D])
    m0 = 131072
    WR = at("WR", m0, [P, KD, NE]); m0 += 1024
    lg = at("lg", m0, [P, NCH, NE]); m0 += 512
    sel = at("sel", m0, [P, NCH, NE]); m0 += 512
    selm = at("selm", m0, [P, NCH, NE]); m0 += 512
    oh = at("oh", m0, [P, 2, NCH, NE]); m0 += 1024
    asg = at("asg", m0, [P, NCH, NE]); m0 += 512
    w32 = at("w32", m0, [P, NCH, NE]); m0 += 512
    w32b = at("w32b", m0, [P, NCH, NE]); m0 += 512
    g16 = at("g16", m0, [P, 4, NCH, 16]); m0 += 1024
    g8 = at("g8", m0, [P, 6, NCH, 8]); m0 += 768
    sml = at("sml", m0, [P, 16, NCH]); m0 += 256
    cnt = at("cnt", m0, [P, 4, NE]); m0 += 512
    slotf = at("slotf", m0, [P, 2, NCH]); m0 += 32
    wts = at("wts", m0, [P, 2, NCH]); m0 += 32
    bex = at("bex", m0, [P, NE]); m0 += 128
    bec = at("bec", m0, [P, 2]); m0 += 32
    brow = at("brow", m0, [1, P], I32); m0 += 512
    nbk = at("nbk", m0, [1, 1], I32); m0 += 32
    onep = at("onep", m0, [P, 8, BLK]); oneb = at("oneb", m0 + 4096, [P, 8, NTAB]); m0 += 4096 + 8 * NTAB * 4
    bpf = at("bpf", m0, [P, 4, 8]); m0 += 128
    bpi = at("bpi", m0, [P, 2, 8], I32); m0 += 64
    tabd = at("tabd", m0, [P, NTAB], I32); m0 += up(NTAB * 4)
    tabt = at("tabt", m0, [P, NTAB], I32); m0 += up(NTAB * 4)
    idx = at("idx", m0, [P, 4], U32); m0 += 32
    xb = at("xb", m0, [P, 2, KD * BLK]); lgT = at("lgT", m0, [NE, S]); m0 += 8192
    sg = at("sg", m0, [P, 4 * BLK]); m0 += 2048
    a1 = at("a1", m0, [P, 4 * BLK]); m0 += 2048
    act_ = at("act_", m0, [P, 2, 4 * BLK]); m0 += 4096
    xr = at("xr", m0, [BLK, 2, D]); m0 += 8192
    ysb = at("ysb", 98304, [BLK, 2, D])
    assert m0 <= 173248, m0
    rs2 = at("rs2", 173248, [P, S])
    sq2 = at("sq2", 49152, [P, KD, S])
    gat = at("gat", 0, [P, 2, NCH, D])
    fin = at("fin", 32768, [P, NCH, D])
    sq3 = at("sq3", 49152, [P, KD, S])
    x2 = at("x2", 98304, [P, KD, S])

    psum = ctx.enter_context(nc.psum_tensor("psum", [P, 8, 512], F32))

    def bk(b, n=1):
        return psum[:, b:b + n, :].rearrange("p b n -> p (b n)")

    steps = timeline()
    plan = bank_plan(steps)
    full = [ctx.enter_context(nc.semaphore(f"bank_full{i}")) for i in range(8)]
    empty = [ctx.enter_context(nc.semaphore(f"bank_read{i}")) for i in range(8)]

    def sem(name):
        return ctx.enter_context(nc.semaphore(name))

    x_in, c_in, const_in, cs_in, dft_in, small_in = map(sem, "x_in c_in const_in cs_in dft_in small_in".split())
    unit_in = [sem(f"unit_in{i}") for i in range(RING)]
    ada_free, spare_in, wdt_in, macc_ready = sem("ada_free"), sem("spare_in"), sem("wdt_in"), sem("macc_ready")
    x_again, wr_in = sem("x_again"), sem("wr_in")
    dve_c, act_c, pool_c = sem("dve_chain"), sem("act_chain"), sem("pool_chain")
    sq_ready, std_ready, silu_e, sil_ready, prep_ready = map(sem, "sq_ready std_ready silu_e sil_ready prep_ready".split())
    hm_ready, h_ready, padz = map(sem, "hm_ready h_ready padz".split())
    conv_done, tanh_done, xbc_ready, rope_ready = map(sem, "conv_done tanh_done xbc_ready rope_ready".split())
    dt_abs, dt_exp, dta_ready, ea_ready, wdd_ready, cds_ready = map(sem, "dt_abs dt_exp dta_ready ea_ready wdd_ready cds_ready".split())
    z_tanh, sc_ready = sem("z_tanh"), sem("sc_ready")
    smax_ready, exp_done, prob_ready = sem("smax_ready"), sem("exp_done"), sem("prob_ready")
    xdd_ready, xdd_used, state_ready, am_ready, am_used, xd_ready = map(sem, "xdd_ready xdd_used state_ready am_ready am_used xd_ready".split())
    decay_done, m_ready, gm_ready, y_done, ysq_done, ystd, ynorm_done = map(sem, "decay_done m_ready gm_ready y_done ysq_done ystd ynorm_done".split())
    gate_done, merge_done = sem("gate_done"), sem("merge_done")
    xb_full, xba_ready, xbd_ready, gate_mm, up_mm, down_mm = map(sem, "xb_full xba_ready xbd_ready gate_mm up_mm down_mm".split())
    act_ready, ya_done, yd_done, sig_ready, a1_done, xr_zero, idx_ready, idx_used, y_left, all_out = map(sem, "act_ready ya_done yd_done sig_ready a1_done xr_zero idx_ready idx_used y_left all_out".split())
    w_in = [[sem(f"w_in{j}_{k}") for k in range(3)] for j in range(2)]
    y_out, gat_in, h2_out, tab_ready = sem("y_out"), [sem(f"gat_in{c}") for c in range(NCH)], sem("h2_out"), sem("tab_ready")
    xr_in = [sem(f"xr_in{j}") for j in range(2)]
    fin_ready, fT_full, x2_ready, sq3_ready, ssq3_full, std3, out_ready, out_done, lg_ready, slot_ready = map(
        sem, "fin_ready fT_full x2_ready sq3_ready ssq3_full std3 out_ready out_done lg_ready slot_ready".split())
    x1_done, sq2_ready, h2_pre, h2_ready, half_ready = map(sem, "x1_done sq2_ready h2_pre h2_ready half_ready".split())
    rexp, rt_ready, asg_ready, bex_ready, route_done, brow_done, h2t_done = map(sem, "rexp rt_ready asg_ready bex_ready route_done brow_done h2t_done".split())

    SPARE = N_ADA1 - 1

    def ring_pos(u):
        return u if u < SPARE else u - 1

    def slot(u):
        return ada3[:, :] if u == SPARE else ring[:, ring_pos(u) % RING, :]

    def arrived(eng, u):
        if u == SPARE:
            eng.wait_ge(spare_in, 16)
        else:
            eng.wait_ge(unit_in[ring_pos(u) % RING], 16 * (ring_pos(u) // RING + 1))

    def job_full(eng, s):
        b, n = plan[s]
        eng.wait_ge(full[b], n)

    def job_read(eng, s):
        b, n = plan[s]
        eng.wait_ge(empty[b], n)

    def claim(eng, s):
        b, n = plan[s]
        if n > 1:
            eng.wait_ge(empty[b], n - 1)
        return b

    U_IN = N_ADA1
    mix_unit = {}
    u = U_IN + 2 * N_IN
    for i, n in enumerate(MIX_ORDER):
        mix_unit[n] = u
        u += 3
    U_WO = u
    N_UNITS = u + 2
    in_unit = {"xbc": lambda m: (0, m) if m < 4 else (1, m - 4), "k": lambda m: (1, 2), "v": lambda m: (1, 3),
               "fu": lambda m: (2, m), "q": lambda m: (3, m), "cg": lambda m: (4 + 3 * m // 4, 3 * m % 4),
               "sx": lambda m: (4 + (3 * m + 1) // 4, (3 * m + 1) % 4),
               "bg": lambda m: (4 + (3 * m + 2) // 4, (3 * m + 2) % 4)}
    unit_last = {}
    for i, x in enumerate([("xbcc", 3), ("vc",), ("fu", 3), ("q", 3), ("cg", 1), ("sx", 2), ("bg", 3), ("z", 3)]):
        unit_last[U_IN + 2 * i] = x
        unit_last[U_IN + 2 * i + 1] = ("mod", 1 + i)
    for n, x in mix_unit.items():
        unit_last.update({x: ("gate", n, 3), x + 1: ("proj", n, 7), x + 2: ("gate", n, 7)})

    st_chunk = ([4, 5, 0, 1, 2, 3], [5, 4, 3, 2, 1, 0])
    st_steps = [s for s in steps if s[0] == "st"]
    st_index = {s: i for i, s in enumerate(st_steps)}
    st_prev = {s: st_steps[i - 1] for i, s in enumerate(st_steps) if i}

    block = ctx.enter_context(nc.Block())

    @block.sync
    def _(sp):
        sp.dma_start(QC[:, :], cols).then_inc(small_in, 16)
        sp.dma_start(RW[:, :], rows).then_inc(small_in, 16)
        sp.dma_start(slot(0), stream[0]).then_inc(unit_in[0], 16)
        sp.dma_start(slot(1), stream[1]).then_inc(unit_in[1], 16)
        sp.dma_start(H[:, :, :], xT).then_inc(x_in, 16)
        sp.dma_start(CT[:, :], consts).then_inc(const_in, 16)
        sp.dma_start(slot(2), stream[2]).then_inc(unit_in[2], 16)
        sp.dma_start(hc[:, :, :], ctxT).then_inc(c_in, 16)
        sp.dma_start(slot(SPARE), stream[SPARE]).then_inc(spare_in, 16)
        for u in range(N_ADA1, N_UNITS):
            if ring_pos(u) < 2 * RING:
                sp.wait_ge(ada_free, ring_pos(u) - RING + 1)
            else:
                job_full(sp, unit_last[u - RING])
            sp.dma_start(slot(u), stream[u]).then_inc(unit_in[ring_pos(u) % RING], 16)
            if u == N_ADA1:
                sp.dma_start(WDT[:, :, :], wdt).then_inc(wdt_in, 16)
                sp.dma_start(cs[:, :, :], cossin).then_inc(cs_in, 16)
            if u == N_ADA1 + 2:
                job_full(sp, ("ssq",))
                job_full(sp, ("ssqc",))
                sp.dma_start(dftm[:, :, :, :], dft).then_inc(dft_in, 16)
        job_full(sp, ("gate", MIX_ORDER[-1], 7))
        sp.dma_start(H[:, :, :], xT).then_inc(x_again, 16)
        job_full(sp, ("proj", MIX_ORDER[-1], 7))
        sp.dma_start(WR[:, :, :], wrt).then_inc(wr_in, 16)

        for c in range(NCH):
            job_read(sp, ("h2tr", c))
            sp.dma_start(h2d[c * P:(c + 1) * P, :], h2t[:, c, :]).then_inc(h2_out, 16)

        job_full(sp, ("bexp",))
        sp.wait_ge(route_done, 2)
        n = sp.value_load(nbk[0:1, 0:1], min_val=1, max_val=MAXB)
        with sp.Fori(0, PAIRS) as i:
            for j in range(2):
                b = i * 2 + j
                with sp.If(b < n):
                    e = sp.value_load(brow[0:1, bass.ds(b, 1)], min_val=0, max_val=NE - 1)
                    for k, (w, used) in enumerate(((w1, gate_mm), (w3, up_mm), (w2, down_mm))):
                        sp.wait_ge(used, b + 1)
                        sp.dma_start(ering[:, j, k, :], w[bass.ds(e, 1), :, :].rearrange("a p n -> (a p) n")
                                     ).then_inc(w_in[j][k], 16)
        sp.wait_ge(all_out, 1)
        for c in range(NCH):
            sp.dma_start(gat[:, :, c, :], ybuf.rearrange("(k c p) n -> p k c n", k=2, p=P)[:, :, c, :]
                         ).then_inc(gat_in[c], 16)
        for k in range(KD):
            sp.wait_ge(out_ready, k + 1)
            sp.dma_start(outT[:, k, :], x2[:, k, :]).then_inc(out_done, 16)
        sp.wait_ge(out_done, 16 * KD)

    @block.tensor
    def _(pe):
        def mm(out, lhsT, rhs, start, stop):
            return nc.tensor.matmul(out, lhsT, rhs, start=start, stop=stop)

        ID = CT[:, C_ID:C_ID + P]

        def project(s, cols, unit, tile, ctx_side):
            b = claim(pe, s)
            w = slot(unit)
            for k in range(KD):
                rhs = hc[:, k, :] if ctx_side else H[:, k, :]
                ins = mm(bk(b)[:, 0:cols], w[:, k * S + tile * P:k * S + tile * P + P], rhs, k == 0, k == KD - 1)
            return ins.then_inc(full[b], 1)

        for s in steps:
            k0 = s[0]
            if k0 in ("ssq", "ssqc"):
                if k0 == "ssq":
                    pe.wait_ge(const_in, 16)
                b = claim(pe, s)
                n = S if k0 == "ssq" else SC
                for k in range(KD):
                    if k0 == "ssq":
                        pe.wait_ge(sq_ready, k + 1)
                        rhs = sq[:, k, :]
                    else:
                        pe.wait_ge(sq_ready, KD + k // 2 + 1)
                        rhs = sq[:, KD + k // 2, (k % 2) * SC:(k % 2) * SC + SC]
                    ins = mm(bk(b)[:, 0:n], CT[:, C_ONE:C_ONE + P], rhs, k == 0, k == KD - 1)
                ins.then_inc(full[b], 1)
            elif k0 == "mod" and s[1]:
                b = claim(pe, s)
                pe.wait_ge(macc_ready, s[1])
                for j in range(4):
                    ins = mm(bk(b)[:, 2 * j:2 * j + 2], macc[:, j * P:j * P + P], CT[:, C_ONE:C_ONE + 2], True, True)
                ins.then_inc(full[b], 1)
            elif k0 in ("mod01", "mod"):
                b = plan[("mod", 0)][0]
                units = (0, 1) if k0 == "mod01" else (2, 3)
                if k0 == "mod01":
                    pe.wait_ge(sil_ready, 1)
                for u in units:
                    arrived(pe, u)
                    for j in range(4):
                        o = (u * 4 + j) * 2
                        for k in range(KD):
                            ins = mm(bk(b)[:, o:o + 2], slot(u)[:, k * S + j * P:k * S + j * P + P],
                                     sil[:, 2 * k:2 * k + 2], k == 0, k == KD - 1)
                    ins.then_inc(*((full[b], 1) if u == SPARE else (ada_free, 1)))
            elif k0 in ("xbc", "xbcc", "k", "kc", "fu", "q", "cg", "sx", "bg"):
                ctx_side = k0 in ("xbcc", "kc")
                base, m = {"xbcc": "xbc", "kc": "k"}.get(k0, k0), s[1] if len(s) > 1 else 0
                iu, tile = in_unit[base](m)
                arrived(pe, U_IN + 2 * iu)
                if s == ("xbc", 0):
                    pe.wait_ge(h_ready, KD)
                if s == ("xbcc", 0):
                    pe.wait_ge(h_ready, 2 * KD)
                project(s, SC if ctx_side else S, U_IN + 2 * iu, tile, ctx_side)
            elif k0 in ("v", "vc"):
                b = claim(pe, s)
                for c in range(NCH if k0 == "v" else NCC):
                    for k in range(KD):
                        src = H if k0 == "v" else hc
                        ins = mm(bk(b)[:, c * P:c * P + P], src[:, k, c * P:c * P + P],
                                 slot(U_IN + 2)[:, k * S + 3 * P:k * S + 4 * P], k == 0, k == KD - 1)
                ins.then_inc(full[b], 1)
            elif k0 == "dt":
                b = claim(pe, s)
                pe.wait_ge(wdt_in, 16)
                for c in range(6):
                    src, cc = (H, c) if c < NCH else (hc, c - NCH)
                    for k in range(KD):
                        ins = mm(bk(b)[:, c * 16:c * 16 + 16], src[:, k, cc * P:cc * P + P], WDT[:, k, :],
                                 k == 0, k == KD - 1)
                ins.then_inc(full[b], 1)
            elif k0 == "z":
                b = claim(pe, s)
                c = s[1]
                arrived(pe, U_IN + 14)
                for k in range(KD):
                    ins = mm(bk(b), H[:, k, c * P:c * P + P], slot(U_IN + 14)[:, k * S:k * S + S], k == 0, k == KD - 1)
                ins.then_inc(full[b], 1)
            elif k0 == "rot":
                b = claim(pe, s)
                job_read(pe, ("k",) if s[1] == 0 else ("q", s[1] - 1))
                mm(bk(b), CT[:, C_PERM:C_PERM + P], ropet[:, s[1] % 2, :], True, True).then_inc(full[b], 1)
            elif k0 == "dec":
                b = claim(pe, s)
                pe.wait_ge(dta_ready, 1)
                for c in range(6):
                    o = c * 48
                    for col, (m, r0, r1) in zip((0, 8, 16, 24, 32), ((C_LE, 0, 8), (C_GE, 8, 16), (C_GT, 0, 8),
                                                                     (C_LT, 8, 16), (C_ONE, 0, 16))):
                        ins = mm(bk(b)[:, o + col:o + col + r1 - r0], CT[:, m:m + P], dta[:, c, r0:r1], True, True)
                ins.then_inc(full[b], 1)
            elif k0 == "xtr":
                b = claim(pe, s)
                pe.wait_ge(xbc_ready, 6)
                o = chunk_cols(s[1])
                for m in range(4):
                    ins = nc.tensor.transpose(bk(b)[:, m * P:m * P + P], xbcT[:, m, o:o + P], ID)
                ins.then_inc(full[b], 1)
            elif k0 == "btr":
                b = claim(pe, s)
                for i in range(3):
                    o = chunk_cols(3 * s[1] + i)
                    ins = nc.tensor.transpose(bk(b)[:, i * P:i * P + P], xbcT[:, 4, o:o + P], ID)
                ins.then_inc(full[b], 1)
            elif k0 == "V":
                b = claim(pe, s)
                ft = s[1]
                job_read(pe, ("fu", ft))
                for c in range(NCH):
                    ins = mm(bk(b, 2)[:, c * 256:c * 256 + 256], uT[:, ft, c * P:c * P + P],
                             CT[:, C_BD:C_BD + 256], True, True)
                ins.then_inc(full[b], 1)
            elif k0 == "F":
                b = claim(pe, s)
                ft = s[1]
                job_read(pe, ("V", ft))
                pe.wait_ge(dft_in, 16)
                for i in range(8):
                    c, part = i // 2, i % 2
                    ins = mm(bk(b), V[:, ft % 2, c * 256 + part * P:c * 256 + part * P + P],
                             dftm[:, part, c, :], i == 0, i == 7)
                ins.then_inc(full[b], 1)
            elif k0 == "st":
                d, k = s[1:]
                b = claim(pe, s)
                pe.wait_ge(xdd_ready, st_index[s] + 1)
                if s == ("st", 0, 0):
                    job_read(pe, ("btr", 1))
                c = st_chunk[d][k]
                for g in range(2):
                    ins = mm(bk(b)[g * 64:g * 64 + 64, 0:256], btm[:, c, g * 64:g * 64 + 64],
                             xdd[:, g * 256:g * 256 + 256], True, True)
                ins.then_inc(full[b], 1)
            elif k0 == "G":
                c, g = s[1:]
                b = claim(pe, s)
                o = c * P
                mm(bk(b)[:, 0:P], xbcT[g * 64:g * 64 + 64, 4, o:o + P], xbcT[g * 64:g * 64 + 64, 5, o:o + P],
                   True, True).then_inc(full[b], 1)
            elif k0 == "seg":
                c, g, d = s[1:]
                b = claim(pe, s)
                pe.wait_ge(am_ready, 2 * (2 * c + g) + d + 1)
                m = C_GT if d == 0 else C_LT
                mm(bk(b), CT[:, m:m + P], Am[:, d, :], True, True).then_inc(full[b], 1)
            elif k0 == "yoff":
                c, g = s[1:]
                b = claim(pe, s)
                for d in range(2):
                    if (c, g) == (0, 0):
                        job_read(pe, ("st", d, 4))
                    ins = mm(bk(b)[:, d * 256:d * 256 + 256], xbcT[g * 64:g * 64 + 64, 5, c * P:c * P + P],
                             prevS[g * 64:g * 64 + 64, d, c, :], True, True)
                ins.then_inc(full[b], 1)
            elif k0 == "y":
                c, g = s[1:]
                b = claim(pe, s)
                pe.wait_ge(m_ready, 2 * (2 * c + g + 1))
                pe.wait_ge(xd_ready, 2 * (c + 1))
                for h in range(4):
                    for d in range(2):
                        ins = mm(bk(b)[:, h * HD:h * HD + HD], E[:, d, h * P:h * P + P],
                                 xd[:, d, (g * 4 + h) * HD:(g * 4 + h) * HD + HD], d == 0, d == 1)
                ins.then_inc(full[b], 1)
            elif k0 == "ytr":
                b = claim(pe, s)
                c = s[1]
                pe.wait_ge(ynorm_done, c + 1)
                for m in range(4):
                    ins = nc.tensor.transpose(bk(b)[:, m * P:m * P + P], zs[:, c, m * P:m * P + P], ID)
                ins.then_inc(full[b], 1)
            elif k0 == "S":
                blk, g, j, keys, _ = head(s[1])
                b = claim(pe, s)
                if s[1] == 0:
                    pe.wait_ge(rope_ready, 5)
                    job_read(pe, ("kc",))
                rows_ = slice(g * 64, g * 64 + 64)
                for i, c in enumerate(keys):
                    rhs = kT[rows_, c * P:c * P + P] if c < NCH else kcT[rows_, (c - NCH) * P:(c - NCH) * P + P]
                    ins = mm(bk(b, 2)[:, i * P:i * P + P], qT[rows_, j, blk * P:blk * P + P], rhs, True, True)
                ins.then_inc(full[b], 1)
            elif k0 == "T":
                h = s[1]
                b = claim(pe, s)
                pe.wait_ge(prob_ready, h + 1)
                for i in range(len(head(h)[3])):
                    ins = nc.tensor.transpose(bk(b, 2)[:, i * P:i * P + P], sc[:, h % 3, i * P:i * P + P], ID)
                ins.then_inc(full[b], 1)
            elif k0 == "O":
                h = s[1]
                blk, g, j, keys, _ = head(h)
                b = claim(pe, s)
                job_read(pe, ("T", h))
                if h == 0:
                    job_read(pe, ("vc",))
                for i, c in enumerate(keys):
                    ins = mm(bk(b)[g * 64:g * 64 + 64, 0:P], vt[:, c, g * 64:g * 64 + 64], PT[:, i * P:i * P + P],
                             i == 0, i == len(keys) - 1)
                ins.then_inc(full[b], 1)
            elif k0 == "gate":
                n, d = s[1:]
                u = mix_unit[n] + (0 if d < 4 else 2)
                arrived(pe, u)
                project(s, S, u, d % 4, False)
            elif k0 == "proj":
                n, d = s[1:]
                b = claim(pe, s)
                if d == 0:
                    arrived(pe, mix_unit[n] + 1)
                    job_read(pe, {3: ("bg", 3), 2: ("F", 3), 0: ("O", 31), 1: ("ytr", 3)}[n])
                src = {3: scT, 2: uT, 0: attT, 1: ssmT}[n]
                for k in range(4):
                    ins = mm(bk(b), slot(mix_unit[n] + 1)[:, k * D + d * P:k * D + d * P + P], src[:, k, :],
                             k == 0, k == 3)
                ins.then_inc(full[b], 1)
            elif k0 == "wo":
                d = s[1]
                b = claim(pe, s)
                arrived(pe, U_WO + d // 4)
                pe.wait_ge(merge_done, 32)
                for k in range(KD):
                    ins = mm(bk(b), slot(U_WO + d // 4)[:, k * S + (d % 4) * P:k * S + (d % 4) * P + P],
                             merged[:, k, :], k == 0, k == KD - 1)
                ins.then_inc(full[b], 1)
            elif k0 == "ssq2":
                b = claim(pe, s)
                for k in range(KD):
                    pe.wait_ge(sq2_ready, k + 1)
                    ins = mm(bk(b), CT[:, C_ONE:C_ONE + P], sq2[:, k, :], k == 0, k == KD - 1)
                ins.then_inc(full[b], 1)
            elif k0 == "h2tr":
                b = claim(pe, s)
                c = s[1]
                pe.wait_ge(h2_ready, KD)
                for k in range(KD):
                    ins = nc.tensor.transpose(bk(b, 2)[:, k * P:k * P + P], h2[:, k, c * P:c * P + P], ID)
                ins.then_inc(full[b], 1)
            elif k0 == "rt":
                b = claim(pe, s)
                pe.wait_ge(wr_in, 16)
                for k in range(KD):
                    pe.wait_ge(h2_ready, k + 1)
                    ins = mm(bk(b)[0:NE, :], WR[:, k, :], h2[:, k, :], k == 0, k == KD - 1)
                ins.then_inc(full[b], 1)
            elif k0 == "rtt":
                b = claim(pe, s)
                job_read(pe, ("rt",))
                for c in range(NCH):
                    ins = nc.tensor.transpose(bk(b)[:, c * NE:c * NE + NE], lgT[:, c * P:c * P + P], CT[0:NE, C_ID:C_ID + NE])
                ins.then_inc(full[b], 1)
            elif k0 == "cnt":
                b = claim(pe, s)
                pe.wait_ge(asg_ready, 1)
                ones = CT[:, C_ONE:C_ONE + P]
                for c in range(NCH):
                    mm(bk(b)[:, 0:NE], ones, asg[:, c, :], c == 0, c == NCH - 1)
                for c in range(NCH):
                    for c2 in range(c + 1):
                        ins = mm(bk(b)[:, NE + c * NE:NE + c * NE + NE],
                                 CT[:, C_LT:C_LT + P] if c2 == c else ones, asg[:, c2, :], c2 == 0, c2 == c)
                ins.then_inc(full[b], 1)
            elif k0 == "bexp":
                b = claim(pe, s)
                pe.wait_ge(bex_ready, 1)
                mm(bk(b)[0:1, 0:P], bec[:, 0:1], ID, True, True).then_inc(full[b], 1)
            elif k0 == "tab":
                b = claim(pe, s)
                pe.wait_ge(tab_ready, 1)
                for i in range(8):
                    ins = mm(bk(b)[:, 0:NTAB], onep[:, i, :], oneb[:, i, :], i == 0, i == 7)
                ins.then_inc(full[b], 1)

        for credit, v in ((gate_mm, 2), (up_mm, 2), (down_mm, 2)):
            pe.sem_inc(credit, v)
        XB, HB, YB = bk(0, 2), bk(3, 2), bk(5, 2)

        def to_channels(j):
            for d in range(KD):
                ins = nc.tensor.transpose(XB[:, d * BLK:d * BLK + BLK], xr[:, j, d * P:d * P + P], ID)
            return ins

        for c in range(NCH):
            job_read(pe, ("h2tr", c))
        pe.wait_ge(route_done, 2)
        pe.wait_ge(xr_in[0], 16)
        to_channels(0).then_inc(xb_full, 1)
        n = pe.value_load(nbk[0:1, 0:1], min_val=1, max_val=MAXB)
        with pe.Fori(0, PAIRS) as i:
            for j in range(2):
                b = i * 2 + j
                with pe.If(b < n):
                    pe.wait_ge(xba_ready, b + 1)
                    pe.wait_ge(xbd_ready, b + 1)
                    pe.wait_ge(act_ready, b + 1)
                    for k, done in ((0, gate_mm), (1, up_mm)):
                        pe.wait_ge(w_in[j][k], i * 16 + 16)
                        for f in range(4):
                            for d in range(KD):
                                o = (4 * k + f) * BLK
                                ins = mm(HB[:, o:o + BLK], ering[:, j, k, d * S + f * P:d * S + f * P + P],
                                         xb[:, j, d * BLK:d * BLK + BLK], d == 0, d == KD - 1)
                        ins.then_inc(done, 1)
                    pe.wait_ge(xr_in[1 - j], i * 16 + 16 + 16 * j)
                    to_channels(1 - j).then_inc(xb_full, 1)
                    pe.wait_ge(act_ready, b + 2)
                    pe.wait_ge(ya_done, b + 1)
                    pe.wait_ge(yd_done, b + 1)
                    pe.wait_ge(w_in[j][2], i * 16 + 16)
                    for hf in range(2):
                        for f in range(4):
                            ins = mm(YB[:, hf * S:hf * S + S], act_[:, j, f * BLK:f * BLK + BLK],
                                     ering[:, j, 2, f * D + hf * S:f * D + hf * S + S], f == 0, f == 3)
                    ins.then_inc(down_mm, 1)
        for k in range(KD):
            b = k % 2
            if k == 0:
                pe.wait_ge(fin_ready, NCH)
            if k >= 2:
                pe.wait_ge(x2_ready, k - 1)
            for c in range(NCH):
                ins = nc.tensor.transpose(bk(b)[:, c * P:c * P + P], fin[:, c, k * P:k * P + P], ID)
            ins.then_inc(fT_full, 1)
        for k in range(KD):
            pe.wait_ge(sq3_ready, k + 1)
            ins = mm(bk(2), CT[:, C_ONE:C_ONE + P], sq3[:, k, :], k == 0, k == KD - 1)
        ins.then_inc(ssq3_full, 1)

    @block.scalar
    def _(act):
        t = Tally(act)
        def A(out, in_, f, **kw):
            return nc.scalar.activation(out, in_, f, **kw)

        act.wait_ge(small_in, 32)
        A(sil[:, :], QC[:, Q_C:Q_C + 16], ACT.Exp, scale=-1.0).then_inc(*t(silu_e))
        A(ea[:, :], RW[:, R_ALOG:R_ALOG + 16], ACT.Exp).then_inc(*t(ea_ready))
        act.wait_ge(x_in, 16)
        for k in range(KD):
            A(sq[:, k, :], H[:, k, :], ACT.Square).then_inc(*t(sq_ready))
        act.wait_ge(c_in, 16)
        for k in range(NCC * 2):
            A(sq[:, KD + k, :], hc[:, 2 * k:2 * k + 2, :].rearrange("p a n -> p (a n)"), ACT.Square).then_inc(*t(sq_ready))
        convs, ropes, z_i = 0, 0, 0
        for s in steps:
            k0 = s[0]
            t.settle()
            if k0 in ("ssq", "ssqc"):
                b, _n = plan[s]
                job_full(act, s)
                n, out = (S, rsx) if k0 == "ssq" else (SC, rsc)
                A(out[:, :], bk(b)[:, 0:n], ACT.Sqrt, scale=1.0 / D, bias=QC[:, Q_EPS:Q_EPS + 1]).then_inc(*t(empty[b], plan[s][1]))
            elif s == ("mod", 0):
                for w, dst in enumerate((H, hc)):
                    for k in range(KD):
                        act.wait_ge(hm_ready, w * KD + k + 1)
                        A(dst[:, k, :], dst[:, k, :], ACT.Identity, bias=mods[:, k, w:w + 1]).then_inc(*t(h_ready))
            elif k0 in ("xbc", "xbcc"):
                m = s[1]
                b, _n = plan[s]
                if k0 == "xbc" and m >= 2:
                    act.wait_ge(conv_done, m - 1)
                if s == ("xbc", 0):
                    act.wait_ge(padz, 1)
                job_full(act, s)
                if k0 == "xbc":
                    A(pads[:, m % 2, 1:1 + S], bk(b), ACT.Copy).then_inc(*t(empty[b], plan[s][1]))
                else:
                    A(pads[:, m % 2, S + 3:S + 3 + SC], bk(b)[:, 0:SC], ACT.Copy).then_inc(*t(empty[b], plan[s][1]))
                    for mm_ in ([m - 1] if m else []) + ([m] if m == 5 else []):
                        act.wait_ge(conv_done, mm_ + 1)
                        if mm_ >= 2:
                            act.wait_ge(xbc_ready, mm_ - 1)
                        A(th[:, mm_ % 2, 0:770], acc[:, mm_ % 2, 0:770], ACT.Tanh).then_inc(*t(tanh_done))
            elif k0 in ("k", "q"):
                i = 0 if k0 == "k" else s[1] + 1
                b, _n = plan[s]
                job_full(act, s)
                if i >= 2:
                    act.wait_ge(rope_ready, i - 1)
                A(ropet[:, i % 2, :], bk(b), ACT.Copy).then_inc(*t(empty[b], plan[s][1]))
            elif k0 in ("kc", "v", "vc", "fu"):
                b, _n = plan[s]
                job_full(act, s)
                out = {"kc": lambda: kcT[:, :], "v": lambda: vt[:, 0:4, :].rearrange("p a n -> p (a n)"),
                       "vc": lambda: vt[:, 4:6, :].rearrange("p a n -> p (a n)"), "fu": lambda: uT[:, s[1], :]}[k0]()
                n = SC if k0 in ("kc", "vc") else S
                A(out, bk(b)[:, 0:n], ACT.Copy).then_inc(*t(empty[b], plan[s][1]))
            elif k0 == "dt":
                act.wait_ge(dt_abs, 1)
                A(dts[:, 2, :], dts[:, 1, :], ACT.Exp, scale=-1.0).then_inc(*t(dt_exp))
            elif k0 == "dec":
                b, _n = plan[s]
                job_full(act, s)
                A(dec[:, :, :].rearrange("p a n -> p (a n)"), bk(b)[:, 0:288], ACT.Exp).then_inc(*t(empty[b], plan[s][1]))
            elif k0 == "cg":
                m = s[1]
                b, _n = plan[s]
                job_full(act, s)
                if m == 0:
                    act.wait_ge(xbc_ready, 6)
                else:
                    job_read(act, ("sx", m - 1))
                A(th[:, 0, 0:S], bk(b), ACT.Copy).then_inc(*t(empty[b], plan[s][1]))
            elif k0 == "z":
                c = s[1]
                b, _n = plan[s]
                job_full(act, s)
                if c == 0:
                    job_read(act, ("sx", 3))
                else:
                    job_read(act, ("z", c - 1))
                A(th[:, 0, 0:S], bk(b), ACT.Tanh, scale=0.5).then_inc(*t(z_tanh))
            elif k0 in ("xtr", "btr"):
                b, _n = plan[s]
                job_full(act, s)
                if k0 == "xtr":
                    A(xs[:, s[1], :], bk(b), ACT.Copy).then_inc(*t(empty[b], plan[s][1]))
                else:
                    A(btm[:, 3 * s[1]:3 * s[1] + 3, :].rearrange("p a n -> p (a n)"), bk(b)[:, 0:384],
                      ACT.Copy).then_inc(*t(empty[b], plan[s][1]))
            elif k0 == "V":
                ft = s[1]
                b, _n = plan[s]
                job_full(act, s)
                if ft == 0:
                    act.wait_ge(rope_ready, 5)
                if ft >= 2:
                    job_full(act, ("F", ft - 2))
                A(V[:, ft % 2, :], bk(b, 2), ACT.Copy).then_inc(*t(empty[b], plan[s][1]))
            elif k0 == "S":
                h = s[1]
                W = len(head(h)[3]) * P
                act.wait_ge(smax_ready, h + 1)
                A(sc[:, h % 3, 0:W], sc[:, h % 3, 0:W], ACT.Exp, bias=amx[:, h, 1:2],
                  accum_out=amx[:, h, 2:3]).then_inc(*t(exp_done))
                A(amx[:, h, 3:4], RW[:, R_SINK + hd_index(h):R_SINK + hd_index(h) + 1], ACT.Exp,
                  bias=amx[:, h, 1:2]).then_inc(*t(exp_done))
            elif k0 == "T":
                h = s[1]
                b, _n = plan[s]
                W = len(head(h)[3]) * P
                job_full(act, s)
                if h == 0:
                    job_read(act, ("z", 3))
                else:
                    job_full(act, ("O", h - 1))
                A(PT[:, 0:W], bk(b, 2)[:, 0:W], ACT.Copy).then_inc(*t(empty[b], plan[s][1]))
            elif k0 == "seg":
                c, g, d = s[1:]
                b, _n = plan[s]
                job_full(act, s)
                if 2 * c + g == 0:
                    job_full(act, ("F", 3))
                else:
                    job_full(act, ("y", (2 * c + g - 1) // 2, (2 * c + g - 1) % 2))
                A(E[:, d, :], bk(b), ACT.Exp).then_inc(*t(empty[b], plan[s][1]))
            elif k0 == "ynorm":
                act.wait_ge(y_done, 8)
                for c in range(NCH):
                    t.settle()
                    A(E[:, 0, :], zs[:, c, :], ACT.Square, accum_out=yst[:, c:c + 1]).then_inc(*t(ysq_done))
                act.wait_ge(ysq_done, NCH)
                A(yst[:, 4:8], yst[:, 0:4], ACT.Sqrt, scale=1.0 / S, bias=QC[:, Q_EPS4:Q_EPS4 + 1]).then_inc(*t(ystd))
            elif k0 == "gate":
                n, d = s[1:]
                b, _n = plan[s]
                job_full(act, s)
                i = MIX_ORDER.index(n) * 8 + d
                if i:
                    job_read(act, ("proj", MIX_ORDER[(i - 1) // 8], (i - 1) % 8))
                else:
                    job_read(act, ("z", 3))
                    act.wait_ge(half_ready, 1)
                A(gth[:, :], bk(b), ACT.Tanh, scale=0.5, bias=half[:, n * 8 + d:n * 8 + d + 1]).then_inc(*t(empty[b], plan[s][1]))
            elif k0 == "ssq2":
                for k in range(KD):
                    if k == 0:
                        job_full(act, ("wo", 7))
                    job_read(act, ("wo", k))
                    A(sq2[:, k, :], H[:, k, :], ACT.Square).then_inc(*t(sq2_ready))
                b, _n = plan[s]
                A(sqw[:, :], QC[:, Q_EPS:Q_EPS + 1], ACT.Sqrt).then_inc(*t(act_c))
                job_full(act, s)
                A(rs2[:, :], bk(b), ACT.Sqrt, scale=1.0 / D, bias=QC[:, Q_EPS:Q_EPS + 1]).then_inc(*t(empty[b], plan[s][1]))
                for k in range(KD):
                    act.wait_ge(h2_pre, k + 1)
                    A(h2[:, k, :], h2[:, k, :], ACT.Identity, bias=mods[:, 24 + k, 0:1]).then_inc(*t(h2_ready))
            elif k0 == "h2tr":
                b, _n = plan[s]
                job_full(act, s)
                A(h2t[:, s[1], :], bk(b, 2), ACT.Copy).then_inc(*t(empty[b], plan[s][1]))
            elif k0 == "rt":
                b, _n = plan[s]
                job_full(act, s)
                A(lgT[:, :], bk(b)[0:NE, :], ACT.Copy).then_inc(*t(empty[b], plan[s][1]))
            elif k0 == "rtt":
                act.wait_ge(lg_ready, 1)
                A(w32[:, :, :], lg[:, :, :], ACT.Exp, scale=-1.0).then_inc(*t(rexp))

        act.sem_inc(ya_done, 1)
        XB, HB, YB = bk(0), bk(3), bk(5)
        act.wait_ge(xb_full, 1)
        A(xb[:, 0, 0:S], XB, ACT.Copy).then_inc(xba_ready, 1)
        act.wait_ge(route_done, 2)
        n = act.value_load(nbk[0:1, 0:1], min_val=1, max_val=MAXB)
        with act.Fori(0, PAIRS) as i:
            for j in range(2):
                b = i * 2 + j
                with act.If(b < n):
                    act.wait_ge(gate_mm, b + 3)
                    A(sg[:, :], HB, ACT.Sigmoid).then_inc(sig_ready, 1)
                    act.wait_ge(xb_full, b + 2)
                    A(xb[:, 1 - j, 0:S], XB, ACT.Copy).then_inc(xba_ready, 1)
                    act.wait_ge(down_mm, b + 3)
                    act.wait_ge(y_left, b + 1)
                    A(ysb[:, j, 0:S], YB, ACT.Copy).then_inc(ya_done, 1)
        for k in range(KD):
            act.wait_ge(x2_ready, k + 1)
            A(sq3[:, k, :], x2[:, k, :], ACT.Square).then_inc(sq3_ready, 1)
        act.wait_ge(ssq3_full, 1)
        A(rs2[:, :], bk(2), ACT.Sqrt, scale=1.0 / D, bias=QC[:, Q_EPS:Q_EPS + 1]).then_inc(std3, 1)

    @block.vector
    def _(v):
        t = Tally(v)
        V_ = nc.vector

        def link(ins):
            ins.then_inc(*t(dve_c))
            t.settle()

        def TT(out, a, b, op):
            return V_.tensor_tensor(out, a, b, op)

        link(V_.memset(pads[:, :, :], 0.0))
        V_.memset(yst[:, :], 0.0).then_inc(*t(padz))
        v.wait_ge(small_in, 32)
        V_.tensor_scalar(half[:, :], QC[:, Q_BG:Q_BG + 56], 0.5, None, ALU.mult).then_inc(*t(half_ready))
        v.wait_ge(silu_e, 1)
        link(V_.tensor_scalar(sil[:, :], sil[:, :], 1.0, None, ALU.add))
        link(V_.reciprocal(sil[:, :], sil[:, :]))
        TT(sil[:, :], sil[:, :], QC[:, Q_C:Q_C + 16], ALU.mult).then_inc(*t(sil_ready))

        def conv(x, w, a, n):
            link(V_.scalar_tensor_tensor(a, x[:, 1:1 + n], w[1], a, ALU.mult, ALU.add))
            return V_.scalar_tensor_tensor(a, x[:, 2:2 + n], w[2], a, ALU.mult, ALU.add)

        def xbc_finish(m):
            v.wait_ge(tanh_done, m + 1)
            V_.scalar_tensor_tensor(xbcT[:, m, :], th[:, m % 2, 0:770], 1.0, acc[:, m % 2, 0:770], ALU.add,
                                    ALU.mult).then_inc(*t(xbc_ready))

        def norm_probs(h):
            W = len(head(h)[3]) * P
            v.wait_ge(exp_done, 2 * h + 2)
            link(TT(amx[:, h, 4:5], amx[:, h, 2:3], amx[:, h, 3:4], ALU.add))
            link(V_.reciprocal(amx[:, h, 5:6], amx[:, h, 4:5]))
            V_.tensor_scalar(sc[:, h % 3, 0:W], sc[:, h % 3, 0:W], amx[:, h, 5:6], None, ALU.mult).then_inc(*t(prob_ready))

        def hb(ap, n):
            return ap.unsqueeze(2).to_broadcast([P, ap.shape[1], n])

        for s in steps:
            k0 = s[0]
            t.settle()
            b = plan[s][0] if s in plan else None
            if k0 in ("ssq", "ssqc", "ssq2"):
                if k0 == "ssq2":
                    link(V_.scalar_tensor_tensor(A1[:, :, 1], mods[:, 32:40, 0], 1.0, QC[:, Q_G2:Q_G2 + 8], ALU.add,
                                                 ALU.mult))
                job_read(v, s)
                out = {"ssq": rsx, "ssqc": rsc, "ssq2": rs2}[k0]
                link(V_.reciprocal(out[:, :], out[:, :]))
                if k0 == "ssq2":
                    for k in range(KD):
                        V_.scalar_tensor_tensor(h2[:, k, :], H[:, k, :], A1[:, k, 1:2], rs2[:, :], ALU.mult,
                                                ALU.mult).then_inc(*t(h2_pre))
            elif s == ("mod", 0):
                job_full(v, s)
                TT(mods[:, 0:16, :], bk(b)[:, 0:32].rearrange("p (j w) -> p j w", w=2),
                   hb(QC[:, Q_BADA:Q_BADA + 16], 2), ALU.add).then_inc(*t(empty[b], plan[s][1]))
                job_read(v, s)
                link(V_.scalar_tensor_tensor(A1[:, :, :], mods[:, 8:16, :], 1.0, hb(QC[:, Q_G1:Q_G1 + 8], 2),
                                             ALU.add, ALU.mult))
                for k in range(KD):
                    V_.scalar_tensor_tensor(H[:, k, :], H[:, k, :], A1[:, k, 0:1], rsx[:, :], ALU.mult,
                                            ALU.mult).then_inc(*t(hm_ready))
                for k in range(KD):
                    V_.scalar_tensor_tensor(hc[:, k, :], hc[:, k, :], A1[:, k, 1:2], rsc[:, :], ALU.mult,
                                            ALU.mult).then_inc(*t(hm_ready))
            elif k0 == "macc":
                if s[1] > 1:
                    job_full(v, ("mod", s[1] - 1))
                u = U_IN + 2 * s[1] - 1
                arrived(v, u)
                link(V_.tensor_scalar(macc[:, :], slot(u)[:, 0:S], sil[:, 0:1], None, ALU.mult))
                for k in range(1, KD):
                    ins = V_.scalar_tensor_tensor(macc[:, :], slot(u)[:, k * S:k * S + S], sil[:, 2 * k:2 * k + 1],
                                                  macc[:, :], ALU.mult, ALU.add)
                    if k < KD - 1:
                        link(ins)
                ins.then_inc(*t(macc_ready))
            elif k0 == "mod":
                job_full(v, s)
                o = 16 + 4 * (s[1] - 1)
                TT(mods[:, o:o + 4, :], bk(b)[:, 0:8].rearrange("p (j w) -> p j w", w=2),
                   hb(QC[:, Q_BADA + o:Q_BADA + o + 4], 2), ALU.add).then_inc(*t(empty[b], plan[s][1]))
            elif k0 == "xbcc":
                m = s[1]
                job_read(v, ("xbc", m))
                job_read(v, s)
                w = [half[:, 32 + q * 6 + m:33 + q * 6 + m] for q in range(3)]
                x, a = pads[:, m % 2, :], acc[:, m % 2, 0:770]
                link(V_.tensor_scalar(a, x[:, 0:770], w[0], half[:, 50 + m:51 + m], ALU.mult, ALU.add))
                conv(x, w, a, 770).then_inc(*t(conv_done))
                if m:
                    xbc_finish(m - 1)
                if m == 5:
                    xbc_finish(5)
            elif k0 == "dt":
                job_full(v, s)
                T_ = [dts[:, i, :] for i in range(8)]
                x3 = dts[:, 0, :].rearrange("p (c n) -> p c n", n=16)
                TT(x3, bk(b)[:, 0:96].rearrange("p (c n) -> p c n", n=16),
                   RW[:, R_DTB:R_DTB + 16].unsqueeze(1).to_broadcast([P, 6, 16]), ALU.add).then_inc(*t(empty[b], plan[s][1]))
                job_read(v, s)
                V_.scalar_tensor_tensor(T_[1], T_[0], -1.0, T_[0], ALU.mult, ALU.max).then_inc(*t(dt_abs))
                v.wait_ge(dt_exp, 1)
                link(V_.tensor_scalar(T_[3], T_[2], 2.0, None, ALU.add))
                link(V_.reciprocal(T_[3], T_[3]))
                link(TT(T_[3], T_[2], T_[3], ALU.mult))
                link(TT(T_[4], T_[3], T_[3], ALU.mult))
                link(V_.tensor_scalar(T_[5], T_[4], 1.0 / 15, None, ALU.mult))
                for q in (13, 11, 9, 7, 5, 3):
                    link(V_.scalar_tensor_tensor(T_[5], T_[5], 1.0 / q, T_[4], ALU.add, ALU.mult))
                link(V_.scalar_tensor_tensor(T_[5], T_[5], 1.0, T_[3], ALU.add, ALU.mult))
                link(V_.tensor_scalar(T_[6], T_[0], 0.0, None, ALU.max))
                link(V_.scalar_tensor_tensor(dtv[:, :, :].rearrange("p c n -> p (c n)"), T_[5], 2.0, T_[6],
                                             ALU.mult, ALU.add))
                v.wait_ge(ea_ready, 1)
                V_.scalar_tensor_tensor(dta[:, :, :], dtv[:, :, :], -1.0,
                                        ea[:, :].unsqueeze(1).to_broadcast([P, 6, 16]), ALU.mult,
                                        ALU.mult).then_inc(*t(dta_ready))
            elif k0 == "dec":
                job_read(v, s)
                TT(wdd[:, :, :], dtv[:, :, :], dec[:, :, 16:32], ALU.mult).then_inc(*t(wdd_ready))
                for g in range(2):
                    r = slice(g * 64, g * 64 + 64)
                    for d in range(2):
                        V_.tensor_copy(cds[r, :, d, :], dec[r, :, 32 + d * 8 + g * 4:36 + d * 8 + g * 4]).then_inc(*t(cds_ready))
            elif k0 == "rot":
                i = s[1]
                job_full(v, s)
                v.wait_ge(cs_in, 16)
                link(TT(ropet[:, 2, :], ropet[:, i % 2, :], cs[:, 0, :], ALU.mult))
                TT(ropet[:, 3, :], bk(b), cs[:, 1, :], ALU.mult).then_inc(*t(empty[b], plan[s][1]))
                job_read(v, s)
                TT(kT[:, :] if i == 0 else qT[:, i - 1, :], ropet[:, 2, :], ropet[:, 3, :], ALU.add).then_inc(*t(rope_ready))
            elif k0 == "sx":
                m = s[1]
                job_read(v, ("cg", m))
                job_full(v, s)
                TT(pads[:, m % 2, 1:1 + S], bk(b), th[:, 0, 0:S], ALU.mult).then_inc(*t(empty[b], plan[s][1]))
                job_read(v, s)
                if m < 2:
                    link(V_.memset(pads[:, m % 2, 1 + S:2 + S], 0.0))
                w = [QC[:, Q_SW + q * 4 + m:Q_SW + q * 4 + m + 1] for q in range(3)]
                x, a = pads[:, m % 2, :], acc[:, m % 2, 0:S]
                link(V_.tensor_scalar(a, x[:, 0:S], w[0], None, ALU.mult))
                link(conv(x, w, a, S))
            elif k0 == "bg":
                m = s[1]
                job_full(v, s)
                TT(scT[:, m, :], bk(b), acc[:, m % 2, 0:S], ALU.mult).then_inc(*t(empty[b], plan[s][1]))
            elif k0 == "z":
                c = s[1]
                v.wait_ge(z_tanh, c + 1)
                V_.scalar_tensor_tensor(zs[:, c, :], th[:, 0, 0:S], 1.0, bk(b), ALU.add, ALU.mult).then_inc(*t(empty[b], plan[s][1]))
            elif k0 == "F":
                job_full(v, s)
                V_.tensor_copy(uT[:, s[1], :], bk(b)).then_inc(*t(empty[b], plan[s][1]))
            elif k0 == "S":
                h = s[1]
                keys, mo = head(h)[3:]
                W = len(keys) * P
                job_full(v, s)
                if h >= 3:
                    job_full(v, ("T", h - 3))
                V_.scalar_tensor_tensor(sc[:, h % 3, 0:W], bk(b, 2)[:, 0:W], HD ** -0.5,
                                        CT[:, C_MASK + mo:C_MASK + mo + W], ALU.mult, ALU.add).then_inc(*t(empty[b], plan[s][1]))
                job_read(v, s)
                link(V_.tensor_reduce(amx[:, h, 0:1], sc[:, h % 3, 0:W], AX.X, ALU.max))
                V_.tensor_scalar(amx[:, h, 1:2], amx[:, h, 0:1], RW[:, R_SINK + hd_index(h):R_SINK + hd_index(h) + 1],
                                 -1.0, ALU.max, ALU.mult).then_inc(*t(smax_ready))
                if h >= 1:
                    norm_probs(h - 1)
            elif k0 == "T":
                if s[1] == 30:
                    norm_probs(31)
            elif k0 == "O":
                h = s[1]
                blk, g, j = head(h)[:3]
                r = slice(g * 64, g * 64 + 64)
                job_full(v, s)
                V_.tensor_copy(attT[r, j, blk * P:blk * P + P], bk(b)[r, 0:P]).then_inc(*t(empty[b], plan[s][1]))
            elif k0 == "st":
                d, k = s[1:]
                c = st_chunk[d][k]
                if s == ("st", 0, 0):
                    job_full(v, ("xtr", 3))
                    v.wait_ge(cds_ready, 4)
                dst = tmpS[:, d, :] if k == 0 else prevS[:, d, st_chunk[d][k + 1], :]
                job_full(v, s)
                if k == 0:
                    V_.tensor_copy(dst, bk(b)[:, 0:256]).then_inc(*t(empty[b], plan[s][1]))
                else:
                    old = tmpS[:, d, :] if k == 1 else prevS[:, d, c, :]
                    job_read(v, ("st", d, k - 1))
                    link(TT(ytmp[:, 0, :].rearrange("p (h n) -> p h n", h=4), old.rearrange("p (h n) -> p h n", h=4),
                            hb(cds[:, c, d, :], HD), ALU.mult))
                    TT(dst, ytmp[:, 0, :], bk(b)[:, 0:256], ALU.add).then_inc(*t(empty[b], plan[s][1]))
            elif k0 == "G":
                job_full(v, s)
                if s[1:] == (0, 0):
                    link(TT(Gm[:, 0, :], bk(b)[:, 0:P], CT[:, C_LE:C_LE + P], ALU.mult))
                else:
                    TT(Gm[:, 0, :], bk(b)[:, 0:P], CT[:, C_LE:C_LE + P], ALU.mult).then_inc(*t(gm_ready))
                TT(Gm[:, 1, :], bk(b)[:, 0:P], CT[:, C_GE:C_GE + P], ALU.mult).then_inc(*t(empty[b], plan[s][1]))
            elif k0 == "seg":
                c, g, d = s[1:]
                job_read(v, ("G", c, g))
                job_read(v, s)
                e3 = E[:, d, :].rearrange("p (h n) -> p h n", h=4)
                TT(e3, e3, Gm[:, d, :].unsqueeze(1).to_broadcast([P, 4, P]), ALU.mult).then_inc(*t(m_ready))
            elif k0 == "yoff":
                c, g = s[1:]
                job_full(v, s)
                y4 = ytmp[:, 0:2, :].rearrange("p d (h n) -> p d h n", h=4)
                e4 = dec[:, c, 0:16].rearrange("p (d h) -> p d h", d=2)[:, :, g * 4:g * 4 + 4]
                TT(y4, bk(b).rearrange("p (d h n) -> p d h n", d=2, h=4),
                   e4.unsqueeze(3).to_broadcast([P, 2, 4, HD]), ALU.mult).then_inc(*t(empty[b], plan[s][1]))
            elif k0 == "y":
                c, g = s[1:]
                job_read(v, ("yoff", c, g))
                x3 = xs[:, c, g * 256:g * 256 + 256].rearrange("p (h n) -> p h n", h=4)
                link(TT(ytmp[:, 2, :].rearrange("p (h n) -> p h n", h=4), x3,
                        hb(RW[:, R_D + g * 4:R_D + g * 4 + 4], HD), ALU.mult))
                link(TT(ytmp[:, 0, :], ytmp[:, 0, :], ytmp[:, 1, :], ALU.add))
                link(TT(ytmp[:, 0, :], ytmp[:, 0, :], ytmp[:, 2, :], ALU.add))
                job_full(v, s)
                TT(ytmp[:, 0, :], ytmp[:, 0, :], bk(b)[:, 0:256], ALU.add).then_inc(*t(empty[b], plan[s][1]))
                job_read(v, s)
                zz = zs[:, c, g * 256:g * 256 + 256]
                TT(zz, zz, ytmp[:, 0, :], ALU.mult).then_inc(*t(y_done))
            elif k0 == "ynorm":
                v.wait_ge(ystd, 1)
                link(V_.reciprocal(yst[:, 8:12], yst[:, 4:8]))
                for c in range(NCH):
                    V_.tensor_scalar(zs[:, c, :], zs[:, c, :], yst[:, 8 + c:9 + c], None, ALU.mult).then_inc(*t(ynorm_done))
            elif k0 == "ytr":
                c = s[1]
                job_full(v, s)
                TT(ssmT[:, :, c * P:c * P + P], bk(b).rearrange("p (m n) -> p m n", m=4),
                   hb(QC[:, Q_SN:Q_SN + 4], P), ALU.mult).then_inc(*t(empty[b], plan[s][1]))
            elif k0 == "proj":
                n, d = s[1:]
                job_full(v, s)
                job_read(v, ("gate", n, d))
                first = n == MIX_ORDER[0]
                V_.scalar_tensor_tensor(merged[:, d, :] if first else mtmp[:, :], gth[:, :], 1.0, bk(b), ALU.add,
                                        ALU.mult).then_inc(*t(empty[b], plan[s][1]))
                if first:
                    V_.memset(yst[:, 0:1], 0.0).then_inc(*t(merge_done))
                else:
                    job_read(v, s)
                    TT(merged[:, d, :], merged[:, d, :], mtmp[:, :], ALU.add).then_inc(*t(merge_done))
            elif k0 == "wo":
                d = s[1]
                if d == 0:
                    link(V_.tensor_scalar(A1[:, :, 0], mods[:, 16:24, 0], 0.5, None, ALU.mult))
                    v.wait_ge(x_again, 16)
                job_full(v, s)
                V_.scalar_tensor_tensor(H[:, d, :], bk(b), A1[:, d, 0:1], H[:, d, :], ALU.mult,
                                        ALU.add).then_inc(*t(empty[b], plan[s][1]))
            elif k0 == "rtt":
                job_full(v, s)
                V_.tensor_scalar(lg[:, :, :].rearrange("p c n -> p (c n)"), bk(b)[:, 0:NCH * NE], -87.0, None,
                                 ALU.max).then_inc(*t(lg_ready))
                v.wait_ge(rexp, 1)
                link(V_.tensor_scalar(w32[:, :, :], w32[:, :, :], 1.0, None, ALU.add))
                link(V_.reciprocal(lg[:, :, :], w32[:, :, :]))
                link(TT(sel[:, :, :], lg[:, :, :], RW[:, R_RB:R_RB + NE].unsqueeze(1).to_broadcast([P, NCH, NE]), ALU.add))
                p2 = sel[:, :, :].rearrange("p c (h t) -> p c h t", t=2)
                link(TT(g16[:, 0], p2[:, :, :, 0], p2[:, :, :, 1], ALU.max))
                link(TT(g16[:, 1], p2[:, :, :, 0], p2[:, :, :, 1], ALU.min))
                hi = g16[:, 0].rearrange("p c (g t) -> p c g t", t=2)
                lo = g16[:, 1].rearrange("p c (g t) -> p c g t", t=2)
                link(TT(g8[:, 0], hi[:, :, :, 0], hi[:, :, :, 1], ALU.max))
                link(TT(g8[:, 1], hi[:, :, :, 0], hi[:, :, :, 1], ALU.min))
                link(TT(g8[:, 2], lo[:, :, :, 0], lo[:, :, :, 1], ALU.max))
                link(TT(g8[:, 1], g8[:, 1], g8[:, 2], ALU.max))
                link(TT(g8[:, 0], g8[:, 0], g8[:, 1], ALU.add))

                def first_max(out, x, iota, tmp, sm):
                    n = x.shape[2]
                    link(V_.tensor_reduce(sm, x, AX.X, ALU.max))
                    link(TT(tmp, x, sm.unsqueeze(2).to_broadcast([P, NCH, n]), ALU.is_equal))
                    link(V_.scalar_tensor_tensor(tmp, tmp, -1000.0, iota.unsqueeze(1).to_broadcast([P, NCH, n]),
                                                 ALU.mult, ALU.add))
                    link(V_.tensor_reduce(sm, tmp, AX.X, ALU.min))
                    link(TT(out, tmp, sm.unsqueeze(2).to_broadcast([P, NCH, n]), ALU.is_equal))

                first_max(g8[:, 3], g8[:, 0], RW[:, R_IG:R_IG + 8], g8[:, 1], sml[:, 0])
                link(V_.tensor_scalar(g8[:, 4], g8[:, 3], 1.0e30, -1.0e30, ALU.mult, ALU.add))
                s4 = sel[:, :, :].rearrange("p c (g t) -> p (c g) t", t=4)
                m4 = selm[:, :, :].rearrange("p c (g t) -> p (c g) t", t=4)

                def flat(x):
                    return x.rearrange("p c g -> p (c g)").unsqueeze(2).to_broadcast([P, NCH * 8, 4])

                link(TT(m4, s4, flat(g8[:, 3]), ALU.mult))
                link(TT(m4, m4, flat(g8[:, 4]), ALU.add))
                first_max(oh[:, 0], selm[:, :, :], RW[:, R_IE:R_IE + NE], w32[:, :, :], sml[:, 1])
                link(V_.scalar_tensor_tensor(selm[:, :, :], oh[:, 0], -1.0e31, selm[:, :, :], ALU.mult, ALU.add))
                first_max(oh[:, 1], selm[:, :, :], RW[:, R_IE:R_IE + NE], w32[:, :, :], sml[:, 1])
                TT(asg[:, :, :], oh[:, 0], oh[:, 1], ALU.add).then_inc(*t(asg_ready))
                for k in range(2):
                    link(TT(w32[:, :, :], oh[:, k], lg[:, :, :], ALU.mult))
                    link(V_.tensor_reduce(wts[:, k, :], w32[:, :, :], AX.X, ALU.add))
                link(TT(sml[:, 2], wts[:, 0, :], wts[:, 1, :], ALU.add))
                link(V_.reciprocal(sml[:, 2], sml[:, 2]))
                for k in range(2):
                    link(TT(wts[:, k, :], wts[:, k, :], sml[:, 2], ALU.mult))
            elif k0 == "cnt":
                job_full(v, s)
                C = cnt
                link(V_.tensor_copy(C[:, 0, :], bk(b)[:, 0:NE]))
                link(V_.tensor_scalar(C[:, 1, :], C[:, 0, :], 0.0, None, ALU.is_gt))
                for q in range(1, S // BLK):
                    link(V_.scalar_tensor_tensor(C[:, 1, :], C[:, 0, :], float(q * BLK), C[:, 1, :], ALU.is_gt, ALU.add))
                link(V_.memset(C[:, 3, :], 0.0))
                link(V_.tensor_tensor_scan(C[:, 2, :], C[:, 1, :], C[:, 3, :], 0.0, ALU.add, ALU.add))
                link(TT(C[:, 3, :], C[:, 2, :], C[:, 1, :], ALU.subtract))
                link(V_.tensor_scalar(bex[:, :], C[:, 2, :], QC[:, Q_IOTA:Q_IOTA + 1], None, ALU.is_le))
                link(V_.tensor_reduce(bec[:, 1:2], bex[:, :], AX.X, ALU.add))
                V_.tensor_scalar(bec[:, 0:1], bec[:, 1:2], float(NE - 1), None, ALU.min).then_inc(*t(bex_ready))
                rk = bk(b)[:, NE:NE + NCH * NE].rearrange("p (c n) -> p c n", n=NE)
                st64 = C[:, 3, :].unsqueeze(1).to_broadcast([P, NCH, NE])
                V_.scalar_tensor_tensor(w32b[:, :, :], st64, float(BLK), rk, ALU.mult, ALU.add).then_inc(*t(empty[b], plan[s][1]))
                job_read(v, s)
                for k in range(2):
                    link(TT(w32[:, :, :], oh[:, k], w32b[:, :, :], ALU.mult))
                    link(V_.tensor_reduce(slotf[:, k, :], w32[:, :, :], AX.X, ALU.add))
                sf = slotf[:, :, :].rearrange("p k c -> p (k c)")
                link(V_.tensor_copy(bpi[:, 0], sf))
                link(V_.tensor_scalar(bpi[:, 1], bpi[:, 0], BLK.bit_length() - 1, None, ALU.arith_shift_right))
                link(V_.tensor_copy(bpf[:, 1], bpi[:, 1]))
                link(V_.scalar_tensor_tensor(bpf[:, 0], bpf[:, 1], -float(BLK), sf, ALU.mult, ALU.add))
                link(TT(bpf[:, 2], QC[:, Q_DST:Q_DST + 8], bpf[:, 0], ALU.subtract))
                link(TT(onep[:, :, :], RW[:, R_IB:R_IB + BLK].unsqueeze(1).to_broadcast([P, 8, BLK]), hb(bpf[:, 0], BLK),
                        ALU.is_equal))
                link(TT(oneb[:, :, :], RW[:, R_IB:R_IB + NTAB].unsqueeze(1).to_broadcast([P, 8, NTAB]),
                        hb(bpf[:, 1], NTAB), ALU.is_equal))
                TT(oneb[:, :, :], oneb[:, :, :], hb(bpf[:, 2], NTAB), ALU.mult).then_inc(*t(tab_ready))
            elif k0 == "bexp":
                job_full(v, s)
                V_.tensor_copy(brow[0:1, :], bk(b)[0:1, 0:P]).then_inc(*t(route_done))
                V_.tensor_copy(nbk[0:1, 0:1], cnt[0:1, 2, NE - 1:NE]).then_inc(*t(route_done))
            elif k0 == "tab":
                job_full(v, s)
                link(V_.tensor_scalar(tabd[:, :], bk(b)[:, 0:NTAB], QC[:, Q_DUMP:Q_DUMP + 1], None, ALU.add))
                V_.tensor_scalar(tabt[:, :], tabd[:, :], 2 * S + S - 1, None, ALU.bitwise_and).then_inc(*t(slot_ready))

        v.sem_inc(act_ready, 1)
        v.sem_inc(yd_done, 1)
        XB, HB, YB = bk(1), bk(3, 2), bk(6)
        v.wait_ge(xb_full, 1)
        V_.tensor_copy(xb[:, 0, S:2 * S], XB).then_inc(xbd_ready, 1)
        v.wait_ge(route_done, 2)
        n = v.value_load(nbk[0:1, 0:1], min_val=1, max_val=MAXB)
        with v.Fori(0, PAIRS) as i:
            for j in range(2):
                b = i * 2 + j
                with v.If(b < n):
                    v.wait_ge(sig_ready, b + 1)
                    TT(a1[:, :], sg[:, :], HB[:, 0:4 * BLK], ALU.mult).then_inc(a1_done, 1)
                    v.wait_ge(a1_done, b + 1)
                    v.wait_ge(up_mm, b + 3)
                    TT(act_[:, j, :], a1[:, :], HB[:, 4 * BLK:8 * BLK], ALU.mult).then_inc(act_ready, 1)
                    v.wait_ge(xb_full, b + 2)
                    V_.tensor_copy(xb[:, 1 - j, S:2 * S], XB).then_inc(xbd_ready, 1)
                    v.wait_ge(down_mm, b + 3)
                    v.wait_ge(y_left, b + 1)
                    V_.tensor_copy(ysb[:, j, S:2 * S], YB).then_inc(yd_done, 1)
        for c in range(NCH):
            v.wait_ge(gat_in[c], 16)
            link(V_.tensor_scalar(fin[:, c, :], gat[:, 0, c, :], wts[:, 0, c:c + 1], None, ALU.mult))
            V_.scalar_tensor_tensor(fin[:, c, :], gat[:, 1, c, :], wts[:, 1, c:c + 1], fin[:, c, :], ALU.mult,
                                    ALU.add).then_inc(fin_ready, 1)
        for k in range(KD):
            v.wait_ge(fT_full, k + 1)
            V_.scalar_tensor_tensor(x2[:, k, :], bk(k % 2), mods[:, 40 + k, 0:1], H[:, k, :], ALU.mult,
                                    ALU.add).then_inc(x2_ready, 1)
        v.wait_ge(std3, 1)
        link(V_.reciprocal(rs2[:, :], rs2[:, :]))
        for k in range(KD):
            if k == 0:
                v.wait_ge(sq3_ready, KD)
            V_.scalar_tensor_tensor(x2[:, k, :], x2[:, k, :], QC[:, Q_GF + k:Q_GF + k + 1], rs2[:, :], ALU.mult,
                                    ALU.mult).then_inc(out_ready, 1)

    @block.gpsimd
    def _(g_):
        t = Tally(g_)
        G_ = nc.gpsimd

        def hb(ap, n):
            return ap.unsqueeze(2).to_broadcast([P, ap.shape[1], n])

        seg_i = 0
        for s in steps:
            k0 = s[0]
            t.settle()
            if k0 == "st":
                d, k = s[1:]
                c = st_chunk[d][k]
                if s == ("st", 0, 0):
                    g_.wait_ge(wdd_ready, 1)
                    job_read(g_, ("z", 3))
                else:
                    job_full(g_, st_prev[s])
                job_read(g_, ("xtr", c))
                G_.tensor_tensor(xdd[:, :].rearrange("p (h n) -> p h n", h=8),
                                 xs[:, c, :].rearrange("p (h n) -> p h n", h=8),
                                 hb(wdd[:, c, d * 8:d * 8 + 8], HD), ALU.mult).then_inc(*t(xdd_ready))
            elif k0 == "seg":
                c, g, d = s[1:]
                if (c, g) == (0, 0):
                    job_full(g_, ("F", 3))
                    g_.wait_ge(rope_ready, 5)
                else:
                    job_full(g_, ("seg", (2 * c + g - 1) // 2, (2 * c + g - 1) % 2, d))
                m = C_LE if d == 0 else C_GE
                G_.tensor_tensor(Am[:, d, :].rearrange("p (h n) -> p h n", h=4),
                                 CT[:, m:m + P].unsqueeze(1).to_broadcast([P, 4, P]),
                                 hb(dta[:, c, d * 8 + g * 4:d * 8 + g * 4 + 4], P), ALU.mult).then_inc(*t(am_ready))
                if g == 0:
                    if c:
                        job_full(g_, ("y", c - 1, 1))
                    G_.tensor_tensor(xd[:, d, :].rearrange("p (h n) -> p h n", h=8),
                                     xs[:, c, :].rearrange("p (h n) -> p h n", h=8),
                                     hb(dtv[:, c, d * 8:d * 8 + 8], HD), ALU.mult).then_inc(*t(xd_ready))
        g_.wait_ge(merge_done, 32)
        for j in range(2):
            g_.sem_inc(y_left, 1)
            G_.memset(xr[:, j, :], 0.0).then_inc(*t(xr_zero))
        t.settle()
        g_.wait_ge(slot_ready, 1)
        g_.wait_ge(h2_out, 16 * NCH)

        for j in range(2):
            G_.tensor_copy(idx[:, j:j + 1], tabt[:, j:j + 1]).then_inc(idx_ready, 1)
            g_.wait_ge(idx_ready, j + 1)
            G_.indirect_dma_start(out=xr[:, j, :], out_offset=None, in_=h2d,
                                  in_offset=bass.IndirectOffsetOnAxis(ap=idx[:, j:j + 1], axis=0),
                                  bounds_check=S - 1, oob_is_err=False).then_inc(xr_in[j], 16)
        g_.wait_ge(route_done, 2)
        n = g_.value_load(nbk[0:1, 0:1], min_val=1, max_val=MAXB)
        with g_.Fori(0, PAIRS) as i:
            for j in range(2):
                b = i * 2 + j
                with g_.If(b < n):
                    g_.wait_ge(xb_full, b + 1)
                    g_.wait_ge(xr_in[j], i * 16 + 16)
                    G_.tensor_copy(idx[:, j:j + 1], tabt[:, bass.ds(b + 2, 1)]).then_inc(idx_ready, 1)
                    g_.wait_ge(idx_ready, 2 * b + 3)
                    g_.sem_inc(idx_used, 1)
                    G_.indirect_dma_start(out=xr[:, j, :], out_offset=None, in_=h2d,
                                          in_offset=bass.IndirectOffsetOnAxis(ap=idx[:, j:j + 1], axis=0),
                                          bounds_check=S - 1, oob_is_err=False).then_inc(xr_in[j], 16)
                    G_.tensor_copy(idx[:, 2 + j:3 + j], tabd[:, bass.ds(b, 1)]).then_inc(idx_ready, 1)
                    g_.wait_ge(idx_ready, 2 * b + 4)
                    g_.wait_ge(ya_done, b + 2)
                    g_.wait_ge(yd_done, b + 2)
                    g_.sem_inc(idx_used, 1)
                    G_.indirect_dma_start(out=ybuf, in_=ysb[:, j, :], in_offset=None,
                                          out_offset=bass.IndirectOffsetOnAxis(ap=idx[:, 2 + j:3 + j], axis=0),
                                          bounds_check=2 * S - 1, oob_is_err=False).then_inc(y_out, 16)
                    g_.wait_ge(y_out, b * 16 + 16)
                    g_.sem_inc(y_left, 1)
        g_.sem_inc(all_out, 1)

    ctx.close()


def constants():
    p, f = np.arange(P)[:, None], np.arange(P)[None, :]
    perm = np.zeros((P, P))
    for m in range(P):
        if m % HD < HD // 2:
            perm[m + HD // 2, m] = -1.0
        else:
            perm[m - HD // 2, m] = 1.0
    same = p // HD == f // HD
    w = 2 * np.pi * ((p % HD) * (f % HD) % HD) / HD
    prev = np.where(f >= p, 0.0, NEG)
    nxt = np.where(f <= p, 0.0, NEG)
    z = np.zeros((P, P))
    pack = [np.eye(P), p <= f, p >= f, p < f, p > f, np.ones((P, P)), perm, same * np.cos(w), same * np.sin(w),
            z, z, prev, z, nxt, z, z]
    consts = np.concatenate([np.asarray(x, np.float32) for x in pack], axis=1)
    t = np.arange(S)
    ang = 2 * np.pi * (t[:, None] * t[None, :] % S) / S
    nrm = 1.0 / np.sqrt(S * HD)
    dft = np.stack([np.cos(ang) * nrm, -np.sin(ang) * nrm]).astype(np.float32)
    dft = np.ascontiguousarray(dft.reshape(2, NCH, P, S).transpose(2, 0, 1, 3))
    pairs = HD // 4
    inv = np.float32(10000.0) ** (-np.arange(pairs, dtype=np.float32) / np.float32(pairs))
    row, col = (t // 64).astype(np.float32), (t % 64).astype(np.float32)
    a = np.concatenate([row[:, None] * inv, col[:, None] * inv], axis=1).astype(np.float32).T
    a = a[np.arange(P) % 32]
    cossin = np.ascontiguousarray(np.stack([np.cos(a), np.sin(a)], axis=1).astype(np.float32))
    return consts, cossin, dft


def kernel(**inputs):
    import numpy as _np
    import concourse.bacc as _bacc
    from concourse import mybir as _mybir
    from concourse.bass_utils import run_bass_kernel_spmd as _run

    a = {k: _np.asarray(v) for k, v in inputs.items()}

    def chan(x, n):
        return x.reshape(n, P, -1).transpose(1, 0, 2)

    xT = chan(a["x"][0].T, KD)
    ctxT = chan(a["ctx"][0].T, KD)
    w_in = a["w_in"][0]
    cut = _np.cumsum([0, 512, 128, 128, 512, 768, 16, 512, 1536])
    q, k, v, z, xbc, dt, fu, su = [w_in[:, cut[i]:cut[i + 1]] for i in range(8)]
    q = q.reshape(D, 2, 4, HD).transpose(0, 2, 1, 3).reshape(D, 512)
    su = su.reshape(D, 3, 4, P)[:, [1, 2, 0]].transpose(0, 2, 1, 3).reshape(D, 1536)
    w_in8 = _np.concatenate([xbc[:, :512], xbc[:, 512:], k, v, fu, q, su, z], axis=1)

    def units(w):
        n = w.shape[1] // S
        return w.reshape(KD, P, n, S).transpose(2, 1, 0, 3).reshape(n, P, UNIT)

    ada = units(a["w_ada"][0])
    wg, wb = units(a["w_gate"][0]), a["w_branch"][0]
    parts = [ada[:4], _np.stack([units(w_in8), ada[4:]], axis=1).reshape(16, P, UNIT)]
    for i, n in enumerate(MIX_ORDER):
        b = wb[n]
        if n == 0:
            b = b.reshape(2, 4, HD, D).transpose(1, 0, 2, 3).reshape(512, D)
        parts += [wg[2 * n:2 * n + 1], chan(b, 4).reshape(1, P, UNIT), wg[2 * n + 1:2 * n + 2]]
    parts.append(units(a["w_o"][0]))
    stream = _np.concatenate(parts)

    def col(x):
        return x.reshape(-1, P).T

    consts, cossin, dft = constants()
    cv = _np.stack([a["c"][0], a["c_ctx"]], axis=1)
    cols = _np.concatenate([
        col(a["norm1_w"][0]), col(a["norm2_w"][0]), col(a["final_norm_w"]), col(a["b_ada"][0]), col(a["b_gate"][0]),
        col(a["ssm_conv_w"][0]), col(a["ssm_conv_b"][0]), col(a["sconv_w"][0]), col(a["ssm_norm_w"][0]),
        chan(cv, KD).reshape(P, 16), _np.full((P, 1), EPS, _np.float32), _np.full((P, 1), 4 * EPS, _np.float32),
        _np.zeros((P, 1), _np.float32), _np.arange(P, dtype=_np.float32)[:, None],
        2 * S + _np.arange(P, dtype=_np.float32)[:, None],
        _np.arange(P, dtype=_np.float32)[:, None] + P * _np.arange(8, dtype=_np.float32) - 2 * S], axis=1)
    rows = _np.concatenate([
        a["ssm_dt_bias"][0].reshape(-1), a["ssm_a_log"][0].reshape(-1), a["ssm_d"][0], a["attn_sink"][0],
        a["router_bias"], _np.arange(32, dtype=_np.float32), _np.arange(8, dtype=_np.float32),
        _np.arange(BLK, dtype=_np.float32)])
    rows = _np.broadcast_to(rows[None, :], (P, R_N))
    w2 = a["moe_w2"][0].reshape(NE, 4, P, D).transpose(0, 2, 1, 3).reshape(NE, P, UNIT)
    w1, w3 = [a[x][0].reshape(NE, KD, P, S).transpose(0, 2, 1, 3).reshape(NE, P, UNIT) for x in ("moe_w1", "moe_w3")]
    ins = {"xT": xT, "ctxT": ctxT, "stream": stream, "consts": consts, "cossin": cossin, "dft": dft, "cols": cols,
           "rows": rows, "wdt": chan(dt, KD), "wrt": chan(a["w_router"], KD), "w1": w1, "w3": w3, "w2": w2}
    ins = {"in_" + k: _np.ascontiguousarray(v) for k, v in ins.items()}

    nc = _bacc.Bacc("TRN2", target_bir_lowering=False, num_devices=1)
    aps = {k[3:]: nc.dram_tensor(k, list(v.shape), _mybir.dt.from_np(v.dtype), kind="ExternalInput").ap()
           for k, v in ins.items()}
    aps["ybuf"] = nc.dram_tensor("expert_rows", [2 * S, D], _mybir.dt.float32, kind="Internal").ap()
    aps["h2d"] = nc.dram_tensor("token_rows", [S, D], _mybir.dt.float32, kind="Internal").ap()
    aps["outT"] = nc.dram_tensor("outT", [P, KD, S], _mybir.dt.float32, kind="ExternalOutput").ap()
    build(nc, **aps)
    r = _run(nc, [ins], core_ids=[0])
    o = _np.asarray(r.results[0]["outT"])
    return _np.ascontiguousarray(o.transpose(1, 0, 2).reshape(D, S).T)[None]
```

```python
from contextlib import ExitStack

import numpy as np
import concourse.bass as bass
from concourse import mybir

F32 = mybir.dt.float32
FR = mybir.dt.float32r
I32 = mybir.dt.int32
U32 = mybir.dt.uint32
ALU = mybir.AluOpType
ACT = mybir.ActivationFunctionType
AX = mybir.AxisListType

P = 128
D, KD = 1024, 8
S, NCH = 512, 4
SC, NCC = 256, 2
EPS = 1e-6
NEG = -1.0e30
HD = 64
NE, NG, EPG = 32, 8, 4
BLK = 128
MAXB = 2 * S // BLK + NE - 1
UNIT = 4096
TILE = 1024
RING, HI_RING = 5, 3
PAIRS = (MAXB + 1) // 2
NTAB = 2 * PAIRS + 2

C_ID, C_LE, C_GE, C_LT, C_GT, C_ONE, C_PERM, C_BD, C_MASK = 0, 128, 256, 384, 512, 640, 768, 896, 1152
C_N = C_MASK + 7 * 128
Q_G1, Q_G2, Q_GF, Q_BADA, Q_BG, Q_CW, Q_CB, Q_SW, Q_SN, Q_C, Q_EPS, Q_EPS4, Q_ZERO, Q_IOTA, Q_DUMP, Q_DST = (
    0, 8, 16, 24, 72, 104, 122, 128, 140, 144, 160, 161, 162, 163, 164, 165)
Q_N = 173
R_DTB, R_ALOG, R_D, R_SINK, R_RB, R_IE, R_IG, R_IB = 0, 16, 32, 40, 48, 80, 112, 120
R_N = 248

MIX_ORDER = (3, 2, 0, 1)


def timeline():
    t = [("mr", 0), ("mr", 1), ("ssq",), ("mr", 2), ("ssqc",), ("mr", 3), ("mod", 0)]
    t += [("v",), ("dtr", 0), ("dtr", 1), ("vc",), ("dt",)]
    macc = 0

    def tile(*jobs):
        nonlocal t, macc
        t += [*jobs, ("macc", macc)]
        if macc > 4 and macc % 4 == 1:
            t += [("mod", macc // 4)]
        macc += 1

    for m in range(6):
        tile(("xbc", m), ("xbcc", m))
    tile(("k",), ("kc",))
    for m in range(4):
        tile(("fu", m), *([("rot", 0)] if m == 0 else []))
    t += [("dec",)]
    for m in range(4):
        tile(("q", m), *([("rot", m)] if m else []))
    for m in range(4):
        tile(("cg", m), *([("rot", 4)] if m == 0 else []))
        tile(("sx", m))
        tile(("bg", m))
    for i in range(4):
        tile(("zk", i))
    t += [("macc", 31)] + [("z", c) for c in range(NCH)]
    t += [("xtr", c) for c in (4, 5, 0, 1, 2, 3)] + [("btr", 0), ("btr", 1), ("mod", 8)]

    att_step = 0

    def attention():
        nonlocal att_step
        h, att_step = att_step, att_step + 1
        return ([("S", h)] * (h < 32) + [("T", h - 2)] * (2 <= h < 34) + [("O", h - 3)] * (3 <= h < 35))

    t += [("V", 0), ("V", 1), ("F", 0)] + attention() + [("V", 2), ("F", 1)] + attention()
    t += [("V", 3), ("F", 2)] + attention() + [("F", 3)] + attention()

    ssm = [("st", d, k) for k in range(5) for d in range(2)]
    for c in range(NCH):
        for g in range(2):
            ssm += [("G", c, g), ("seg", c, g, 0), ("seg", c, g, 1), ("yoff", c, g), ("y", c, g)]
    ssm += [("ynorm",)] + [None] * 3 + [("ytr", c) for c in range(NCH)]
    point = 0

    def side():
        nonlocal point
        point += 1
        if point % 2 == 1 and att_step < 35:
            return attention()
        if ssm and (point % 2 == 0 or point % 4 == 3 or len(ssm) < 5):
            return [x for x in [ssm.pop(0)] if x]
        return []

    for i, n in enumerate(MIX_ORDER):
        if i == 3:
            t += [x for x in ssm if x] + [("srow",)]
            ssm = []
        for d in range(8):
            t += [("gate", n, d)] + side() + side() + [("proj", n, d)] + side() + side()
    for d in range(8):
        t += [("wo", d)] + ([("sw",)] if d == 1 else []) + ([("rtk", d - 2)] if d > 1 else [])
    t += [("rtk", 6), ("rtk", 7), ("ssq2",), ("rt",), ("rtt",)] + [("h2tr", c) for c in range(NCH)] + [("cnt",), ("bexp",), ("tab",)]
    return t


def tile_of(s):
    k = s[0]
    if k in ("xbc", "xbcc"):
        return "xbc", s[1]
    if k in ("k", "kc", "v", "vc"):
        return (k[0],)
    if k in ("fu", "q", "cg", "sx", "bg", "zk", "gate", "wo", "macc"):
        return s
    if k == "proj":
        return "branch", s[1], s[2] // 2
    return None


def is_split(x):
    return x[0] not in ("v", "macc", "branch")


def tile_order():
    steps, order, first, last = timeline(), [], {}, {}
    for i, s in enumerate(steps):
        x = tile_of(s)
        if x is not None:
            if x not in last:
                order.append(x)
                first[x] = i
            last[x] = s
    cut = [x for x in order if is_split(x)]
    need = dict(first)
    for i, x in enumerate(cut):
        need[x] = first[cut[i - 2]] - 0.5 if i > 1 else 0
    soonest = len(steps)
    for x in reversed(order):
        if x[0] != "macc":
            soonest = need[x] = min(need[x], soonest)
    return sorted(order, key=lambda x: need[x]), last


ROT3 = {"xbc", "xbcc", "k", "kc", "dt", "v", "vc", "fu", "q", "rot", "cg", "sx", "bg", "wo", "dtr"}


def bank_plan(steps):
    used, plan, rot = {}, {}, 0
    for s in steps:
        k = s[0]
        if k in ROT3:
            b = rot % 3
            rot += 1
        elif k in ("gate", "proj", "O"):
            b = ("gate", "proj", "O").index(k)
        elif k in ("S", "srow"):
            b = 3
        elif k == "sw":
            b = 5
        elif k == "h2tr":
            b = 3 + s[1] % 2 * 2
        elif k in ("V", "T"):
            b = 5
        elif k in ("xtr", "btr", "F", "ytr"):
            b = 3 + s[1] % 2 * 4
        elif k in ("G", "y") and s[1] >= 2:
            b = 3
        elif k == "seg" and s[1] >= 2 and s[3]:
            b = 5
        elif k == "ssq2" or s == ("mod", 0):
            b = 0
        elif k in ("ssqc", "rtt"):
            b = 1
        elif k == "ssq":
            b = 3
        elif k in ("ynorm", "macc", "zk", "rtk"):
            continue
        elif k == "mr":
            b = 4 + s[1]
        elif k == "z":
            b = 3 + s[1]
        elif k == "rt":
            b = 7
        elif k == "cnt":
            b = 2
        elif k == "tab":
            b = 2
        else:
            b = 7
        used[b] = used.get(b, 0) + 1
        plan[s] = (b, used[b])
    return plan


def head(h):
    blk, g, j = h // 8, (h // 4) % 2, h % 4
    if blk == 0:
        return blk, g, j, [0, 1, 4, 5], 3 * P
    keys = [4, 5] + [c for c in (blk - 1, blk, blk + 1) if c < NCH]
    return blk, g, j, keys, 0


def hd_index(h):
    return h // 4 % 2 * 4 + h % 4


def chunk_cols(c):
    return c * P if c < NCH else S + 2 + (c - NCH) * P


class Tally:

    def __init__(self, eng):
        self.eng, self.count, self.last = eng, {}, None

    def __call__(self, sem, value=None):
        n = self.count.get(sem.name, 0) + 1 if value is None else value
        self.count[sem.name] = n
        self.last = (sem, n)
        return sem, 1

    def settle(self):
        if self.last:
            self.eng.wait_ge(*self.last)
            self.last = None


def build(nc, xT, ctxT, adaw, stream, consts, cossin, dft, cols, rows, wdt, wrt, w1, w3, w2, h2d, ybuf, outT):
    ctx = ExitStack()
    BASE = 16512

    def at(name, off, shape, dt=F32):
        return nc.alloc_sbuf_tensor_at(name, shape, dt, offset=BASE + off)

    ring = at("ring", 0, [P, RING, TILE])
    ring_lo = at("ring_lo", 0, [P, RING, TILE], FR)
    ring_hi = at("ring_hi", RING * TILE * 4, [P, HI_RING, TILE], FR)
    Hhi = at("Hhi", 32768, [P, KD, S], FR)
    Hlo = at("Hlo", 177344, [P, KD, S], FR)
    ada = [at(f"ada{i}", o, [P, UNIT]) for i, o in enumerate((32768, 73728, 90112, 177344))]
    modrow = at("modrow", 110784, [2, 4, S])
    dtrow = at("dtrow", 131072, [16, S + SC])
    ada_ring = at("ada_ring", 149696, [P, 2, TILE])
    Hx = at("Hx", 141504, [P, KD, S])
    hcx = at("hcx", 157888, [P, KD, SC])
    hchi = at("hchi", 118976, [P, KD, SC], FR)
    hclo = at("hclo", 49152, [P, KD, SC], FR)
    mhi = at("mhi", 110784, [P, KD, S], FR)
    mlo = at("mlo", 49152, [P, KD, S], FR)
    dftm = at("dftm", 49152, [P, 2, NCH, S])
    merged = at("merged", 49152, [P, KD, S])
    sq = at("sq", 49152, [P, 12, S])
    ropet = at("ropet", 65536, [P, 4, S])
    V = at("V", 65536, [P, 2, NCH * 256])
    E = at("E", 65536, [P, 2, S])
    Am = at("Am", 65536 + 4096, [P, 2, S])
    pads = at("pads", 73728, [P, 2, 772])
    acc = at("acc", 73728 + 6176, [P, 2, 772])
    th = at("th", 73728 + 12352, [P, 2, 772])
    sc = at("sc", 73728, [P, 3, 640])
    PT = at("PT", 73728 + 7680, [P, 640])
    gth = at("gth", 73728 + 10240, [P, S])
    xdd = at("xdd", 73728 + 12288, [P, S])
    ytmp = at("ytmp", 73728 + 14336, [P, 3, 256])
    amx = at("amx", 73728 + 17408, [P, 32, 8])
    xbcT = at("xbcT", 92288, [P, 6, 770])
    prevS = at("prevS", 92288, [P, 2, NCH, 256])
    tmpS = at("tmpS", 92288 + 8192, [P, 2, 256])
    Gm = at("Gm", 92288 + 10240, [P, 2, P])
    uT = at("uT", 110784, [P, NCH, S])
    attT = at("attT", 118976, [P, 4, S])
    qT = at("qT", 127168, [P, 4, S])
    dts = at("dts", 127168, [P, 8, 96])
    ssmT = at("ssmT", 127168, [P, 4, S])
    kT = at("kT", 135360, [P, S])
    kcT = at("kcT", 137408, [P, SC])
    vt = at("vt", 138432, [P, 6, P])
    scT = at("scT", 141504, [P, 4, S])
    zs = at("zs", 149696, [P, NCH, S])
    xs = at("xs", 157888, [P, 6, S])
    btm = at("btm", 157888 + 12288, [P, 6, P])
    cs = at("cs", 173248, [P, 2, S])
    xd = at("xd", 173248, [P, 2, S])
    H = at("H", 177344, [P, KD, S])
    CT = at("CT", 193728, [P, C_N])
    o = 193728 + C_N * 4

    def up(n):
        return (n + 31) // 32 * 32

    QC = at("QC", o, [P, Q_N]); o += up(Q_N * 4)
    RW = at("RW", o, [P, R_N]); o += up(R_N * 4)
    WDT = at("WDT", o, [P, KD, 16]); o += up(512)
    rsx = at("rsx", o, [P, S]); macc = [at("macc0", o, [P, S]), at("macc1", 170176, [P, S])]; mtmp = at("mtmp", o, [P, S]); o += up(2048)
    rsc = at("rsc", o, [P, SC]); o += up(1024)
    mods = at("mods", o, [P, 48, 2]); o += up(384)
    A1 = at("A1", o, [P, KD, 2]); o += up(64)
    half = at("half", o, [P, 56]); o += up(224)
    sil = at("sil", o, [P, 16]); o += up(64)
    dtv = at("dtv", o, [P, 6, 16]); o += up(384)
    dta = at("dta", o, [P, 6, 16]); o += up(384)
    ea = at("ea", o, [P, 16]); o += up(64)
    dec = at("dec", o, [P, 6, 48]); o += up(1152)
    wdd = at("wdd", o, [P, 6, 16]); o += up(384)
    cds = at("cds", o, [P, 6, 2, 4]); o += up(192)
    sqw = at("sqw", o, [P, 1]); o += 32
    yst = at("yst", o, [P, 12]); o += up(64)
    assert o <= 229368 - BASE, o

    ering = at("ering", 0, [P, 2, 3, UNIT])
    ering_lo = at("ering_lo", 0, [P, 2, 3, UNIT], FR)
    ehi = at("ehi", 98304, [P, 3, UNIT // 2], FR)
    sqs = at("sqs", 32768, [P, KD, S])
    hA = at("hA", 81920, [P, KD, S])
    dg = at("dg", 73728, [P, KD, P])
    srow = at("srow", 77824, [P, D])
    h2t = at("h2t", 114688, [P, NCH, D])
    m0 = 131072
    WR = at("WR", m0, [P, KD, NE]); m0 += 1024
    swk = at("swk", m0, [P, KD, NE]); g16 = at("g16", m0, [P, 4, NCH, 16]); m0 += 1024
    swv = at("swv", m0, [P, NE]); m0 += 128
    rst = at("rst", m0, [P, 2, NCH]); m0 += 32
    lg = at("lg", m0, [P, NCH, NE]); m0 += 512
    sel = at("sel", m0, [P, NCH, NE]); m0 += 512
    selm = at("selm", m0, [P, NCH, NE]); m0 += 512
    oh = at("oh", m0, [P, 2, NCH, NE]); m0 += 1024
    asg = at("asg", m0, [P, NCH, NE]); m0 += 512
    w32 = at("w32", m0, [P, NCH, NE]); m0 += 512
    w32b = at("w32b", m0, [P, NCH, NE]); m0 += 512
    g8 = at("g8", m0, [P, 6, NCH, 8]); m0 += 768
    sml = at("sml", m0, [P, 16, NCH]); m0 += 256
    cnt = at("cnt", m0, [P, 4, NE]); m0 += 512
    slotf = at("slotf", m0, [P, 2, NCH]); m0 += 32
    wts = at("wts", m0, [P, 2, NCH]); m0 += 32
    bex = at("bex", m0, [P, NE]); m0 += 128
    bec = at("bec", m0, [P, 2]); m0 += 32
    brow = at("brow", m0, [1, P], I32); m0 += 512
    nbk = at("nbk", m0, [1, 1], I32); m0 += 32
    bpf = at("bpf", m0, [P, 4, 8]); m0 += 128
    bpi = at("bpi", m0, [P, 2, 8], I32); m0 += 64
    tabd = at("tabd", m0, [P, NTAB], I32); m0 += up(NTAB * 4)
    tabt = at("tabt", m0, [P, NTAB], I32); m0 += up(NTAB * 4)
    idx = at("idx", m0, [P, 4], U32); m0 += 32
    lgT = at("lgT", m0, [NE, S])
    x_hi = at("x_hi", m0, [P, 2, KD * BLK], FR); m0 += 8192
    x_lo = at("x_lo", m0, [P, 2, KD * BLK], FR); m0 += 8192
    onep = at("onep", m0, [P, 8, BLK]); oneb = at("oneb", m0 + 4096, [P, 8, NTAB])
    sg = at("sg", m0, [BLK, S]); m0 += 2048
    a1 = at("a1", m0, [BLK, S]); m0 += 2048
    act_ = at("act_", m0, [BLK, S]); m0 += 2048
    act_hi = at("act_hi", m0, [P, 4 * BLK], FR); m0 += 2048
    act_lo = at("act_lo", m0, [P, 4 * BLK], FR); m0 += 2048
    xr = at("xr", m0, [BLK, 2, D]); m0 += 8192
    ysb = at("ysb", 122880, [BLK, 2, D])
    assert m0 <= 175296, m0
    rs2 = at("rs2", 175296, [P, S])
    gat = at("gat", 0, [P, 2, NCH, D])
    fin = at("fin", 32768, [P, NCH, D])
    sq3 = at("sq3", 49152, [P, KD, S])
    x2 = at("x2", 98304, [P, KD, S])

    psum = ctx.enter_context(nc.psum_tensor("psum", [P, 8, 512], F32))

    def bk(b, n=1):
        return psum[:, b:b + n, :].rearrange("p b n -> p (b n)")

    steps = timeline()
    plan = bank_plan(steps)
    full = [ctx.enter_context(nc.semaphore(f"bank_full{i}")) for i in range(8)]
    empty = [ctx.enter_context(nc.semaphore(f"bank_read{i}")) for i in range(8)]

    def sem(name):
        return ctx.enter_context(nc.semaphore(name))

    x_in, c_in, const_in, cs_in, dft_in, small_in = map(sem, "x_in c_in const_in cs_in dft_in small_in".split())
    tile_in = [sem(f"tile_in{i}") for i in range(RING)]
    ada_tile = [sem(f"ada_tile{i}") for i in range(2)]
    ada_in = [sem(f"ada_in{i}") for i in range(4)]
    hi_ready, lo_ready, hhi_ready, hlo_ready, zk_done, mhi_ready, mlo_ready = map(
        sem, "hi_ready lo_ready hhi_ready hlo_ready zk_done mhi_ready mlo_ready".split())
    wdt_in, macc_ready, sum_ready = sem("wdt_in"), sem("macc_ready"), sem("sum_ready")
    x_again, wr_in = sem("x_again"), sem("wr_in")
    dve_c, act_c, pool_c = sem("dve_chain"), sem("act_chain"), sem("pool_chain")
    sq_ready, std_ready, silu_e, sil_ready, prep_ready = map(sem, "sq_ready std_ready silu_e sil_ready prep_ready".split())
    hm_ready, h_ready, padz = map(sem, "hm_ready h_ready padz".split())
    conv_done, tanh_done, xbc_ready, rope_ready = map(sem, "conv_done tanh_done xbc_ready rope_ready".split())
    dt_abs, dt_exp, dta_ready, ea_ready, wdd_ready, cds_ready = map(sem, "dt_abs dt_exp dta_ready ea_ready wdd_ready cds_ready".split())
    z_tanh, sc_ready = sem("z_tanh"), sem("sc_ready")
    smax_ready, exp_done, prob_ready = sem("smax_ready"), sem("exp_done"), sem("prob_ready")
    xdd_ready, xdd_used, state_ready, am_ready, am_used, xd_ready = map(sem, "xdd_ready xdd_used state_ready am_ready am_used xd_ready".split())
    decay_done, m_ready, gm_ready, y_done, ysq_done, ystd, ynorm_done = map(sem, "decay_done m_ready gm_ready y_done ysq_done ystd ynorm_done".split())
    gate_done, merge_done = sem("gate_done"), sem("merge_done")
    xb_full, xhi_ready, xlo_ready, half_done, at_full, ahi_ready, alo_ready = map(
        sem, "xb_full xhi_ready xlo_ready half_done at_full ahi_ready alo_ready".split())
    ehi_ready, elo_ready, gathers_out = map(sem, "ehi_ready elo_ready gathers_out".split())
    act_ready, y_read, sig_ready, a1_done, xr_zero, idx_ready, idx_used, y_left = map(sem, "act_ready y_read sig_ready a1_done xr_zero idx_ready idx_used y_left".split())
    w_in = [[sem(f"w_in{j}_{k}") for k in range(3)] for j in range(2)]
    y_out, gat_in, h2_out, tab_ready = sem("y_out"), [sem(f"gat_in{c}") for c in range(NCH)], sem("h2_out"), sem("tab_ready")
    xr_in = [sem(f"xr_in{j}") for j in range(2)]
    fin_ready, fT_full, x2_ready, sq3_ready, ssq3_full, std3, out_ready, out_done, lg_ready, slot_ready = map(
        sem, "fin_ready fT_full x2_ready sq3_ready ssq3_full std3 out_ready out_done lg_ready slot_ready".split())
    sq2_ready, ha_ready, sum2_ready, half_ready = map(sem, "sq2_ready ha_ready sum2_ready half_ready".split())
    dg_ready, srow_ready, swk_ready, rst_ready = map(sem, "dg_ready srow_ready swk_ready rst_ready".split())
    rexp, rt_ready, asg_ready, bex_ready, route_done, brow_done, h2t_done = map(sem, "rexp rt_ready asg_ready bex_ready route_done brow_done h2t_done".split())

    order, last_use = tile_order()
    raw_index = {}
    for x in order:
        same = sum((y[0] == "macc") == (x[0] == "macc") for y in raw_index)
        raw_index[x] = same
    split_tiles = [x for x in order if is_split(x)]
    split_index = {x: i for i, x in enumerate(split_tiles)}
    split_at = {}
    for s_ in timeline():
        x_ = tile_of(s_)
        if x_ in split_index and x_ not in [tile_of(q_) for q_ in split_at]:
            if split_index[x_] + 2 < len(split_tiles):
                split_at[s_] = split_index[x_] + 2

    def place(x):
        return ada_ring[:, raw_index[x] % 2, :] if x[0] == "macc" else ring[:, raw_index[x] % RING, :]

    def hi_place(x):
        return ring_hi[:, split_index[x] % HI_RING, :]

    def lo_place(x):
        return ring_lo[:, raw_index[x] % RING, :]

    def arrived(eng, x):
        n = 2 if x[0] == "macc" else RING
        i = raw_index[x]
        eng.wait_ge((ada_tile if x[0] == "macc" else tile_in)[i % n], 16 * (i // n + 1))

    def released(eng, x):
        s = last_use[x]
        if s[0] == "macc":
            eng.wait_ge(macc_ready, s[1] + 1)
        elif s[0] == "zk" and s[1] < 3:
            eng.wait_ge(zk_done, s[1] + 1)
        else:
            job_full(eng, ("z", 3) if s[0] == "zk" else s)

    def job_full(eng, s):
        b, n = plan[s]
        eng.wait_ge(full[b], n)

    def job_read(eng, s):
        b, n = plan[s]
        eng.wait_ge(empty[b], n)

    def claim(eng, s):
        b, n = plan[s]
        if n > 1:
            eng.wait_ge(empty[b], n - 1)
        return b

    st_chunk = ([4, 5, 0, 1, 2, 3], [5, 4, 3, 2, 1, 0])
    st_steps = [s for s in steps if s[0] == "st"]
    st_index = {s: i for i, s in enumerate(st_steps)}
    st_prev = {s: st_steps[i - 1] for i, s in enumerate(st_steps) if i}

    block = ctx.enter_context(nc.Block())

    @block.sync
    def _(sp):
        sp.dma_start(QC[:, :], cols).then_inc(small_in, 16)
        sp.dma_start(RW[:, :], rows).then_inc(small_in, 16)
        sp.dma_start(ada[0][:, :], adaw[0]).then_inc(ada_in[0], 16)
        sp.dma_start(ada[1][:, :], adaw[1]).then_inc(ada_in[1], 16)
        sp.dma_start(Hx[:, :, :], xT).then_inc(x_in, 16)
        sp.dma_start(CT[:, :], consts).then_inc(const_in, 16)
        sp.dma_start(ada[2][:, :], adaw[2]).then_inc(ada_in[2], 16)
        sp.dma_start(hcx[:, :, :], ctxT).then_inc(c_in, 16)
        sp.dma_start(ada[3][:, :], adaw[3]).then_inc(ada_in[3], 16)
        sp.dma_start(WDT[:, :, :], wdt).then_inc(wdt_in, 16)
        rings = {True: [], False: []}
        for i, x in enumerate(order):
            ada_side = x[0] == "macc"
            before, n = rings[ada_side], 2 if ada_side else RING
            if len(before) >= n:
                released(sp, before[-n])
            elif ada_side:
                sp.wait_ge(hlo_ready, KD)
                job_full(sp, ("dtr", 0))
            before.append(x)
            j = raw_index[x] % n
            sp.dma_start(place(x), stream[i]).then_inc((ada_tile if ada_side else tile_in)[j], 16)
            if x == ("wo", 2):
                job_full(sp, ("gate", MIX_ORDER[-1], 7))
                job_full(sp, ("proj", MIX_ORDER[-1], 7))
                sp.dma_start(WR[:, :, :], wrt).then_inc(wr_in, 16)
                sp.dma_start(H[:, :, :], xT).then_inc(x_again, 16)
            if x == ("xbc", 0):
                sp.dma_start(cs[:, :, :], cossin).then_inc(cs_in, 16)
            if x == ("fu", 2):
                job_full(sp, ("kc",))
                sp.dma_start(dftm[:, :, :, :], dft).then_inc(dft_in, 16)

        for c in range(NCH):
            sp.wait_ge(h2t_done, c + 1)
            sp.dma_start(h2d[c * P:(c + 1) * P, :], h2t[:, c, :]).then_inc(h2_out, 16)

        job_full(sp, ("bexp",))
        sp.wait_ge(route_done, 2)
        n = sp.value_load(nbk[0:1, 0:1], min_val=1, max_val=MAXB)
        with sp.Fori(0, PAIRS) as i:
            for j in range(2):
                b = i * 2 + j
                with sp.If(b < n):
                    e = sp.value_load(brow[0:1, bass.ds(b, 1)], min_val=0, max_val=NE - 1)
                    for k, w in enumerate((w1, w3, w2)):
                        sp.wait_ge(half_done, b * 6 + 2 * k + 2)
                        if k == 1:
                            sp.wait_ge(gathers_out, 1)
                        sp.dma_start(ering[:, j, k, :], w[bass.ds(e, 1), :, :].rearrange("a p n -> (a p) n")
                                     ).then_inc(w_in[j][k], 16)
        sp.wait_ge(y_left, n + 2)
        for c in range(NCH):
            sp.dma_start(gat[:, :, c, :], ybuf.rearrange("(k c p) n -> p k c n", k=2, p=P)[:, :, c, :]
                         ).then_inc(gat_in[c], 16)
        for k in range(KD):
            sp.wait_ge(out_ready, k + 1)
            sp.dma_start(outT[:, k, :], x2[:, k, :]).then_inc(out_done, 16)
        sp.wait_ge(out_done, 16 * KD)

    @block.tensor
    def _(pe):
        def mm(out, lhsT, rhs, start, stop):
            return nc.tensor.matmul(out, lhsT, rhs, start=start, stop=stop)

        ID = CT[:, C_ID:C_ID + P]

        def three(out, w_hi, w_lo, h_hi, h_lo, start, stop):
            mm(out, w_hi, h_hi, start, False)
            mm(out, w_hi, h_lo, False, False)
            return mm(out, w_lo, h_hi, False, stop)

        def to_columns(u):
            job_read(pe, ("mr", u))
            if u == 0:
                pe.wait_ge(const_in, 16)
            for j in range(4):
                o = (4 * u + j) * 2
                ins = mm(bk(0)[:, o:o + 2], modrow[:, u, j * P:j * P + P], CT[0:2, C_ID:C_ID + 2], True, True)
            return ins

        def split_there(x):
            pe.wait_ge(hi_ready, split_index[x] + 1)
            pe.wait_ge(lo_ready, split_index[x] + 1)

        def project(s, cols, x, ctx_side):
            b = claim(pe, s)
            hi, lo = hi_place(x), lo_place(x)
            h_hi, h_lo = (hchi, hclo) if ctx_side else (Hhi, Hlo)
            for k in range(KD):
                ins = three(bk(b)[:, 0:cols], hi[:, k * P:k * P + P], lo[:, k * P:k * P + P], h_hi[:, k, :], h_lo[:, k, :],
                            k == 0, k == KD - 1)
            return ins.then_inc(full[b], 1)

        for s in steps:
            k0 = s[0]
            if k0 in ("ssq", "ssqc"):
                if k0 == "ssq":
                    pe.wait_ge(const_in, 16)
                b = claim(pe, s)
                pe.wait_ge(sum_ready, 1 if k0 == "ssq" else 2)
                if k0 == "ssq":
                    ins = mm(bk(b), CT[:, C_ONE:C_ONE + P], sq[:, 0, :], True, True)
                else:
                    for i in range(2):
                        ins = mm(bk(b)[:, 0:SC], CT[:, C_ONE:C_ONE + P], sq[:, KD, i * SC:i * SC + SC], i == 0, i == 1)
                ins.then_inc(full[b], 1)
            elif k0 == "mod" and s[1]:
                b = claim(pe, s)
                pe.wait_ge(macc_ready, 4 * s[1])
                for j in range(4):
                    ins = mm(bk(b)[:, 2 * j:2 * j + 2], macc[s[1] % 2][:, j * P:j * P + P], CT[:, C_ONE:C_ONE + 2], True, True)
                ins.then_inc(full[b], 1)
            elif k0 == "mr":
                b = claim(pe, s)
                u = s[1]
                if u == 0:
                    pe.wait_ge(sil_ready, 1)
                if u == 3:
                    for q in range(3):
                        to_columns(q)
                pe.wait_ge(ada_in[u], 16)
                for k in range(KD):
                    ins = mm(bk(b)[0:2, :], sil[:, 2 * k:2 * k + 2], ada[u][:, k * S:k * S + S], k == 0, k == KD - 1)
                ins.then_inc(full[b], 1)
            elif k0 == "mod":
                to_columns(3).then_inc(full[0], 1)
            elif k0 == "dtr":
                b = claim(pe, s)
                src, n = (Hx, S) if s[1] == 0 else (hcx, SC)
                if s[1] == 0:
                    pe.wait_ge(wdt_in, 16)
                else:
                    pe.wait_ge(h_ready, 2 * KD)
                for k in range(KD):
                    ins = mm(bk(b)[0:16, 0:n], WDT[:, k, :], src[:, k, :], k == 0, k == KD - 1)
                ins.then_inc(full[b], 1)
            elif k0 in ("xbc", "xbcc", "k", "kc", "fu", "q", "cg", "sx", "bg"):
                ctx_side = k0 in ("xbcc", "kc")
                split_there(tile_of(s))
                if s == ("xbc", 0):
                    pe.wait_ge(hhi_ready, KD)
                    pe.wait_ge(hlo_ready, KD)
                if s == ("xbcc", 0):
                    pe.wait_ge(hhi_ready, KD + NCH)
                    pe.wait_ge(hlo_ready, KD + NCH)
                project(s, SC if ctx_side else S, tile_of(s), ctx_side)
            elif k0 in ("v", "vc"):
                b = claim(pe, s)
                arrived(pe, ("v",))
                pe.wait_ge(h_ready, KD if k0 == "v" else 2 * KD)
                for c in range(NCH if k0 == "v" else NCC):
                    for k in range(KD):
                        src = Hx if k0 == "v" else hcx
                        ins = mm(bk(b)[:, c * P:c * P + P], src[:, k, c * P:c * P + P],
                                 place(("v",))[:, k * P:k * P + P], k == 0, k == KD - 1)
                ins.then_inc(full[b], 1)
            elif k0 == "dt":
                b = claim(pe, s)
                job_read(pe, ("dtr", 0))
                job_read(pe, ("dtr", 1))
                for c in range(6):
                    ins = mm(bk(b)[:, c * 16:c * 16 + 16], dtrow[:, c * P:c * P + P], CT[0:16, C_ID:C_ID + 16], True, True)
                ins.then_inc(full[b], 1)
            elif k0 == "zk":
                split_there(s)
                hi, lo = hi_place(s), lo_place(s)
                for c in range(NCH):
                    b = claim(pe, ("z", c)) if s[1] == 0 else plan[("z", c)][0]
                    for kk in range(2):
                        k = 2 * s[1] + kk
                        ins = three(bk(b), Hhi[:, k, c * P:c * P + P], Hlo[:, k, c * P:c * P + P], hi[:, kk * S:kk * S + S],
                                    lo[:, kk * S:kk * S + S], k == 0, k == KD - 1)
                    if s[1] == 3:
                        ins.then_inc(full[b], 1)
                if s[1] < 3:
                    ins.then_inc(zk_done, 1)
            elif k0 == "rot":
                b = claim(pe, s)
                job_read(pe, ("k",) if s[1] == 0 else ("q", s[1] - 1))
                mm(bk(b), CT[:, C_PERM:C_PERM + P], ropet[:, s[1] % 2, :], True, True).then_inc(full[b], 1)
            elif k0 == "dec":
                b = claim(pe, s)
                pe.wait_ge(dta_ready, 1)
                for c in range(6):
                    o = c * 48
                    for col, (m, r0, r1) in zip((0, 8, 16, 24, 32), ((C_LE, 0, 8), (C_GE, 8, 16), (C_GT, 0, 8),
                                                                     (C_LT, 8, 16), (C_ONE, 0, 16))):
                        ins = mm(bk(b)[:, o + col:o + col + r1 - r0], CT[:, m:m + P], dta[:, c, r0:r1], True, True)
                ins.then_inc(full[b], 1)
            elif k0 == "xtr":
                b = claim(pe, s)
                pe.wait_ge(xbc_ready, 6)
                o = chunk_cols(s[1])
                for m in range(4):
                    ins = nc.tensor.transpose(bk(b)[:, m * P:m * P + P], xbcT[:, m, o:o + P], ID)
                ins.then_inc(full[b], 1)
            elif k0 == "btr":
                b = claim(pe, s)
                for i in range(3):
                    o = chunk_cols(3 * s[1] + i)
                    ins = nc.tensor.transpose(bk(b)[:, i * P:i * P + P], xbcT[:, 4, o:o + P], ID)
                ins.then_inc(full[b], 1)
            elif k0 == "V":
                b = claim(pe, s)
                if s[1] == 0:
                    job_read(pe, ("z", 3))
                ft = s[1]
                job_read(pe, ("fu", ft))
                for c in range(NCH):
                    ins = mm(bk(b, 2)[:, c * 256:c * 256 + 256], uT[:, ft, c * P:c * P + P],
                             CT[:, C_BD:C_BD + 256], True, True)
                ins.then_inc(full[b], 1)
            elif k0 == "F":
                b = claim(pe, s)
                ft = s[1]
                job_read(pe, ("V", ft))
                pe.wait_ge(dft_in, 16)
                for i in range(8):
                    c, part = i // 2, i % 2
                    ins = mm(bk(b), V[:, ft % 2, c * 256 + part * P:c * 256 + part * P + P],
                             dftm[:, part, c, :], i == 0, i == 7)
                ins.then_inc(full[b], 1)
            elif k0 == "st":
                d, k = s[1:]
                b = claim(pe, s)
                pe.wait_ge(xdd_ready, st_index[s] + 1)
                if s == ("st", 0, 0):
                    job_read(pe, ("btr", 1))
                c = st_chunk[d][k]
                for g in range(2):
                    ins = mm(bk(b)[g * 64:g * 64 + 64, 0:256], btm[:, c, g * 64:g * 64 + 64],
                             xdd[:, g * 256:g * 256 + 256], True, True)
                ins.then_inc(full[b], 1)
            elif k0 == "G":
                c, g = s[1:]
                b = claim(pe, s)
                o = c * P
                mm(bk(b)[:, 0:P], xbcT[g * 64:g * 64 + 64, 4, o:o + P], xbcT[g * 64:g * 64 + 64, 5, o:o + P],
                   True, True).then_inc(full[b], 1)
            elif k0 == "seg":
                c, g, d = s[1:]
                b = claim(pe, s)
                pe.wait_ge(am_ready, 2 * (2 * c + g) + d + 1)
                m = C_GT if d == 0 else C_LT
                mm(bk(b), CT[:, m:m + P], Am[:, d, :], True, True).then_inc(full[b], 1)
            elif k0 == "yoff":
                c, g = s[1:]
                b = claim(pe, s)
                for d in range(2):
                    if (c, g) == (0, 0):
                        job_read(pe, ("st", d, 4))
                    ins = mm(bk(b)[:, d * 256:d * 256 + 256], xbcT[g * 64:g * 64 + 64, 5, c * P:c * P + P],
                             prevS[g * 64:g * 64 + 64, d, c, :], True, True)
                ins.then_inc(full[b], 1)
            elif k0 == "y":
                c, g = s[1:]
                b = claim(pe, s)
                pe.wait_ge(m_ready, 2 * (2 * c + g + 1))
                pe.wait_ge(xd_ready, 2 * (c + 1))
                for h in range(4):
                    for d in range(2):
                        ins = mm(bk(b)[:, h * HD:h * HD + HD], E[:, d, h * P:h * P + P],
                                 xd[:, d, (g * 4 + h) * HD:(g * 4 + h) * HD + HD], d == 0, d == 1)
                ins.then_inc(full[b], 1)
            elif k0 == "ytr":
                b = claim(pe, s)
                c = s[1]
                pe.wait_ge(ynorm_done, c + 1)
                for m in range(4):
                    ins = nc.tensor.transpose(bk(b)[:, m * P:m * P + P], zs[:, c, m * P:m * P + P], ID)
                ins.then_inc(full[b], 1)
            elif k0 == "S":
                blk, g, j, keys, _ = head(s[1])
                b = claim(pe, s)
                if s[1] == 0:
                    pe.wait_ge(rope_ready, 5)
                    job_read(pe, ("kc",))
                rows_ = slice(g * 64, g * 64 + 64)
                for i, c in enumerate(keys):
                    rhs = kT[rows_, c * P:c * P + P] if c < NCH else kcT[rows_, (c - NCH) * P:(c - NCH) * P + P]
                    ins = mm(bk(b, 2)[:, i * P:i * P + P], qT[rows_, j, blk * P:blk * P + P], rhs, True, True)
                ins.then_inc(full[b], 1)
            elif k0 == "T":
                h = s[1]
                b = claim(pe, s)
                pe.wait_ge(prob_ready, h + 1)
                for i in range(len(head(h)[3])):
                    ins = nc.tensor.transpose(bk(b, 2)[:, i * P:i * P + P], sc[:, h % 3, i * P:i * P + P], ID)
                ins.then_inc(full[b], 1)
            elif k0 == "O":
                h = s[1]
                blk, g, j, keys, _ = head(h)
                b = claim(pe, s)
                job_read(pe, ("T", h))
                if h == 0:
                    job_read(pe, ("vc",))
                for i, c in enumerate(keys):
                    ins = mm(bk(b)[g * 64:g * 64 + 64, 0:P], vt[:, c, g * 64:g * 64 + 64], PT[:, i * P:i * P + P],
                             i == 0, i == len(keys) - 1)
                ins.then_inc(full[b], 1)
            elif k0 == "gate":
                split_there(s)
                project(s, S, s, False)
            elif k0 == "proj":
                n, d = s[1:]
                b = claim(pe, s)
                if d == 0:
                    job_read(pe, {3: ("bg", 3), 2: ("F", 3), 0: ("O", 31), 1: ("ytr", 3)}[n])
                if d % 2 == 0:
                    arrived(pe, tile_of(s))
                src = {3: scT, 2: uT, 0: attT, 1: ssmT}[n]
                for k in range(4):
                    o = k * 256 + d % 2 * P
                    ins = mm(bk(b), place(tile_of(s))[:, o:o + P], src[:, k, :], k == 0, k == 3)
                ins.then_inc(full[b], 1)
            elif k0 == "wo":
                d = s[1]
                b = claim(pe, s)
                split_there(s)
                hi, lo = hi_place(s), lo_place(s)
                for k in range(KD):
                    if d == 0:
                        pe.wait_ge(mhi_ready, k + 1)
                        pe.wait_ge(mlo_ready, k + 1)
                    ins = three(bk(b), hi[:, k * P:k * P + P], lo[:, k * P:k * P + P], mhi[:, k, :], mlo[:, k, :],
                                k == 0, k == KD - 1)
                ins.then_inc(full[b], 1)
            elif k0 == "ssq2":
                b = claim(pe, s)
                pe.wait_ge(sum2_ready, 1)
                for c in range(NCH):
                    ins = mm(bk(b)[:, 2 * c:2 * c + 2], sqs[:, 0, c * P:c * P + P], CT[:, C_ONE:C_ONE + 2], True, True)
                ins.then_inc(full[b], 1)
            elif k0 == "srow":
                b = claim(pe, s)
                pe.wait_ge(dg_ready, 1)
                for k in range(KD):
                    ins = mm(bk(b, 2)[:, k * P:k * P + P], CT[:, C_ONE:C_ONE + P], dg[:, k, :], True, True)
                ins.then_inc(full[b], 1)
            elif k0 == "sw":
                b = claim(pe, s)
                pe.wait_ge(swk_ready, 1)
                for k in range(KD):
                    ins = mm(bk(b)[:, 0:NE], CT[:, C_ONE:C_ONE + P], swk[:, k, :], k == 0, k == KD - 1)
                ins.then_inc(full[b], 1)
            elif k0 == "rtk":
                k = s[1]
                b = claim(pe, ("rt",)) if k == 0 else plan[("rt",)][0]
                pe.wait_ge(wr_in, 16)
                pe.wait_ge(ha_ready, k + 1)
                ins = mm(bk(b)[0:NE, :], WR[:, k, :], hA[:, k, :], k == 0, k == KD - 1)
                if k == KD - 1:
                    ins.then_inc(full[b], 1)
            elif k0 == "h2tr":
                b = claim(pe, s)
                c = s[1]
                for k in range(KD):
                    ins = nc.tensor.transpose(bk(b, 2)[:, k * P:k * P + P], hA[:, k, c * P:c * P + P], ID)
                ins.then_inc(full[b], 1)
            elif k0 == "rtt":
                b = claim(pe, s)
                job_read(pe, ("rt",))
                for c in range(NCH):
                    ins = nc.tensor.transpose(bk(b)[:, c * NE:c * NE + NE], lgT[:, c * P:c * P + P], CT[0:NE, C_ID:C_ID + NE])
                ins.then_inc(full[b], 1)
            elif k0 == "cnt":
                b = claim(pe, s)
                pe.wait_ge(asg_ready, 1)
                ones = CT[:, C_ONE:C_ONE + P]
                for c in range(NCH):
                    mm(bk(b)[:, 0:NE], ones, asg[:, c, :], c == 0, c == NCH - 1)
                for c in range(NCH):
                    for c2 in range(c + 1):
                        ins = mm(bk(b)[:, NE + c * NE:NE + c * NE + NE],
                                 CT[:, C_LT:C_LT + P] if c2 == c else ones, asg[:, c2, :], c2 == 0, c2 == c)
                ins.then_inc(full[b], 1)
            elif k0 == "bexp":
                b = claim(pe, s)
                pe.wait_ge(bex_ready, 1)
                mm(bk(b)[0:1, 0:P], bec[:, 0:1], ID, True, True).then_inc(full[b], 1)
            elif k0 == "tab":
                b = claim(pe, s)
                pe.wait_ge(tab_ready, 1)
                for i in range(8):
                    ins = mm(bk(b)[:, 0:NTAB], onep[:, i, :], oneb[:, i, :], i == 0, i == 7)
                ins.then_inc(full[b], 1)

        pe.sem_inc(half_done, 12)
        XB, AT, HB, YB = bk(0, 2), bk(2), bk(3, 2), bk(5, 2)

        def to_channels(j):
            for d in range(KD):
                ins = nc.tensor.transpose(XB[:, d * BLK:d * BLK + BLK], xr[:, j, d * P:d * P + P], ID)
            return ins

        for c in range(NCH):
            job_read(pe, ("h2tr", c))
        pe.wait_ge(route_done, 2)
        pe.wait_ge(xr_in[0], 16)
        to_channels(0).then_inc(xb_full, 1)
        n = pe.value_load(nbk[0:1, 0:1], min_val=1, max_val=MAXB)
        with pe.Fori(0, PAIRS) as i:
            for j in range(2):
                b = i * 2 + j
                with pe.If(b < n):
                    pe.wait_ge(xlo_ready, b + 1)
                    pe.wait_ge(act_ready, b + 1)
                    for h in range(4):
                        pe.wait_ge(elo_ready, b * 6 + h + 1)
                        out = HB[:, h // 2 * S:h // 2 * S + S]
                        for kk in range(4):
                            k, o = h % 2 * 4 + kk, kk * S
                            x = slice(k * BLK, k * BLK + BLK)
                            wl = ering_lo[:, j, h // 2, h % 2 * 2048 + o:h % 2 * 2048 + o + S]
                            wh = ehi[:, h % 3, o:o + S]
                            ins = three(out, x_hi[:, j, x], x_lo[:, j, x], wh, wl, k == 0, k == KD - 1)
                        ins.then_inc(half_done, 1)
                    pe.wait_ge(xr_in[1 - j], i * 16 + 16 + 16 * j)
                    to_channels(1 - j).then_inc(xb_full, 1)
                    pe.wait_ge(act_ready, b + 2)
                    for f in range(4):
                        ins = nc.tensor.transpose(AT[:, f * BLK:f * BLK + BLK], act_[:, f * P:f * P + P], ID)
                    ins.then_inc(at_full, 1)
                    pe.wait_ge(alo_ready, b + 1)
                    pe.wait_ge(y_read, b + 1)
                    for h in (4, 5):
                        pe.wait_ge(elo_ready, b * 6 + h + 1)
                        for ff in range(2):
                            f = 2 * (h - 4) + ff
                            x = slice(f * BLK, f * BLK + BLK)
                            for hf in range(2):
                                o = ff * D + hf * S
                                ins = three(YB[:, hf * S:hf * S + S], act_hi[:, x], act_lo[:, x], ehi[:, h % 3, o:o + S],
                                            ering_lo[:, j, 2, h % 2 * 2048 + o:h % 2 * 2048 + o + S], f == 0, f == 3)
                        ins.then_inc(half_done, 1)
        for k in range(KD):
            b = k % 2
            if k == 0:
                pe.wait_ge(fin_ready, NCH)
            if k >= 2:
                pe.wait_ge(x2_ready, k - 1)
            for c in range(NCH):
                ins = nc.tensor.transpose(bk(b)[:, c * P:c * P + P], fin[:, c, k * P:k * P + P], ID)
            ins.then_inc(fT_full, 1)
        for k in range(KD):
            pe.wait_ge(sq3_ready, k + 1)
            ins = mm(bk(2), CT[:, C_ONE:C_ONE + P], sq3[:, k, :], k == 0, k == KD - 1)
        ins.then_inc(ssq3_full, 1)

    @block.scalar
    def _(act):
        t = Tally(act)
        def A(out, in_, f, **kw):
            return nc.scalar.activation(out, in_, f, **kw)

        act.wait_ge(small_in, 32)
        A(sil[:, :], QC[:, Q_C:Q_C + 16], ACT.Exp, scale=-1.0).then_inc(*t(silu_e))
        A(ea[:, :], RW[:, R_ALOG:R_ALOG + 16], ACT.Exp).then_inc(*t(ea_ready))
        act.wait_ge(x_in, 16)
        for k in range(KD):
            A(sq[:, k, :], Hx[:, k, :], ACT.Square).then_inc(*t(sq_ready))
        act.wait_ge(c_in, 16)
        for k in range(NCC * 2):
            A(sq[:, KD + k, :], hcx[:, 2 * k:2 * k + 2, :].rearrange("p a n -> p (a n)"), ACT.Square).then_inc(*t(sq_ready))

        def split_hi(i):
            x = split_tiles[i]
            arrived(act, x)
            if i >= HI_RING:
                released(act, split_tiles[i - HI_RING])
            A(hi_place(x), place(x), ACT.Copy).then_inc(*t(hi_ready))
            t.settle()

        for s in steps:
            k0 = s[0]
            t.settle()
            if s in split_at:
                split_hi(split_at[s])
            if k0 in ("ssq", "ssqc"):
                b, _n = plan[s]
                job_full(act, s)
                n, out = (S, rsx) if k0 == "ssq" else (SC, rsc)
                A(out[:, :], bk(b)[:, 0:n], ACT.Sqrt, scale=1.0 / D, bias=QC[:, Q_EPS:Q_EPS + 1]).then_inc(*t(empty[b], plan[s][1]))
            elif k0 == "mr":
                b, _n = plan[s]
                job_full(act, s)
                A(modrow[:, s[1], :], bk(b)[0:2, :], ACT.Copy).then_inc(*t(empty[b], plan[s][1]))
            elif k0 == "dtr":
                b, _n = plan[s]
                job_full(act, s)
                o, n = (0, S) if s[1] == 0 else (S, SC)
                A(dtrow[:, o:o + n], bk(b)[0:16, 0:n], ACT.Copy).then_inc(*t(empty[b], plan[s][1]))
            elif s == ("mod", 0):
                for w, dst in enumerate((Hx, hcx)):
                    for k in range(KD):
                        act.wait_ge(hm_ready, w * KD + k + 1)
                        A(dst[:, k, :], dst[:, k, :], ACT.Identity, bias=mods[:, k, w:w + 1]).then_inc(*t(h_ready))
                act.wait_ge(h_ready, 2 * KD)
                for k in range(KD):
                    A(Hhi[:, k, :], Hx[:, k, :], ACT.Copy).then_inc(*t(hhi_ready))
                split_hi(0)
                for k in range(NCH):
                    A(hchi[:, 2 * k:2 * k + 2, :], hcx[:, 2 * k:2 * k + 2, :], ACT.Copy).then_inc(*t(hhi_ready))
                split_hi(1)
            elif k0 in ("xbc", "xbcc"):
                m = s[1]
                b, _n = plan[s]
                if k0 == "xbc" and m >= 2:
                    act.wait_ge(conv_done, m - 1)
                if s == ("xbc", 0):
                    act.wait_ge(padz, 1)
                job_full(act, s)
                if k0 == "xbc":
                    A(pads[:, m % 2, 1:1 + S], bk(b), ACT.Copy).then_inc(*t(empty[b], plan[s][1]))
                else:
                    A(pads[:, m % 2, S + 3:S + 3 + SC], bk(b)[:, 0:SC], ACT.Copy).then_inc(*t(empty[b], plan[s][1]))
                    for mm_ in ([m - 1] if m else []) + ([m] if m == 5 else []):
                        act.wait_ge(conv_done, mm_ + 1)
                        if mm_ >= 2:
                            act.wait_ge(xbc_ready, mm_ - 1)
                        A(th[:, mm_ % 2, 0:770], acc[:, mm_ % 2, 0:770], ACT.Tanh).then_inc(*t(tanh_done))
            elif k0 in ("k", "q"):
                i = 0 if k0 == "k" else s[1] + 1
                b, _n = plan[s]
                job_full(act, s)
                if i >= 2:
                    act.wait_ge(rope_ready, i - 1)
                A(ropet[:, i % 2, :], bk(b), ACT.Copy).then_inc(*t(empty[b], plan[s][1]))
            elif k0 in ("kc", "v", "vc", "fu"):
                b, _n = plan[s]
                job_full(act, s)
                out = {"kc": lambda: kcT[:, :], "v": lambda: vt[:, 0:4, :].rearrange("p a n -> p (a n)"),
                       "vc": lambda: vt[:, 4:6, :].rearrange("p a n -> p (a n)"), "fu": lambda: uT[:, s[1], :]}[k0]()
                n = SC if k0 in ("kc", "vc") else S
                A(out, bk(b)[:, 0:n], ACT.Copy).then_inc(*t(empty[b], plan[s][1]))
            elif k0 == "dt":
                act.wait_ge(dt_abs, 1)
                A(dts[:, 2, :], dts[:, 1, :], ACT.Exp, scale=-1.0).then_inc(*t(dt_exp))
            elif k0 == "dec":
                b, _n = plan[s]
                job_full(act, s)
                A(dec[:, :, :].rearrange("p a n -> p (a n)"), bk(b)[:, 0:288], ACT.Exp).then_inc(*t(empty[b], plan[s][1]))
            elif k0 == "cg":
                m = s[1]
                b, _n = plan[s]
                job_full(act, s)
                if m == 0:
                    act.wait_ge(xbc_ready, 6)
                else:
                    job_read(act, ("sx", m - 1))
                A(th[:, 0, 0:S], bk(b), ACT.Copy).then_inc(*t(empty[b], plan[s][1]))
            elif k0 == "z":
                c = s[1]
                b, _n = plan[s]
                job_full(act, s)
                if c == 0:
                    job_read(act, ("sx", 3))
                else:
                    job_read(act, ("z", c - 1))
                A(th[:, 0, 0:S], bk(b), ACT.Tanh, scale=0.5).then_inc(*t(z_tanh))
            elif k0 in ("xtr", "btr"):
                b, _n = plan[s]
                job_full(act, s)
                if k0 == "xtr":
                    A(xs[:, s[1], :], bk(b), ACT.Copy).then_inc(*t(empty[b], plan[s][1]))
                else:
                    A(btm[:, 3 * s[1]:3 * s[1] + 3, :].rearrange("p a n -> p (a n)"), bk(b)[:, 0:384],
                      ACT.Copy).then_inc(*t(empty[b], plan[s][1]))
            elif k0 == "V":
                ft = s[1]
                b, _n = plan[s]
                job_full(act, s)
                if ft == 0:
                    act.wait_ge(rope_ready, 5)
                if ft >= 2:
                    job_full(act, ("F", ft - 2))
                A(V[:, ft % 2, :], bk(b, 2), ACT.Copy).then_inc(*t(empty[b], plan[s][1]))
            elif k0 == "S":
                h = s[1]
                W = len(head(h)[3]) * P
                act.wait_ge(smax_ready, h + 1)
                A(sc[:, h % 3, 0:W], sc[:, h % 3, 0:W], ACT.Exp, bias=amx[:, h, 1:2],
                  accum_out=amx[:, h, 2:3]).then_inc(*t(exp_done))
                A(amx[:, h, 3:4], RW[:, R_SINK + hd_index(h):R_SINK + hd_index(h) + 1], ACT.Exp,
                  bias=amx[:, h, 1:2]).then_inc(*t(exp_done))
            elif k0 == "T":
                h = s[1]
                b, _n = plan[s]
                W = len(head(h)[3]) * P
                job_full(act, s)
                if h == 0:
                    job_read(act, ("z", 3))
                else:
                    job_full(act, ("O", h - 1))
                A(PT[:, 0:W], bk(b, 2)[:, 0:W], ACT.Copy).then_inc(*t(empty[b], plan[s][1]))
            elif k0 == "seg":
                c, g, d = s[1:]
                b, _n = plan[s]
                job_full(act, s)
                if 2 * c + g == 0:
                    job_full(act, ("F", 3))
                else:
                    job_full(act, ("y", (2 * c + g - 1) // 2, (2 * c + g - 1) % 2))
                A(E[:, d, :], bk(b), ACT.Exp).then_inc(*t(empty[b], plan[s][1]))
            elif k0 == "ynorm":
                act.wait_ge(y_done, 8)
                for c in range(NCH):
                    t.settle()
                    A(E[:, 0, :], zs[:, c, :], ACT.Square, accum_out=yst[:, c:c + 1]).then_inc(*t(ysq_done))
                act.wait_ge(ysq_done, NCH)
                A(yst[:, 4:8], yst[:, 0:4], ACT.Sqrt, scale=1.0 / S, bias=QC[:, Q_EPS4:Q_EPS4 + 1]).then_inc(*t(ystd))
            elif k0 == "gate":
                n, d = s[1:]
                b, _n = plan[s]
                job_full(act, s)
                i = MIX_ORDER.index(n) * 8 + d
                if i:
                    job_read(act, ("proj", MIX_ORDER[(i - 1) // 8], (i - 1) % 8))
                else:
                    job_read(act, ("z", 3))
                    act.wait_ge(half_ready, 1)
                A(gth[:, :], bk(b), ACT.Tanh, scale=0.5, bias=half[:, n * 8 + d:n * 8 + d + 1]).then_inc(*t(empty[b], plan[s][1]))
            elif k0 == "proj" and s[1] == MIX_ORDER[-1]:
                k = s[2]
                act.wait_ge(merge_done, 3 * KD + k + 1)
                A(mhi[:, k, :], merged[:, k, :], ACT.Copy).then_inc(*t(mhi_ready))
            elif k0 == "wo":
                d = s[1]
                job_read(act, s)
                A(sqs[:, d, :], H[:, d, :], ACT.Square).then_inc(*t(sq2_ready))
                A(hA[:, d, :], H[:, d, :], ACT.Copy, scale=A1[:, d, 1:2]).then_inc(*t(ha_ready))
            elif k0 == "srow":
                b, _n = plan[s]
                job_full(act, s)
                A(srow[:, :], bk(b, 2), ACT.Copy).then_inc(*t(empty[b], plan[s][1]))
            elif k0 == "ssq2":
                b, _n = plan[s]
                job_full(act, s)
                A(rst[:, 0, :], bk(b)[:, 0:8].rearrange("p (c t) -> p c t", t=2)[:, :, 0], ACT.Sqrt, scale=1.0 / D,
                  bias=QC[:, Q_EPS:Q_EPS + 1]).then_inc(*t(empty[b], plan[s][1]))
            elif k0 == "h2tr":
                b, _n = plan[s]
                job_full(act, s)
                act.wait_ge(rst_ready, 1)
                A(h2t[:, s[1], :], bk(b, 2), ACT.Copy, scale=rst[:, 1, s[1]:s[1] + 1]).then_inc(*t(empty[b], plan[s][1]))
            elif k0 == "rt":
                b, _n = plan[s]
                job_full(act, s)
                A(lgT[:, :], bk(b)[0:NE, :], ACT.Copy).then_inc(*t(empty[b], plan[s][1]))
            elif k0 == "rtt":
                act.wait_ge(lg_ready, 1)
                A(w32[:, :, :], lg[:, :, :], ACT.Exp, scale=-1.0).then_inc(*t(rexp))

        act.sem_inc(y_read, 1)
        XB, AT, HB, YB = bk(0, 2), bk(2), bk(3), bk(5, 2)

        def half_hi(h, j, arrived_at, done):
            k = h // 2
            act.wait_ge(w_in[j][k], arrived_at)
            act.wait_ge(half_done, done)
            A(ehi[:, h % 3, :], ering[:, j, k, h % 2 * 2048:h % 2 * 2048 + 2048], ACT.Copy).then_inc(ehi_ready, 1)

        act.wait_ge(h2_out, 16 * NCH)
        act.wait_ge(xb_full, 1)
        A(x_hi[:, 0, :], XB, ACT.Copy).then_inc(xhi_ready, 1)
        for h in range(3):
            half_hi(h, 0, 16, 12)
        act.wait_ge(route_done, 2)
        n = act.value_load(nbk[0:1, 0:1], min_val=1, max_val=MAXB)
        with act.Fori(0, PAIRS) as i:
            for j in range(2):
                b = i * 2 + j
                with act.If(b < n):
                    half_hi(3, j, i * 16 + 16, b * 6 + 13)
                    act.wait_ge(half_done, b * 6 + 14)
                    act.wait_ge(a1_done, b + 1)
                    A(sg[:, :], HB, ACT.Sigmoid).then_inc(sig_ready, 1)
                    half_hi(4, j, i * 16 + 16, b * 6 + 14)
                    half_hi(5, j, i * 16 + 16, b * 6 + 15)
                    act.wait_ge(xb_full, b + 2)
                    A(x_hi[:, 1 - j, :], XB, ACT.Copy).then_inc(xhi_ready, 1)
                    act.wait_ge(at_full, b + 1)
                    A(act_hi[:, :], AT, ACT.Copy).then_inc(ahi_ready, 1)
                    with act.If(b + 1 < n):
                        half_hi(0, 1 - j, i * 16 + 16 + 16 * j, b * 6 + 16)
                        half_hi(1, 1 - j, i * 16 + 16 + 16 * j, b * 6 + 17)
                    act.wait_ge(half_done, b * 6 + 18)
                    act.wait_ge(y_left, b + 1)
                    A(ysb[:, j, :], YB, ACT.Copy).then_inc(y_read, 1)
                    with act.If(b + 1 < n):
                        half_hi(2, 1 - j, i * 16 + 16 + 16 * j, b * 6 + 18)
        for k in range(KD):
            act.wait_ge(x2_ready, k + 1)
            A(sq3[:, k, :], x2[:, k, :], ACT.Square).then_inc(sq3_ready, 1)
        act.wait_ge(ssq3_full, 1)
        A(rs2[:, :], bk(2), ACT.Sqrt, scale=1.0 / D, bias=QC[:, Q_EPS:Q_EPS + 1]).then_inc(std3, 1)

    @block.vector
    def _(v):
        t = Tally(v)
        V_ = nc.vector

        def link(ins):
            ins.then_inc(*t(dve_c))
            t.settle()

        def TT(out, a, b, op):
            return V_.tensor_tensor(out, a, b, op)

        v.wait_ge(small_in, 32)
        V_.tensor_scalar(half[:, :], QC[:, Q_BG:Q_BG + 56], 0.5, None, ALU.mult).then_inc(*t(half_ready))
        v.wait_ge(silu_e, 1)
        link(V_.tensor_scalar(sil[:, :], sil[:, :], 1.0, None, ALU.add))
        link(V_.reciprocal(sil[:, :], sil[:, :]))
        TT(sil[:, :], sil[:, :], QC[:, Q_C:Q_C + 16], ALU.mult).then_inc(*t(sil_ready))

        def merge_lo(k):
            v.wait_ge(mhi_ready, k + 1)
            TT(mlo[:, k, :], merged[:, k, :], mhi[:, k, :].bitcast(F32), ALU.subtract).then_inc(*t(mlo_ready))

        def split_lo(i):
            x = split_tiles[i]
            v.wait_ge(hi_ready, i + 1)
            TT(lo_place(x), place(x), hi_place(x).bitcast(F32), ALU.subtract).then_inc(*t(lo_ready))
            t.settle()

        def conv(x, w, a, n):
            link(V_.scalar_tensor_tensor(a, x[:, 1:1 + n], w[1], a, ALU.mult, ALU.add))
            return V_.scalar_tensor_tensor(a, x[:, 2:2 + n], w[2], a, ALU.mult, ALU.add)

        def xbc_finish(m):
            v.wait_ge(tanh_done, m + 1)
            V_.scalar_tensor_tensor(xbcT[:, m, :], th[:, m % 2, 0:770], 1.0, acc[:, m % 2, 0:770], ALU.add,
                                    ALU.mult).then_inc(*t(xbc_ready))

        def norm_probs(h):
            W = len(head(h)[3]) * P
            v.wait_ge(exp_done, 2 * h + 2)
            link(TT(amx[:, h, 4:5], amx[:, h, 2:3], amx[:, h, 3:4], ALU.add))
            link(V_.reciprocal(amx[:, h, 5:6], amx[:, h, 4:5]))
            V_.tensor_scalar(sc[:, h % 3, 0:W], sc[:, h % 3, 0:W], amx[:, h, 5:6], None, ALU.mult).then_inc(*t(prob_ready))

        def hb(ap, n):
            return ap.unsqueeze(2).to_broadcast([P, ap.shape[1], n])

        for first, last in ((0, KD), (KD, KD + NCH)):
            v.wait_ge(sq_ready, first + 1)
            for k in range(first + 1, last):
                v.wait_ge(sq_ready, k + 1)
                ins = TT(sq[:, first, :], sq[:, first, :], sq[:, k, :], ALU.add)
                if k < last - 1:
                    link(ins)
            ins.then_inc(*t(sum_ready))
            t.settle()

        for s in steps:
            k0 = s[0]
            t.settle()
            b = plan[s][0] if s in plan else None
            if s in split_at:
                split_lo(split_at[s])
            if k0 in ("ssq", "ssqc", "ssq2"):
                job_read(v, s)
                if k0 == "ssq2":
                    V_.reciprocal(rst[:, 1, :], rst[:, 0, :]).then_inc(*t(rst_ready))
                else:
                    out = {"ssq": rsx, "ssqc": rsc}[k0]
                    link(V_.reciprocal(out[:, :], out[:, :]))
            elif k0 == "srow":
                TT(dg[:, :, :], CT[:, C_ID:C_ID + P].unsqueeze(1).to_broadcast([P, KD, P]),
                   hb(mods[:, 24:32, 0], P), ALU.mult).then_inc(*t(dg_ready))
            elif k0 == "sw":
                v.wait_ge(wr_in, 16)
                TT(swk[:, :, :], WR[:, :, :], hb(mods[:, 24:32, 0], NE), ALU.mult).then_inc(*t(swk_ready))
                job_full(v, s)
                V_.tensor_copy(swv[:, :], bk(b)[:, 0:NE]).then_inc(*t(empty[b], plan[s][1]))
            elif s == ("mod", 0):
                job_full(v, s)
                TT(mods[:, 0:16, :], bk(b)[:, 0:32].rearrange("p (j w) -> p j w", w=2),
                   hb(QC[:, Q_BADA:Q_BADA + 16], 2), ALU.add).then_inc(*t(empty[b], plan[s][1]))
                job_read(v, s)
                link(V_.scalar_tensor_tensor(A1[:, :, :], mods[:, 8:16, :], 1.0, hb(QC[:, Q_G1:Q_G1 + 8], 2),
                                             ALU.add, ALU.mult))
                for k in range(KD):
                    V_.scalar_tensor_tensor(Hx[:, k, :], Hx[:, k, :], A1[:, k, 0:1], rsx[:, :], ALU.mult,
                                            ALU.mult).then_inc(*t(hm_ready))
                for k in range(KD):
                    V_.scalar_tensor_tensor(hcx[:, k, :], hcx[:, k, :], A1[:, k, 1:2], rsc[:, :], ALU.mult,
                                            ALU.mult).then_inc(*t(hm_ready))
                link(V_.memset(pads[:, :, :], 0.0))
                V_.memset(yst[:, :], 0.0).then_inc(*t(padz))
                for k in range(KD):
                    v.wait_ge(hhi_ready, k + 1)
                    TT(Hlo[:, k, :], Hx[:, k, :], Hhi[:, k, :].bitcast(F32), ALU.subtract).then_inc(*t(hlo_ready))
                split_lo(0)
                for k in range(NCH):
                    v.wait_ge(hhi_ready, KD + k + 1)
                    TT(hclo[:, 2 * k:2 * k + 2, :], hcx[:, 2 * k:2 * k + 2, :], hchi[:, 2 * k:2 * k + 2, :].bitcast(F32),
                       ALU.subtract).then_inc(*t(hlo_ready))
                split_lo(1)
            elif k0 == "macc":
                j = s[1]
                if j >= 8 and j % 4 == 0:
                    job_full(v, ("mod", j // 4 - 1))
                acc_ = macc[(j // 4 + 1) % 2][:, :]
                arrived(v, s)
                for kk in range(2):
                    k = 2 * (j % 4) + kk
                    w, sc_ = place(s)[:, kk * S:kk * S + S], sil[:, 2 * k:2 * k + 1]
                    if k == 0:
                        link(V_.tensor_scalar(acc_, w, sc_, None, ALU.mult))
                    elif kk == 0:
                        link(V_.scalar_tensor_tensor(acc_, w, sc_, acc_, ALU.mult, ALU.add))
                    else:
                        V_.scalar_tensor_tensor(acc_, w, sc_, acc_, ALU.mult, ALU.add).then_inc(*t(macc_ready))
            elif k0 == "mod":
                job_full(v, s)
                o = 16 + 4 * (s[1] - 1)
                TT(mods[:, o:o + 4, :], bk(b)[:, 0:8].rearrange("p (j w) -> p j w", w=2),
                   hb(QC[:, Q_BADA + o:Q_BADA + o + 4], 2), ALU.add).then_inc(*t(empty[b], plan[s][1]))
            elif k0 == "xbcc":
                m = s[1]
                job_read(v, ("xbc", m))
                job_read(v, s)
                w = [half[:, 32 + q * 6 + m:33 + q * 6 + m] for q in range(3)]
                x, a = pads[:, m % 2, :], acc[:, m % 2, 0:770]
                link(V_.tensor_scalar(a, x[:, 0:770], w[0], half[:, 50 + m:51 + m], ALU.mult, ALU.add))
                conv(x, w, a, 770).then_inc(*t(conv_done))
                if m:
                    xbc_finish(m - 1)
                if m == 5:
                    xbc_finish(5)
            elif k0 == "dt":
                job_full(v, s)
                T_ = [dts[:, i, :] for i in range(8)]
                x3 = dts[:, 0, :].rearrange("p (c n) -> p c n", n=16)
                TT(x3, bk(b)[:, 0:96].rearrange("p (c n) -> p c n", n=16),
                   RW[:, R_DTB:R_DTB + 16].unsqueeze(1).to_broadcast([P, 6, 16]), ALU.add).then_inc(*t(empty[b], plan[s][1]))
                job_read(v, s)
                V_.scalar_tensor_tensor(T_[1], T_[0], -1.0, T_[0], ALU.mult, ALU.max).then_inc(*t(dt_abs))
                v.wait_ge(dt_exp, 1)
                link(V_.tensor_scalar(T_[3], T_[2], 2.0, None, ALU.add))
                link(V_.reciprocal(T_[3], T_[3]))
                link(TT(T_[3], T_[2], T_[3], ALU.mult))
                link(TT(T_[4], T_[3], T_[3], ALU.mult))
                link(V_.tensor_scalar(T_[5], T_[4], 1.0 / 15, None, ALU.mult))
                for q in (13, 11, 9, 7, 5, 3):
                    link(V_.scalar_tensor_tensor(T_[5], T_[5], 1.0 / q, T_[4], ALU.add, ALU.mult))
                link(V_.scalar_tensor_tensor(T_[5], T_[5], 1.0, T_[3], ALU.add, ALU.mult))
                link(V_.tensor_scalar(T_[6], T_[0], 0.0, None, ALU.max))
                link(V_.scalar_tensor_tensor(dtv[:, :, :].rearrange("p c n -> p (c n)"), T_[5], 2.0, T_[6],
                                             ALU.mult, ALU.add))
                v.wait_ge(ea_ready, 1)
                V_.scalar_tensor_tensor(dta[:, :, :], dtv[:, :, :], -1.0,
                                        ea[:, :].unsqueeze(1).to_broadcast([P, 6, 16]), ALU.mult,
                                        ALU.mult).then_inc(*t(dta_ready))
            elif k0 == "dec":
                job_read(v, s)
                TT(wdd[:, :, :], dtv[:, :, :], dec[:, :, 16:32], ALU.mult).then_inc(*t(wdd_ready))
                for g in range(2):
                    r = slice(g * 64, g * 64 + 64)
                    for d in range(2):
                        V_.tensor_copy(cds[r, :, d, :], dec[r, :, 32 + d * 8 + g * 4:36 + d * 8 + g * 4]).then_inc(*t(cds_ready))
            elif k0 == "rot":
                i = s[1]
                job_full(v, s)
                v.wait_ge(cs_in, 16)
                link(TT(ropet[:, 2, :], ropet[:, i % 2, :], cs[:, 0, :], ALU.mult))
                TT(ropet[:, 3, :], bk(b), cs[:, 1, :], ALU.mult).then_inc(*t(empty[b], plan[s][1]))
                job_read(v, s)
                TT(kT[:, :] if i == 0 else qT[:, i - 1, :], ropet[:, 2, :], ropet[:, 3, :], ALU.add).then_inc(*t(rope_ready))
            elif k0 == "sx":
                m = s[1]
                job_read(v, ("cg", m))
                job_full(v, s)
                TT(pads[:, m % 2, 1:1 + S], bk(b), th[:, 0, 0:S], ALU.mult).then_inc(*t(empty[b], plan[s][1]))
                job_read(v, s)
                if m < 2:
                    link(V_.memset(pads[:, m % 2, 1 + S:2 + S], 0.0))
                w = [QC[:, Q_SW + q * 4 + m:Q_SW + q * 4 + m + 1] for q in range(3)]
                x, a = pads[:, m % 2, :], acc[:, m % 2, 0:S]
                link(V_.tensor_scalar(a, x[:, 0:S], w[0], None, ALU.mult))
                link(conv(x, w, a, S))
            elif k0 == "bg":
                m = s[1]
                job_full(v, s)
                TT(scT[:, m, :], bk(b), acc[:, m % 2, 0:S], ALU.mult).then_inc(*t(empty[b], plan[s][1]))
            elif k0 == "z":
                c = s[1]
                v.wait_ge(z_tanh, c + 1)
                V_.scalar_tensor_tensor(zs[:, c, :], th[:, 0, 0:S], 1.0, bk(b), ALU.add, ALU.mult).then_inc(*t(empty[b], plan[s][1]))
            elif k0 == "F":
                job_full(v, s)
                V_.tensor_copy(uT[:, s[1], :], bk(b)).then_inc(*t(empty[b], plan[s][1]))
            elif k0 == "S":
                h = s[1]
                keys, mo = head(h)[3:]
                W = len(keys) * P
                job_full(v, s)
                if h >= 3:
                    job_full(v, ("T", h - 3))
                V_.scalar_tensor_tensor(sc[:, h % 3, 0:W], bk(b, 2)[:, 0:W], HD ** -0.5,
                                        CT[:, C_MASK + mo:C_MASK + mo + W], ALU.mult, ALU.add).then_inc(*t(empty[b], plan[s][1]))
                job_read(v, s)
                link(V_.tensor_reduce(amx[:, h, 0:1], sc[:, h % 3, 0:W], AX.X, ALU.max))
                V_.tensor_scalar(amx[:, h, 1:2], amx[:, h, 0:1], RW[:, R_SINK + hd_index(h):R_SINK + hd_index(h) + 1],
                                 -1.0, ALU.max, ALU.mult).then_inc(*t(smax_ready))
                if h >= 1:
                    norm_probs(h - 1)
            elif k0 == "T":
                if s[1] == 30:
                    norm_probs(31)
            elif k0 == "O":
                h = s[1]
                blk, g, j = head(h)[:3]
                r = slice(g * 64, g * 64 + 64)
                job_full(v, s)
                V_.tensor_copy(attT[r, j, blk * P:blk * P + P], bk(b)[r, 0:P]).then_inc(*t(empty[b], plan[s][1]))
            elif k0 == "st":
                d, k = s[1:]
                c = st_chunk[d][k]
                if s == ("st", 0, 0):
                    job_full(v, ("xtr", 3))
                    v.wait_ge(cds_ready, 4)
                dst = tmpS[:, d, :] if k == 0 else prevS[:, d, st_chunk[d][k + 1], :]
                job_full(v, s)
                if k == 0:
                    V_.tensor_copy(dst, bk(b)[:, 0:256]).then_inc(*t(empty[b], plan[s][1]))
                else:
                    old = tmpS[:, d, :] if k == 1 else prevS[:, d, c, :]
                    job_read(v, ("st", d, k - 1))
                    link(TT(ytmp[:, 0, :].rearrange("p (h n) -> p h n", h=4), old.rearrange("p (h n) -> p h n", h=4),
                            hb(cds[:, c, d, :], HD), ALU.mult))
                    TT(dst, ytmp[:, 0, :], bk(b)[:, 0:256], ALU.add).then_inc(*t(empty[b], plan[s][1]))
            elif k0 == "G":
                job_full(v, s)
                if s[1:] == (0, 0):
                    link(TT(Gm[:, 0, :], bk(b)[:, 0:P], CT[:, C_LE:C_LE + P], ALU.mult))
                else:
                    TT(Gm[:, 0, :], bk(b)[:, 0:P], CT[:, C_LE:C_LE + P], ALU.mult).then_inc(*t(gm_ready))
                TT(Gm[:, 1, :], bk(b)[:, 0:P], CT[:, C_GE:C_GE + P], ALU.mult).then_inc(*t(empty[b], plan[s][1]))
            elif k0 == "seg":
                c, g, d = s[1:]
                job_read(v, ("G", c, g))
                job_read(v, s)
                e3 = E[:, d, :].rearrange("p (h n) -> p h n", h=4)
                TT(e3, e3, Gm[:, d, :].unsqueeze(1).to_broadcast([P, 4, P]), ALU.mult).then_inc(*t(m_ready))
            elif k0 == "yoff":
                c, g = s[1:]
                job_full(v, s)
                y4 = ytmp[:, 0:2, :].rearrange("p d (h n) -> p d h n", h=4)
                e4 = dec[:, c, 0:16].rearrange("p (d h) -> p d h", d=2)[:, :, g * 4:g * 4 + 4]
                TT(y4, bk(b).rearrange("p (d h n) -> p d h n", d=2, h=4),
                   e4.unsqueeze(3).to_broadcast([P, 2, 4, HD]), ALU.mult).then_inc(*t(empty[b], plan[s][1]))
            elif k0 == "y":
                c, g = s[1:]
                job_read(v, ("yoff", c, g))
                x3 = xs[:, c, g * 256:g * 256 + 256].rearrange("p (h n) -> p h n", h=4)
                link(TT(ytmp[:, 2, :].rearrange("p (h n) -> p h n", h=4), x3,
                        hb(RW[:, R_D + g * 4:R_D + g * 4 + 4], HD), ALU.mult))
                link(TT(ytmp[:, 0, :], ytmp[:, 0, :], ytmp[:, 1, :], ALU.add))
                link(TT(ytmp[:, 0, :], ytmp[:, 0, :], ytmp[:, 2, :], ALU.add))
                job_full(v, s)
                TT(ytmp[:, 0, :], ytmp[:, 0, :], bk(b)[:, 0:256], ALU.add).then_inc(*t(empty[b], plan[s][1]))
                job_read(v, s)
                zz = zs[:, c, g * 256:g * 256 + 256]
                TT(zz, zz, ytmp[:, 0, :], ALU.mult).then_inc(*t(y_done))
            elif k0 == "ynorm":
                v.wait_ge(ystd, 1)
                link(V_.reciprocal(yst[:, 8:12], yst[:, 4:8]))
                for c in range(NCH):
                    V_.tensor_scalar(zs[:, c, :], zs[:, c, :], yst[:, 8 + c:9 + c], None, ALU.mult).then_inc(*t(ynorm_done))
            elif k0 == "ytr":
                c = s[1]
                job_full(v, s)
                TT(ssmT[:, :, c * P:c * P + P], bk(b).rearrange("p (m n) -> p m n", m=4),
                   hb(QC[:, Q_SN:Q_SN + 4], P), ALU.mult).then_inc(*t(empty[b], plan[s][1]))
            elif k0 == "proj":
                n, d = s[1:]
                job_full(v, s)
                job_read(v, ("gate", n, d))
                first = n == MIX_ORDER[0]
                V_.scalar_tensor_tensor(merged[:, d, :] if first else mtmp[:, :], gth[:, :], 1.0, bk(b), ALU.add,
                                        ALU.mult).then_inc(*t(empty[b], plan[s][1]))
                if first:
                    V_.memset(yst[:, 0:1], 0.0).then_inc(*t(merge_done))
                else:
                    job_read(v, s)
                    TT(merged[:, d, :], merged[:, d, :], mtmp[:, :], ALU.add).then_inc(*t(merge_done))
                if n == MIX_ORDER[-1] and d:
                    merge_lo(d - 1)
            elif k0 == "wo":
                d = s[1]
                if d == 0:
                    link(V_.tensor_scalar(A1[:, :, 0], mods[:, 16:24, 0], 0.5, None, ALU.mult))
                    merge_lo(KD - 1)
                    link(V_.scalar_tensor_tensor(A1[:, :, 1], mods[:, 32:40, 0], 1.0, QC[:, Q_G2:Q_G2 + 8], ALU.add,
                                                 ALU.mult))
                    v.wait_ge(x_again, 16)
                job_full(v, s)
                V_.scalar_tensor_tensor(H[:, d, :], bk(b), A1[:, d, 0:1], H[:, d, :], ALU.mult,
                                        ALU.add).then_inc(*t(empty[b], plan[s][1]))
                for k in ([d - 1] if d > 1 else []) + ([d] if d == KD - 1 else []):
                    v.wait_ge(sq2_ready, k + 1)
                    ins = TT(sqs[:, 0, :], sqs[:, 0, :], sqs[:, k, :], ALU.add)
                    ins.then_inc(*t(sum2_ready if k == KD - 1 else dve_c))
                    t.settle()
            elif k0 == "rtt":
                job_full(v, s)
                link(TT(lg[:, :, :], bk(b)[:, 0:NCH * NE].rearrange("p (c n) -> p c n", n=NE), hb(rst[:, 1, :], NE),
                        ALU.mult))
                link(TT(lg[:, :, :], lg[:, :, :], swv[:, :].unsqueeze(1).to_broadcast([P, NCH, NE]), ALU.add))
                V_.tensor_scalar(lg[:, :, :].rearrange("p c n -> p (c n)"), lg[:, :, :].rearrange("p c n -> p (c n)"),
                                 -87.0, None, ALU.max).then_inc(*t(lg_ready))
                v.wait_ge(rexp, 1)
                link(V_.tensor_scalar(w32[:, :, :], w32[:, :, :], 1.0, None, ALU.add))
                link(V_.reciprocal(lg[:, :, :], w32[:, :, :]))
                link(TT(sel[:, :, :], lg[:, :, :], RW[:, R_RB:R_RB + NE].unsqueeze(1).to_broadcast([P, NCH, NE]), ALU.add))
                p2 = sel[:, :, :].rearrange("p c (h t) -> p c h t", t=2)
                link(TT(g16[:, 0], p2[:, :, :, 0], p2[:, :, :, 1], ALU.max))
                link(TT(g16[:, 1], p2[:, :, :, 0], p2[:, :, :, 1], ALU.min))
                hi = g16[:, 0].rearrange("p c (g t) -> p c g t", t=2)
                lo = g16[:, 1].rearrange("p c (g t) -> p c g t", t=2)
                link(TT(g8[:, 0], hi[:, :, :, 0], hi[:, :, :, 1], ALU.max))
                link(TT(g8[:, 1], hi[:, :, :, 0], hi[:, :, :, 1], ALU.min))
                link(TT(g8[:, 2], lo[:, :, :, 0], lo[:, :, :, 1], ALU.max))
                link(TT(g8[:, 1], g8[:, 1], g8[:, 2], ALU.max))
                link(TT(g8[:, 0], g8[:, 0], g8[:, 1], ALU.add))

                def first_max(out, x, iota, tmp, sm):
                    n = x.shape[2]
                    link(V_.tensor_reduce(sm, x, AX.X, ALU.max))
                    link(TT(tmp, x, sm.unsqueeze(2).to_broadcast([P, NCH, n]), ALU.is_equal))
                    link(V_.scalar_tensor_tensor(tmp, tmp, -1000.0, iota.unsqueeze(1).to_broadcast([P, NCH, n]),
                                                 ALU.mult, ALU.add))
                    link(V_.tensor_reduce(sm, tmp, AX.X, ALU.min))
                    link(TT(out, tmp, sm.unsqueeze(2).to_broadcast([P, NCH, n]), ALU.is_equal))

                first_max(g8[:, 3], g8[:, 0], RW[:, R_IG:R_IG + 8], g8[:, 1], sml[:, 0])
                link(V_.tensor_scalar(g8[:, 4], g8[:, 3], 1.0e30, -1.0e30, ALU.mult, ALU.add))
                s4 = sel[:, :, :].rearrange("p c (g t) -> p (c g) t", t=4)
                m4 = selm[:, :, :].rearrange("p c (g t) -> p (c g) t", t=4)

                def flat(x):
                    return x.rearrange("p c g -> p (c g)").unsqueeze(2).to_broadcast([P, NCH * 8, 4])

                link(TT(m4, s4, flat(g8[:, 3]), ALU.mult))
                link(TT(m4, m4, flat(g8[:, 4]), ALU.add))
                first_max(oh[:, 0], selm[:, :, :], RW[:, R_IE:R_IE + NE], w32[:, :, :], sml[:, 1])
                link(V_.scalar_tensor_tensor(selm[:, :, :], oh[:, 0], -1.0e31, selm[:, :, :], ALU.mult, ALU.add))
                first_max(oh[:, 1], selm[:, :, :], RW[:, R_IE:R_IE + NE], w32[:, :, :], sml[:, 1])
                TT(asg[:, :, :], oh[:, 0], oh[:, 1], ALU.add).then_inc(*t(asg_ready))
                for k in range(2):
                    link(TT(w32[:, :, :], oh[:, k], lg[:, :, :], ALU.mult))
                    link(V_.tensor_reduce(wts[:, k, :], w32[:, :, :], AX.X, ALU.add))
                link(TT(sml[:, 2], wts[:, 0, :], wts[:, 1, :], ALU.add))
                link(V_.reciprocal(sml[:, 2], sml[:, 2]))
                for k in range(2):
                    link(TT(wts[:, k, :], wts[:, k, :], sml[:, 2], ALU.mult))
            elif k0 == "cnt":
                job_full(v, s)
                C = cnt
                link(V_.tensor_copy(C[:, 0, :], bk(b)[:, 0:NE]))
                link(V_.tensor_scalar(C[:, 1, :], C[:, 0, :], 0.0, None, ALU.is_gt))
                for q in range(1, S // BLK):
                    link(V_.scalar_tensor_tensor(C[:, 1, :], C[:, 0, :], float(q * BLK), C[:, 1, :], ALU.is_gt, ALU.add))
                link(V_.memset(C[:, 3, :], 0.0))
                link(V_.tensor_tensor_scan(C[:, 2, :], C[:, 1, :], C[:, 3, :], 0.0, ALU.add, ALU.add))
                link(TT(C[:, 3, :], C[:, 2, :], C[:, 1, :], ALU.subtract))
                link(V_.tensor_scalar(bex[:, :], C[:, 2, :], QC[:, Q_IOTA:Q_IOTA + 1], None, ALU.is_le))
                link(V_.tensor_reduce(bec[:, 1:2], bex[:, :], AX.X, ALU.add))
                V_.tensor_scalar(bec[:, 0:1], bec[:, 1:2], float(NE - 1), None, ALU.min).then_inc(*t(bex_ready))
                rk = bk(b)[:, NE:NE + NCH * NE].rearrange("p (c n) -> p c n", n=NE)
                st64 = C[:, 3, :].unsqueeze(1).to_broadcast([P, NCH, NE])
                V_.scalar_tensor_tensor(w32b[:, :, :], st64, float(BLK), rk, ALU.mult, ALU.add).then_inc(*t(empty[b], plan[s][1]))
                job_read(v, s)
                for k in range(2):
                    link(TT(w32[:, :, :], oh[:, k], w32b[:, :, :], ALU.mult))
                    link(V_.tensor_reduce(slotf[:, k, :], w32[:, :, :], AX.X, ALU.add))
                sf = slotf[:, :, :].rearrange("p k c -> p (k c)")
                link(V_.tensor_copy(bpi[:, 0], sf))
                link(V_.tensor_scalar(bpi[:, 1], bpi[:, 0], BLK.bit_length() - 1, None, ALU.arith_shift_right))
                link(V_.tensor_copy(bpf[:, 1], bpi[:, 1]))
                link(V_.scalar_tensor_tensor(bpf[:, 0], bpf[:, 1], -float(BLK), sf, ALU.mult, ALU.add))
                link(TT(bpf[:, 2], QC[:, Q_DST:Q_DST + 8], bpf[:, 0], ALU.subtract))
                link(TT(onep[:, :, :], RW[:, R_IB:R_IB + BLK].unsqueeze(1).to_broadcast([P, 8, BLK]), hb(bpf[:, 0], BLK),
                        ALU.is_equal))
                link(TT(oneb[:, :, :], RW[:, R_IB:R_IB + NTAB].unsqueeze(1).to_broadcast([P, 8, NTAB]),
                        hb(bpf[:, 1], NTAB), ALU.is_equal))
                TT(oneb[:, :, :], oneb[:, :, :], hb(bpf[:, 2], NTAB), ALU.mult).then_inc(*t(tab_ready))
            elif k0 == "bexp":
                job_full(v, s)
                V_.tensor_copy(brow[0:1, :], bk(b)[0:1, 0:P]).then_inc(*t(route_done))
                V_.tensor_copy(nbk[0:1, 0:1], cnt[0:1, 2, NE - 1:NE]).then_inc(*t(route_done))
            elif k0 == "tab":
                job_full(v, s)
                link(V_.tensor_scalar(tabd[:, :], bk(b)[:, 0:NTAB], QC[:, Q_DUMP:Q_DUMP + 1], None, ALU.add))
                V_.tensor_scalar(tabt[:, :], tabd[:, :], 2 * S + S - 1, None, ALU.bitwise_and).then_inc(*t(slot_ready))

        v.sem_inc(act_ready, 1)
        v.sem_inc(a1_done, 1)
        XB, AT, HB = bk(0, 2), bk(2), bk(3, 2)

        def half_lo(h, j, count):
            k, o = h // 2, h % 2 * 2048
            v.wait_ge(ehi_ready, count)
            TT(ering_lo[:, j, k, o:o + 2048], ering[:, j, k, o:o + 2048], ehi[:, h % 3, :].bitcast(F32),
               ALU.subtract).then_inc(elo_ready, 1)

        v.wait_ge(xhi_ready, 1)
        TT(x_lo[:, 0, :], XB, x_hi[:, 0, :].bitcast(F32), ALU.subtract).then_inc(xlo_ready, 1)
        for h in range(3):
            half_lo(h, 0, h + 1)
        v.wait_ge(route_done, 2)
        n = v.value_load(nbk[0:1, 0:1], min_val=1, max_val=MAXB)
        with v.Fori(0, PAIRS) as i:
            for j in range(2):
                b = i * 2 + j
                with v.If(b < n):
                    half_lo(3, j, b * 6 + 4)
                    v.wait_ge(sig_ready, b + 1)
                    TT(a1[:, :], sg[:, :], HB[:, 0:S], ALU.mult).then_inc(a1_done, 1)
                    half_lo(4, j, b * 6 + 5)
                    v.wait_ge(a1_done, b + 2)
                    v.wait_ge(half_done, b * 6 + 16)
                    TT(act_[:, :], a1[:, :], HB[:, S:2 * S], ALU.mult).then_inc(act_ready, 1)
                    v.wait_ge(xhi_ready, b + 2)
                    TT(x_lo[:, 1 - j, :], XB, x_hi[:, 1 - j, :].bitcast(F32), ALU.subtract).then_inc(xlo_ready, 1)
                    v.wait_ge(ahi_ready, b + 1)
                    TT(act_lo[:, :], AT, act_hi[:, :].bitcast(F32), ALU.subtract).then_inc(alo_ready, 1)
                    half_lo(5, j, b * 6 + 6)
                    with v.If(b + 1 < n):
                        for h in range(3):
                            half_lo(h, 1 - j, b * 6 + 7 + h)
        for c in range(NCH):
            v.wait_ge(gat_in[c], 16)
            link(V_.tensor_scalar(fin[:, c, :], gat[:, 0, c, :], wts[:, 0, c:c + 1], None, ALU.mult))
            V_.scalar_tensor_tensor(fin[:, c, :], gat[:, 1, c, :], wts[:, 1, c:c + 1], fin[:, c, :], ALU.mult,
                                    ALU.add).then_inc(fin_ready, 1)
        for k in range(KD):
            v.wait_ge(fT_full, k + 1)
            V_.scalar_tensor_tensor(x2[:, k, :], bk(k % 2), mods[:, 40 + k, 0:1], H[:, k, :], ALU.mult,
                                    ALU.add).then_inc(x2_ready, 1)
        v.wait_ge(std3, 1)
        link(V_.reciprocal(rs2[:, :], rs2[:, :]))
        for k in range(KD):
            if k == 0:
                v.wait_ge(sq3_ready, KD)
            V_.scalar_tensor_tensor(x2[:, k, :], x2[:, k, :], QC[:, Q_GF + k:Q_GF + k + 1], rs2[:, :], ALU.mult,
                                    ALU.mult).then_inc(out_ready, 1)

    @block.gpsimd
    def _(g_):
        t = Tally(g_)
        G_ = nc.gpsimd

        def hb(ap, n):
            return ap.unsqueeze(2).to_broadcast([P, ap.shape[1], n])

        seg_i = 0
        for s in steps:
            k0 = s[0]
            t.settle()
            if k0 == "st":
                d, k = s[1:]
                c = st_chunk[d][k]
                if s == ("st", 0, 0):
                    g_.wait_ge(wdd_ready, 1)
                    job_read(g_, ("z", 3))
                else:
                    job_full(g_, st_prev[s])
                job_read(g_, ("xtr", c))
                G_.tensor_tensor(xdd[:, :].rearrange("p (h n) -> p h n", h=8),
                                 xs[:, c, :].rearrange("p (h n) -> p h n", h=8),
                                 hb(wdd[:, c, d * 8:d * 8 + 8], HD), ALU.mult).then_inc(*t(xdd_ready))
            elif k0 == "seg":
                c, g, d = s[1:]
                if (c, g) == (0, 0):
                    job_full(g_, ("F", 3))
                    g_.wait_ge(rope_ready, 5)
                else:
                    job_full(g_, ("seg", (2 * c + g - 1) // 2, (2 * c + g - 1) % 2, d))
                m = C_LE if d == 0 else C_GE
                G_.tensor_tensor(Am[:, d, :].rearrange("p (h n) -> p h n", h=4),
                                 CT[:, m:m + P].unsqueeze(1).to_broadcast([P, 4, P]),
                                 hb(dta[:, c, d * 8 + g * 4:d * 8 + g * 4 + 4], P), ALU.mult).then_inc(*t(am_ready))
                if g == 0:
                    if c:
                        job_full(g_, ("y", c - 1, 1))
                    G_.tensor_tensor(xd[:, d, :].rearrange("p (h n) -> p h n", h=8),
                                     xs[:, c, :].rearrange("p (h n) -> p h n", h=8),
                                     hb(dtv[:, c, d * 8:d * 8 + 8], HD), ALU.mult).then_inc(*t(xd_ready))
        for c in range(NCH):
            job_read(g_, ("h2tr", c))
            job_read(g_, ("srow",))
            G_.tensor_tensor(h2t[:, c, :], h2t[:, c, :], srow[:, :], ALU.add).then_inc(*t(h2t_done))
        t.settle()
        g_.wait_ge(merge_done, 32)
        for j in range(2):
            g_.sem_inc(y_left, 1)
            G_.memset(xr[:, j, :], 0.0).then_inc(*t(xr_zero))
        t.settle()
        g_.wait_ge(slot_ready, 1)
        g_.wait_ge(h2_out, 16 * NCH)

        for j in range(2):
            G_.tensor_copy(idx[:, j:j + 1], tabt[:, j:j + 1]).then_inc(idx_ready, 1)
            g_.wait_ge(idx_ready, j + 1)
            G_.indirect_dma_start(out=xr[:, j, :], out_offset=None, in_=h2d,
                                  in_offset=bass.IndirectOffsetOnAxis(ap=idx[:, j:j + 1], axis=0),
                                  bounds_check=S - 1, oob_is_err=False).then_inc(xr_in[j], 16)
        g_.sem_inc(gathers_out, 1)
        g_.wait_ge(route_done, 2)
        n = g_.value_load(nbk[0:1, 0:1], min_val=1, max_val=MAXB)
        with g_.Fori(0, PAIRS) as i:
            for j in range(2):
                b = i * 2 + j
                with g_.If(b < n):
                    g_.wait_ge(xb_full, b + 1)
                    g_.wait_ge(xr_in[j], i * 16 + 16)
                    G_.tensor_copy(idx[:, j:j + 1], tabt[:, bass.ds(b + 2, 1)]).then_inc(idx_ready, 1)
                    g_.wait_ge(idx_ready, 2 * b + 3)
                    g_.sem_inc(idx_used, 1)
                    G_.indirect_dma_start(out=xr[:, j, :], out_offset=None, in_=h2d,
                                          in_offset=bass.IndirectOffsetOnAxis(ap=idx[:, j:j + 1], axis=0),
                                          bounds_check=S - 1, oob_is_err=False).then_inc(xr_in[j], 16)
                    G_.tensor_copy(idx[:, 2 + j:3 + j], tabd[:, bass.ds(b, 1)]).then_inc(idx_ready, 1)
                    g_.wait_ge(idx_ready, 2 * b + 4)
                    g_.wait_ge(y_read, b + 2)
                    g_.sem_inc(idx_used, 1)
                    G_.indirect_dma_start(out=ybuf, in_=ysb[:, j, :], in_offset=None,
                                          out_offset=bass.IndirectOffsetOnAxis(ap=idx[:, 2 + j:3 + j], axis=0),
                                          bounds_check=2 * S - 1, oob_is_err=False).then_inc(y_out, 16)
                    g_.wait_ge(y_out, b * 16 + 16)
                    g_.sem_inc(y_left, 1)

    ctx.close()


def constants():
    p, f = np.arange(P)[:, None], np.arange(P)[None, :]
    perm = np.zeros((P, P))
    for m in range(P):
        if m % HD < HD // 2:
            perm[m + HD // 2, m] = -1.0
        else:
            perm[m - HD // 2, m] = 1.0
    same = p // HD == f // HD
    w = 2 * np.pi * ((p % HD) * (f % HD) % HD) / HD
    prev = np.where(f >= p, 0.0, NEG)
    nxt = np.where(f <= p, 0.0, NEG)
    z = np.zeros((P, P))
    pack = [np.eye(P), p <= f, p >= f, p < f, p > f, np.ones((P, P)), perm, same * np.cos(w), same * np.sin(w),
            z, z, prev, z, nxt, z, z]
    consts = np.concatenate([np.asarray(x, np.float32) for x in pack], axis=1)
    t = np.arange(S)
    ang = 2 * np.pi * (t[:, None] * t[None, :] % S) / S
    nrm = 1.0 / np.sqrt(S * HD)
    dft = np.stack([np.cos(ang) * nrm, -np.sin(ang) * nrm]).astype(np.float32)
    dft = np.ascontiguousarray(dft.reshape(2, NCH, P, S).transpose(2, 0, 1, 3))
    pairs = HD // 4
    inv = np.float32(10000.0) ** (-np.arange(pairs, dtype=np.float32) / np.float32(pairs))
    row, col = (t // 64).astype(np.float32), (t % 64).astype(np.float32)
    a = np.concatenate([row[:, None] * inv, col[:, None] * inv], axis=1).astype(np.float32).T
    a = a[np.arange(P) % 32]
    cossin = np.ascontiguousarray(np.stack([np.cos(a), np.sin(a)], axis=1).astype(np.float32))
    return consts, cossin, dft


def kernel(**inputs):
    import numpy as _np
    import concourse.bacc as _bacc
    from concourse import mybir as _mybir
    from concourse.bass_utils import run_bass_kernel_spmd as _run

    a = {k: _np.asarray(v) for k, v in inputs.items()}

    def chan(x, n):
        return x.reshape(n, P, -1).transpose(1, 0, 2)

    xT = chan(a["x"][0].T, KD)
    ctxT = chan(a["ctx"][0].T, KD)
    w_in = a["w_in"][0]
    cut = _np.cumsum([0, 512, 128, 128, 512, 768, 16, 512, 1536])
    q, k, v, z, xbc, dt, fu, su = [w_in[:, cut[i]:cut[i + 1]] for i in range(8)]
    q = q.reshape(D, 2, 4, HD).transpose(0, 2, 1, 3).reshape(D, 512)
    in_tiles = {"xbc": xbc, "k": k, "v": v, "fu": fu, "q": q, "z": z}
    wo, wg = a["w_o"][0], a["w_gate"][0]

    def units(w):
        n = w.shape[1] // S
        return w.reshape(KD, P, n, S).transpose(2, 1, 0, 3).reshape(n, P, UNIT)

    ada = units(a["w_ada"][0])

    def tile(x):
        kind = x[0]
        if kind == "macc":
            return ada[4 + x[1] // 4][:, x[1] % 4 * TILE:x[1] % 4 * TILE + TILE]
        if kind == "branch":
            b = a["w_branch"][0][x[1]]
            if x[1] == 0:
                b = b.reshape(2, 4, HD, D).transpose(1, 0, 2, 3).reshape(512, D)
            return chan(b[:, x[2] * 256:x[2] * 256 + 256], 4).reshape(P, TILE)
        if kind == "zk":
            return chan(z[x[1] * 256:x[1] * 256 + 256], 2).reshape(P, TILE)
        if kind == "gate":
            w, m = wg, x[1] * KD + x[2]
        elif kind == "wo":
            w, m = wo, x[1]
        elif kind in ("bg", "cg", "sx"):
            w, m = su, ("bg", "cg", "sx").index(kind) * 4 + x[1]
        else:
            w, m = in_tiles[kind], x[1] if len(x) > 1 else 0
        return chan(w[:, m * P:m * P + P], KD).reshape(P, TILE)

    stream = _np.stack([tile(x) for x in tile_order()[0]])

    def col(x):
        return x.reshape(-1, P).T

    consts, cossin, dft = constants()
    cv = _np.stack([a["c"][0], a["c_ctx"]], axis=1)
    cols = _np.concatenate([
        col(a["norm1_w"][0]), col(a["norm2_w"][0]), col(a["final_norm_w"]), col(a["b_ada"][0]), col(a["b_gate"][0]),
        col(a["ssm_conv_w"][0]), col(a["ssm_conv_b"][0]), col(a["sconv_w"][0]), col(a["ssm_norm_w"][0]),
        chan(cv, KD).reshape(P, 16), _np.full((P, 1), EPS, _np.float32), _np.full((P, 1), 4 * EPS, _np.float32),
        _np.zeros((P, 1), _np.float32), _np.arange(P, dtype=_np.float32)[:, None],
        2 * S + _np.arange(P, dtype=_np.float32)[:, None],
        _np.arange(P, dtype=_np.float32)[:, None] + P * _np.arange(8, dtype=_np.float32) - 2 * S], axis=1)
    rows = _np.concatenate([
        a["ssm_dt_bias"][0].reshape(-1), a["ssm_a_log"][0].reshape(-1), a["ssm_d"][0], a["attn_sink"][0],
        a["router_bias"], _np.arange(32, dtype=_np.float32), _np.arange(8, dtype=_np.float32),
        _np.arange(BLK, dtype=_np.float32)])
    rows = _np.broadcast_to(rows[None, :], (P, R_N))
    w2 = a["moe_w2"][0].reshape(NE, 4, P, D).transpose(0, 2, 1, 3).reshape(NE, P, UNIT)
    w1, w3 = [a[x][0].reshape(NE, KD, P, S).transpose(0, 2, 1, 3).reshape(NE, P, UNIT) for x in ("moe_w1", "moe_w3")]
    ins = {"xT": xT, "ctxT": ctxT, "adaw": ada[:4], "stream": stream, "consts": consts, "cossin": cossin, "dft": dft, "cols": cols,
           "rows": rows, "wdt": chan(dt, KD), "wrt": chan(a["w_router"], KD), "w1": w1, "w3": w3, "w2": w2}
    ins = {"in_" + k: _np.ascontiguousarray(v) for k, v in ins.items()}

    nc = _bacc.Bacc("TRN2", target_bir_lowering=False, num_devices=1)
    aps = {k[3:]: nc.dram_tensor(k, list(v.shape), _mybir.dt.from_np(v.dtype), kind="ExternalInput").ap()
           for k, v in ins.items()}
    aps["ybuf"] = nc.dram_tensor("expert_rows", [2 * S, D], _mybir.dt.float32, kind="Internal").ap()
    aps["h2d"] = nc.dram_tensor("token_rows", [S, D], _mybir.dt.float32, kind="Internal").ap()
    aps["outT"] = nc.dram_tensor("outT", [P, KD, S], _mybir.dt.float32, kind="ExternalOutput").ap()
    build(nc, **aps)
    r = _run(nc, [ins], core_ids=[0])
    o = _np.asarray(r.results[0]["outT"])
    return _np.ascontiguousarray(o.transpose(1, 0, 2).reshape(D, S).T)[None]
```
